# Optimizing a Trainium2 kernel written in Bass

```python
import math
import jax, jax.numpy as jnp
from jax import lax
import numpy as np

D_MODEL = 1024
BATCH = 1
SEQ = 256
DEPTH = 2

GRID_W = 64
CTX_LEN = 256
EPS = 1e-6
ROPE_THETA = 10000.0
Q_BLOCK = 128
FOURIER_WIDTH = D_MODEL // 4
FOURIER_GROUPS = 4
FOURIER_GROUP_DIM = FOURIER_WIDTH // FOURIER_GROUPS
DIFF_WIDTH = D_MODEL - FOURIER_WIDTH
DIFF_HEAD_DIM = 64
DIFF_V_DIM = 2 * DIFF_HEAD_DIM
DIFF_HEADS = DIFF_WIDTH // DIFF_V_DIM
IN_WIDTH_EVEN = 3 * DIFF_WIDTH + FOURIER_WIDTH
ATTN_SCALE = DIFF_HEAD_DIM ** -0.5
LAMBDA_STD = 0.1
CONV_WIDTH = 31
D_FF = -(-8 * D_MODEL // (3 * 256)) * 256


def rmsnorm(x, g):
    x32 = x.astype(jnp.float32)
    y = x32 * lax.rsqrt(jnp.mean(x32 * x32, axis=-1, keepdims=True) + EPS)
    return (y * g.astype(jnp.float32)).astype(x.dtype)

def layernorm(x, g, b):
    x32 = x.astype(jnp.float32)
    mu = jnp.mean(x32, axis=-1, keepdims=True)
    xc = x32 - mu
    y = xc * lax.rsqrt(jnp.mean(xc * xc, axis=-1, keepdims=True) + EPS)
    return (y * g.astype(jnp.float32) + b.astype(jnp.float32)).astype(x.dtype)

def modulate(h, shift, scale):
    return h * (1 + scale) + shift

def axial_rope_tables(rows_n):
    row = jnp.repeat(jnp.arange(rows_n, dtype=jnp.float32), GRID_W)
    col = jnp.tile(jnp.arange(GRID_W, dtype=jnp.float32), rows_n)
    axis_dim = DIFF_HEAD_DIM // 2
    inv_freq = ROPE_THETA ** (-jnp.arange(0, axis_dim, 2, dtype=jnp.float32) / axis_dim)
    ang = jnp.concatenate([row[:, None] * inv_freq, col[:, None] * inv_freq], axis=-1)
    return jnp.cos(ang), jnp.sin(ang)

def apply_rope(x, cos, sin):
    x1, x2 = jnp.split(x, 2, axis=-1)
    c = cos[:, None, :].astype(x.dtype)
    s = sin[:, None, :].astype(x.dtype)
    return jnp.concatenate([x1 * c - x2 * s, x1 * s + x2 * c], axis=-1)

def rope_heads(q, cos, sin):
    B, S, H, two, d = q.shape
    return apply_rope(q.reshape(B, S, H * two, d), cos, sin).reshape(q.shape)

def diff_attend(q, k, v, lam):
    s = jnp.einsum('bqhcd,bkhcd->bhcqk', q, k, preferred_element_type=jnp.float32) * ATTN_SCALE
    p = jax.nn.softmax(s, axis=-1)
    a = p[:, :, 0] - lam * p[:, :, 1]
    return jnp.einsum('bhqk,bkhe->bqhe', a.astype(v.dtype), v)

def fourier_groups(f, w):
    B, T, _ = f.shape
    fg = f.reshape(B, T, FOURIER_GROUPS, FOURIER_GROUP_DIM).astype(jnp.float32)
    z = jnp.fft.fft2(fg, axes=(1, 3), norm='ortho').real.astype(f.dtype)
    return jnp.einsum('btgc,gce->btge', z, w).reshape(B, T, FOURIER_WIDTH)

def split_proj(u):
    B, T, _ = u.shape
    q, k, v, f = jnp.split(u, [DIFF_WIDTH, 2 * DIFF_WIDTH, 3 * DIFF_WIDTH], axis=-1)
    return (q.reshape(B, T, DIFF_HEADS, 2, DIFF_HEAD_DIM),
            k.reshape(B, T, DIFF_HEADS, 2, DIFF_HEAD_DIM),
            v.reshape(B, T, DIFF_HEADS, DIFF_V_DIM),
            f)

def merge_heads(o, f, subln_g, fourier_w, w_out, lambda_init):
    B, T = o.shape[:2]
    o = (rmsnorm(o, subln_g) * (1.0 - lambda_init)).reshape(B, T, DIFF_WIDTH)
    return jnp.concatenate([o, fourier_groups(f, fourier_w)], axis=-1) @ w_out

def diff_fourier_mixer(h_l, h_c, cos, sin, w_in, lq1, lk1, lq2, lk2, subln_g, fourier_w, w_out,
                       lambda_init, ctx_update):
    B, S, _ = h_l.shape
    q_l, k_l, v_l, f_l = split_proj(h_l @ w_in)
    q_c, k_c, v_c, f_c = split_proj(h_c @ w_in)
    q_l = rope_heads(q_l, cos, sin)
    k_l = rope_heads(k_l, cos, sin)
    lam = (jnp.exp(jnp.sum(lq1.astype(jnp.float32) * lk1.astype(jnp.float32)))
           - jnp.exp(jnp.sum(lq2.astype(jnp.float32) * lk2.astype(jnp.float32))) + lambda_init)
    k_all = jnp.concatenate([k_c, k_l], axis=1)
    v_all = jnp.concatenate([v_c, v_l], axis=1)
    n_blk = S // Q_BLOCK
    q_blocks = jnp.moveaxis(q_l.reshape(B, n_blk, Q_BLOCK, DIFF_HEADS, 2, DIFF_HEAD_DIM), 1, 0)
    o = lax.map(lambda qb: diff_attend(qb, k_all, v_all, lam), q_blocks)
    o_l = jnp.moveaxis(o, 0, 1).reshape(B, S, DIFF_HEADS, DIFF_V_DIM)
    y_l = merge_heads(o_l, f_l, subln_g, fourier_w, w_out, lambda_init)
    y_c = None
    if ctx_update:
        y_c = merge_heads(diff_attend(q_c, k_c, v_c, lam), f_c, subln_g, fourier_w, w_out, lambda_init)
    return y_l, y_c

def depthwise_conv(u, w):
    return lax.conv_general_dilated(
        u, w[:, None, :].astype(u.dtype), window_strides=(1,),
        padding=[(CONV_WIDTH // 2, CONV_WIDTH // 2)],
        dimension_numbers=('NWC', 'WIO', 'NWC'), feature_group_count=u.shape[-1])

def conformer_conv(h, pw1_w, pw1_b, dw_w, dw_b, ln_g, ln_b, pw2_w, pw2_b):
    a, g = jnp.split(h @ pw1_w + pw1_b, 2, axis=-1)
    u = a * jax.nn.sigmoid(g)
    u = depthwise_conv(u, dw_w) + dw_b
    u = jax.nn.silu(layernorm(u, ln_g, ln_b))
    return u @ pw2_w + pw2_b

def swiglu(h, w1, w3, w2):
    return (jax.nn.silu(h @ w1) * (h @ w3)) @ w2

def first_inputs(seed: int = 0) -> dict:
    key = jax.random.key(seed)
    ks = iter(jax.random.split(key, 32))
    n_even = (DEPTH + 1) // 2
    n_odd = DEPTH // 2
    f32 = jnp.float32

    def nrm(shape):
        return jax.random.normal(next(ks), shape, f32)

    def w(shape, fan_in):
        return nrm(shape) * fan_in ** -0.5

    def gain(shape):
        return 1.0 + 0.05 * nrm(shape)

    def bias(shape):
        return 0.02 * nrm(shape)

    D = D_MODEL
    return {
        'x': nrm((BATCH, SEQ, D)),
        'c': nrm((BATCH, D)),
        'ctx': nrm((BATCH, CTX_LEN, D)),
        'c_ctx': nrm((D,)),
        'ada_w': w((DEPTH, D, 6 * D), D),
        'ada_b': bias((DEPTH, 6 * D)),
        'mix_norm_g': gain((DEPTH, D)),
        'ffn_norm_g': gain((DEPTH, D)),
        'ffn_w1': w((DEPTH, D, D_FF), D),
        'ffn_w3': w((DEPTH, D, D_FF), D),
        'ffn_w2': w((DEPTH, D_FF, D), D_FF),
        'ev_w_in': w((n_even, D, IN_WIDTH_EVEN), D),
        'ev_lambda_q1': LAMBDA_STD * nrm((n_even, DIFF_HEAD_DIM)),
        'ev_lambda_k1': LAMBDA_STD * nrm((n_even, DIFF_HEAD_DIM)),
        'ev_lambda_q2': LAMBDA_STD * nrm((n_even, DIFF_HEAD_DIM)),
        'ev_lambda_k2': LAMBDA_STD * nrm((n_even, DIFF_HEAD_DIM)),
        'ev_subln_g': gain((n_even, DIFF_V_DIM)),
        'ev_fourier_w': w((n_even, FOURIER_GROUPS, FOURIER_GROUP_DIM, FOURIER_GROUP_DIM), FOURIER_GROUP_DIM),
        'ev_w_out': w((n_even, D, D), D),
        'od_pw1_w': w((n_odd, D, 2 * D), D),
        'od_pw1_b': bias((n_odd, 2 * D)),
        'od_dw_w': w((n_odd, CONV_WIDTH, D), CONV_WIDTH),
        'od_dw_b': bias((n_odd, D)),
        'od_ln_g': gain((n_odd, D)),
        'od_ln_b': bias((n_odd, D)),
        'od_pw2_w': w((n_odd, D, D), D),
        'od_pw2_b': bias((n_odd, D)),
        'final_g': gain((D,)),
    }

def first_block(x, c, ctx, c_ctx, ada_w, ada_b, mix_norm_g, ffn_norm_g, ffn_w1, ffn_w3, ffn_w2,
              ev_w_in, ev_lambda_q1, ev_lambda_k1, ev_lambda_q2, ev_lambda_k2, ev_subln_g,
              ev_fourier_w, ev_w_out, od_pw1_w, od_pw1_b, od_dw_w, od_dw_b, od_ln_g, od_ln_b,
              od_pw2_w, od_pw2_b, final_g):
    S = x.shape[1]
    ROWS = S // GRID_W
    cos, sin = axial_rope_tables(ROWS)
    silu_c = jax.nn.silu(c)
    silu_cc = jax.nn.silu(c_ctx)
    xc = ctx
    for i in range(DEPTH):
        j = i // 2
        even = i % 2 == 0
        ctx_update = any(k % 2 == 0 for k in range(i + 1, DEPTH))
        read_ctx = even or ctx_update
        mod_l = jnp.split((silu_c @ ada_w[i] + ada_b[i])[:, None, :], 6, axis=-1)
        h_l = modulate(rmsnorm(x, mix_norm_g[i]), mod_l[0], mod_l[1])
        mod_c = None
        h_c = None
        if read_ctx:
            mod_c = jnp.split((silu_cc @ ada_w[i] + ada_b[i])[None, None, :], 6, axis=-1)
            h_c = modulate(rmsnorm(xc, mix_norm_g[i]), mod_c[0], mod_c[1])
        if even:
            lambda_init = 0.8 - 0.6 * math.exp(-0.3 * i)
            y_l, y_c = diff_fourier_mixer(h_l, h_c, cos, sin, ev_w_in[j], ev_lambda_q1[j], ev_lambda_k1[j],
                                          ev_lambda_q2[j], ev_lambda_k2[j], ev_subln_g[j], ev_fourier_w[j],
                                          ev_w_out[j], lambda_init, ctx_update)
        else:
            conv_args = (od_pw1_w[j], od_pw1_b[j], od_dw_w[j], od_dw_b[j], od_ln_g[j], od_ln_b[j],
                         od_pw2_w[j], od_pw2_b[j])
            y_l = conformer_conv(h_l, *conv_args)
            y_c = conformer_conv(h_c, *conv_args) if ctx_update else None
        x = x + mod_l[2] * y_l
        x = x + mod_l[5] * swiglu(modulate(rmsnorm(x, ffn_norm_g[i]), mod_l[3], mod_l[4]),
                                  ffn_w1[i], ffn_w3[i], ffn_w2[i])
        if ctx_update:
            xc = xc + mod_c[2] * y_c
            xc = xc + mod_c[5] * swiglu(modulate(rmsnorm(xc, ffn_norm_g[i]), mod_c[3], mod_c[4]),
                                        ffn_w1[i], ffn_w3[i], ffn_w2[i])
    return rmsnorm(x, final_g)


HEAD_DIM = 64
CONV_CH = 256
CONV_WIDTH_2 = 3
HGRN_HEADS = 4
HGRN_DK = 64
HGRN_DV = 64
HGRN_QK = HGRN_HEADS * HGRN_DK
HGRN_WIDTH = HGRN_HEADS * HGRN_DV
CHUNK = 64
FOX_HEADS = 8
FOX_WIDTH = FOX_HEADS * HEAD_DIM
MIX_WIDTH = CONV_CH + HGRN_WIDTH + FOX_WIDTH
MIX_IN_SIZES = (CONV_CH, CONV_CH, CONV_CH,
                HGRN_QK, HGRN_QK, HGRN_WIDTH, HGRN_WIDTH,
                FOX_WIDTH, FOX_WIDTH, FOX_WIDTH, FOX_HEADS)
MIX_IN = sum(MIX_IN_SIZES)
D_FF_2 = 2816
MASK_VALUE = -1e30


def rms_norm(x, gain):
    xf = x.astype(jnp.float32)
    inv = lax.rsqrt(jnp.mean(xf * xf, axis=-1, keepdims=True) + EPS)
    return (xf * inv).astype(x.dtype) * gain

def swiglu_2(h, w_in, w_out):
    gate, up = jnp.split(h @ w_in, 2, axis=-1)
    return (jax.nn.silu(gate) * up) @ w_out

def short_conv_mixer(x_in, b_gate, c_gate, conv_w):
    u = c_gate * x_in
    taps = conv_w[:, None, :].astype(u.dtype)
    y = lax.conv_general_dilated(u, taps, window_strides=(1,),
                                 padding=((CONV_WIDTH_2 - 1, 0),),
                                 dimension_numbers=('NWC', 'WIO', 'NWC'),
                                 feature_group_count=CONV_CH)
    return b_gate * y

def hgrn2_mixer(q, f_logit, v, g, lb, out_gain):
    f32 = jnp.float32
    bsz, seqlen, _ = q.shape
    n_chunks = seqlen // CHUNK
    z = f_logit.astype(f32)
    lb = lb.astype(f32)
    log_f = jax.nn.log_sigmoid(z) + jnp.log1p(lb * jnp.exp(-z))
    k = (1.0 - lb) * jax.nn.sigmoid(-z)

    def to_chunks(t, d):
        return t.astype(f32).reshape(bsz, n_chunks, CHUNK, HGRN_HEADS, d).transpose(1, 0, 3, 2, 4)

    qc, kc, lfc = to_chunks(q, HGRN_DK), to_chunks(k, HGRN_DK), to_chunks(log_f, HGRN_DK)
    vc = to_chunks(v, HGRN_DV)
    causal = jnp.tril(jnp.ones((CHUNK, CHUNK), dtype=bool))[:, :, None]

    def step(state, inp):
        qb, kb, vb, lfb = inp
        bcum = jnp.cumsum(lfb, axis=-2)
        rel = bcum[..., :, None, :] - bcum[..., None, :, :]
        decay = jnp.where(causal, jnp.exp(jnp.where(causal, rel, 0.0)), 0.0)
        scores = jnp.einsum('bhtd,bhsd,bhtsd->bhts', qb, kb, decay)
        o = (jnp.einsum('bhts,bhsv->bhtv', scores, vb)
             + jnp.einsum('bhtd,bhdv->bhtv', qb * jnp.exp(bcum), state))
        b_last = bcum[..., -1:, :]
        state = (jnp.exp(b_last[..., 0, :])[..., None] * state
                 + jnp.einsum('bhsd,bhsv->bhdv', kb * jnp.exp(b_last - bcum), vb))
        return state, o

    s0 = jnp.zeros((bsz, HGRN_HEADS, HGRN_DK, HGRN_DV), f32)
    _, o = lax.scan(step, s0, (qc, kc, vc, lfc))
    o = o.transpose(1, 0, 3, 2, 4).reshape(bsz, seqlen, HGRN_HEADS, HGRN_DV)
    gate = g.astype(f32).reshape(bsz, seqlen, HGRN_HEADS, HGRN_DV)
    o = rms_norm(o, out_gain) * jax.nn.silu(gate)
    return o.reshape(bsz, seqlen, HGRN_WIDTH).astype(q.dtype)

def fox_mixer(q, k, v, f_logit, f_bias, q_gain, k_gain):
    f32 = jnp.float32
    bsz, seqlen, _ = q.shape

    def heads(t):
        return t.reshape(bsz, seqlen, FOX_HEADS, HEAD_DIM).transpose(0, 2, 1, 3)

    qh = rms_norm(heads(q), q_gain) * (HEAD_DIM ** -0.5)
    kh = rms_norm(heads(k), k_gain)
    vh = heads(v)
    log_f = jax.nn.log_sigmoid((f_logit + f_bias).astype(f32))
    cum = jnp.cumsum(log_f, axis=1).transpose(0, 2, 1)
    kpos = jnp.arange(seqlen)

    def block(i):
        start = i * Q_BLOCK
        qb = lax.dynamic_slice_in_dim(qh, start, Q_BLOCK, axis=2)
        cb = lax.dynamic_slice_in_dim(cum, start, Q_BLOCK, axis=2)
        qpos = start + jnp.arange(Q_BLOCK)
        s = (jnp.einsum('bhqd,bhkd->bhqk', qb, kh).astype(f32)
             + (cb[..., :, None] - cum[..., None, :]))
        s = jnp.where(qpos[:, None] >= kpos[None, :], s, MASK_VALUE)
        p = jax.nn.softmax(s, axis=-1)
        return jnp.einsum('bhqk,bhkd->bhqd', p.astype(vh.dtype), vh)

    o = lax.map(block, jnp.arange(seqlen // Q_BLOCK))
    return o.transpose(1, 0, 3, 2, 4).reshape(bsz, seqlen, FOX_WIDTH)

def second_inputs(seed: int = 0) -> dict:
    key = jax.random.key(seed)
    ks = jax.random.split(key, 17)
    nrm = jax.random.normal
    f32 = jnp.float32
    return {
        "x": nrm(ks[0], (BATCH, SEQ, D_MODEL), f32),
        "ffn1_norm": 1.0 + 0.02 * nrm(ks[1], (DEPTH, D_MODEL), f32),
        "ffn1_w_in": nrm(ks[2], (DEPTH, D_MODEL, 2 * D_FF_2), f32) * D_MODEL ** -0.5,
        "ffn1_w_out": nrm(ks[3], (DEPTH, D_FF_2, D_MODEL), f32) * D_FF_2 ** -0.5,
        "mix_norm": 1.0 + 0.02 * nrm(ks[4], (DEPTH, D_MODEL), f32),
        "w_mix_in": nrm(ks[5], (DEPTH, D_MODEL, MIX_IN), f32) * D_MODEL ** -0.5,
        "conv_w": nrm(ks[6], (DEPTH, CONV_WIDTH_2, CONV_CH), f32) * CONV_WIDTH_2 ** -0.5,
        "hgrn_lb_logits": nrm(ks[7], (DEPTH, HGRN_QK), f32),
        "hgrn_out_gain": 1.0 + 0.02 * nrm(ks[8], (DEPTH, HGRN_DV), f32),
        "fox_q_gain": 1.0 + 0.02 * nrm(ks[9], (DEPTH, HEAD_DIM), f32),
        "fox_k_gain": 1.0 + 0.02 * nrm(ks[10], (DEPTH, HEAD_DIM), f32),
        "fox_f_bias": 2.0 + 0.5 * nrm(ks[11], (DEPTH, FOX_HEADS), f32),
        "w_mix_out": nrm(ks[12], (DEPTH, MIX_WIDTH, D_MODEL), f32) * MIX_WIDTH ** -0.5,
        "ffn2_norm": 1.0 + 0.02 * nrm(ks[13], (DEPTH, D_MODEL), f32),
        "ffn2_w_in": nrm(ks[14], (DEPTH, D_MODEL, 2 * D_FF_2), f32) * D_MODEL ** -0.5,
        "ffn2_w_out": nrm(ks[15], (DEPTH, D_FF_2, D_MODEL), f32) * D_FF_2 ** -0.5,
    }

def second_block(x, ffn1_norm, ffn1_w_in, ffn1_w_out, mix_norm, w_mix_in, conv_w,
              hgrn_lb_logits, hgrn_out_gain, fox_q_gain, fox_k_gain, fox_f_bias,
              w_mix_out, ffn2_norm, ffn2_w_in, ffn2_w_out):
    lb_soft = jax.nn.softmax(hgrn_lb_logits.astype(jnp.float32), axis=0)
    lower_bounds = jnp.clip(jnp.cumsum(lb_soft, axis=0) - lb_soft[0:1], 0.0, 1.0)
    split_at = [int(s) for s in np.cumsum(MIX_IN_SIZES)[:-1]]
    for l in range(DEPTH):
        x = x + 0.5 * swiglu_2(rms_norm(x, ffn1_norm[l]), ffn1_w_in[l], ffn1_w_out[l])
        h = rms_norm(x, mix_norm[l]) @ w_mix_in[l]
        (c_x, c_b, c_c, h_q, h_f, h_i, h_g, f_q, f_k, f_v, f_f) = jnp.split(h, split_at, axis=-1)
        y = jnp.concatenate([
            short_conv_mixer(c_x, c_b, c_c, conv_w[l]),
            hgrn2_mixer(h_q, h_f, h_i, h_g, lower_bounds[l], hgrn_out_gain[l]),
            fox_mixer(f_q, f_k, f_v, f_f, fox_f_bias[l], fox_q_gain[l], fox_k_gain[l]),
        ], axis=-1)
        x = x + y @ w_mix_out[l]
        x = x + 0.5 * swiglu_2(rms_norm(x, ffn2_norm[l]), ffn2_w_in[l], ffn2_w_out[l])
    return x


def setup_inputs(seed=0):
    out = dict(first_inputs(seed))
    for name, value in second_inputs(seed + 1).items():
        if name != "x":
            out[name + "_2"] = value
    return out


def reference(
    x, c, ctx, c_ctx, ada_w, ada_b, mix_norm_g, ffn_norm_g, ffn_w1, ffn_w3, ffn_w2, ev_w_in,
    ev_lambda_q1, ev_lambda_k1, ev_lambda_q2, ev_lambda_k2, ev_subln_g, ev_fourier_w, ev_w_out,
    od_pw1_w, od_pw1_b, od_dw_w, od_dw_b, od_ln_g, od_ln_b, od_pw2_w, od_pw2_b, final_g,
    ffn1_norm_2, ffn1_w_in_2, ffn1_w_out_2, mix_norm_2, w_mix_in_2, conv_w_2, hgrn_lb_logits_2,
    hgrn_out_gain_2, fox_q_gain_2, fox_k_gain_2, fox_f_bias_2, w_mix_out_2, ffn2_norm_2,
    ffn2_w_in_2, ffn2_w_out_2,
):
    x = first_block(
        x, c, ctx, c_ctx, ada_w, ada_b, mix_norm_g, ffn_norm_g, ffn_w1, ffn_w3, ffn_w2, ev_w_in,
        ev_lambda_q1, ev_lambda_k1, ev_lambda_q2, ev_lambda_k2, ev_subln_g, ev_fourier_w,
        ev_w_out, od_pw1_w, od_pw1_b, od_dw_w, od_dw_b, od_ln_g, od_ln_b, od_pw2_w, od_pw2_b,
        final_g,
    )
    return second_block(
        x, ffn1_norm_2, ffn1_w_in_2, ffn1_w_out_2, mix_norm_2, w_mix_in_2, conv_w_2,
        hgrn_lb_logits_2, hgrn_out_gain_2, fox_q_gain_2, fox_k_gain_2, fox_f_bias_2,
        w_mix_out_2, ffn2_norm_2, ffn2_w_in_2, ffn2_w_out_2,
    )


_drawn_inputs = setup_inputs


def setup_inputs(seed=0):
    import zlib

    import numpy as np

    out = dict(_drawn_inputs(seed))
    spreads = {}
    factors = {'ev_lambda_q2': 8.0,
     'od_pw1_b': 6.774,
     'od_dw_b': 3.988,
     'od_ln_b': 5.133,
     'od_pw2_b': 3.319,
     'ffn1_norm_2': 3.728,
     'hgrn_out_gain_2': 7.802,
     'fox_q_gain_2': 8.0,
     'fox_k_gain_2': 8.0,
     'ffn2_norm_2': 5.632}
    for name, (base, spread) in spreads.items():
        noise = np.random.default_rng([zlib.crc32(name.encode()), seed]).standard_normal(out[name].shape)
        drawn = base * np.exp(spread * noise) if base else spread * noise
        out[name] = __import__('jax').numpy.asarray(drawn.astype(out[name].dtype))
    for name, factor in factors.items():
        out[name] = (out[name] * factor).astype(out[name].dtype)
    return out
```

```python
from contextlib import ExitStack, contextmanager

import numpy as np

import concourse.bass as bass
from concourse import mybir

F32 = mybir.dt.float32
F32R = mybir.dt.float32r
U8 = mybir.dt.uint8
ALU = mybir.AluOpType
ACT = mybir.ActivationFunctionType
AX = mybir.AxisListType

P = 128
D = 1024
KD = D // P
T = 2
S = T * P
FF = 2816
KF = FF // P
HALF = 256
CH = 2 * HALF
SLAB = 2048
RING = 4
EPS = 1e-6
GRID_W, ROPE_THETA, HD = 64, 10000.0, 64
DW, FW = 768, 256
VD = 128
HEADS1 = DW // VD
LAMBDA_INIT = 0.8 - 0.6
TAPS = 31
FOX_H, HG_H = 8, 4
MIX_IN = 3336
LEVELS = (64, 32, 16, 8, 4, 2, 1)


class Signal:

    def __init__(self, sem, step=1):
        self.sem, self.step, self.n, self.term, self.per = sem, step, 0, None, 0

    def on(self, ins):
        ins.then_inc(self.sem, self.step)
        self.n += self.step
        return self.now()

    def now(self, back=0):
        return (self, self.n - back * self.step, self.term)


def wait(eng, *marks):
    for m in marks:
        if m is None:
            continue
        sig, n, term = m
        if term is None:
            if n > 0:
                eng.wait_ge(sig.sem, n)
        else:
            eng.wait_ge(sig.sem, term + n)


@contextmanager
def repeat(loop, turns, per):
    with loop(0, turns) as i:
        starts = {}
        for sig, k in per.items():
            starts[sig] = sig.n
            sig.term = i * (k * sig.step)
        yield i
        for sig, k in per.items():
            assert sig.n - starts[sig] == k * sig.step, (sig.sem, sig.n - starts[sig], k)
    for sig, k in per.items():
        sig.n = starts[sig] + k * sig.step * turns
        sig.term = None


def program(nc, A, out, stop=99):
    sem_count = [0]
    ctx = ExitStack()
    with ctx:
        def signal(name, step=1):
            sem_count[0] += 1
            return Signal(ctx.enter_context(nc.semaphore(name)), step)

        used_bytes = [-(-nc.sbuf_base // 32) * 32]

        def at(name, shape, offset, dt=F32):
            return nc.alloc_sbuf_tensor_at(name, list(shape), dt, offset=offset)

        def place(name, shape, dt=F32, bytes_=4):
            size = bytes_ * int(np.prod(shape[1:]))
            o = used_bytes[0]
            used_bytes[0] += -(-size // 32) * 32
            return at(name, shape, o, dt)

        raw = [place(f"raw{r}", [P, SLAB]) for r in range(RING)]
        hi = [place(f"hi{r}", [P, SLAB], F32R) for r in range(RING)]
        lo = [place(f"lo{r}", [P, SLAB], F32R) for r in range(RING)]
        X = place("X", [P, T, D])
        XTh = place("XTh", [P, KD, S], F32R)
        XTl = place("XTl", [P, KD, S], F32R)
        tmp_at = used_bytes[0]
        XN = place("XN", [P, T, D])
        FULL = place("FULL", [P, KD, S])
        ht_at = used_bytes[0]
        HTh = place("HTh", [P, KF, S], F32R)
        HTl = place("HTl", [P, KF, S], F32R)
        ht_end = used_bytes[0]
        gate_at = used_bytes[0]
        GATE = place("GATE", [P, 4, D])
        IDENT = place("IDENT", [P, P])
        COLS = place("COLS", [P, P])
        MODS = place("MODS", [P, 2, 4, KD])
        MODC = place("MODC", [P, 2, KD])
        cst_at = used_bytes[0]
        used_bytes[0] += 5120
        total_slabs = 62 + 33 + 12 + 33 + 2 * (33 + 17 + 33)
        place2 = place
        SG = place("SG", [P, T, HALF])
        HID = place("HID", [P, T, HALF])
        ST = place("ST", [P, 64])

        bank = [ctx.enter_context(nc.psum_tensor(f"bank{b}", [P, 512], F32)) for b in range(8)]

        pe, act, dve, pool, sp = nc.tensor, nc.scalar, nc.vector, nc.gpsimd, nc.sync

        landed = [signal(f"landed{r}", 16) for r in range(RING)]
        hi_done = signal("hi_done")
        lo_done = signal("lo_done")
        consumed = signal("consumed")
        s_pe, s_act, s_dve, s_pool = signal("s_pe"), signal("s_act"), signal("s_dve"), signal("s_pool")
        s_in = signal("s_in", 16)
        silu_done = signal("silu_done")
        hid_done = signal("hid_done")
        turned = signal("turned")
        hth_done = signal("hth_done")
        htl_done = signal("htl_done")
        out_act = signal("out_act")
        out_dve = signal("out_dve")

        g_load = [0]
        g_split = [0]
        g_use = [0]

        def val(sig, n, i, scale=1):
            return (sig, n, None if i is None else i * (4 * scale))

        def load_slab(parts, i=None):
            g = g_load[0]
            r = g % RING
            if g >= RING:
                wait(sp, val(hi_done, g - RING + 1, i), val(lo_done, g - RING + 1, i))
            for dst, src in parts(raw[r]):
                landed[r].on(sp.dma_start(dst, src))
            g_load[0] += 1

        def load_slabs(n, parts):
            first = n if g_load[0] == 0 or n < 8 else n % 4
            if first < n and g_load[0] < RING:
                first += 4
            for s in range(first):
                load_slab(parts(s, 0))
            turns = (n - first) // 4
            if turns == 1:
                for s in range(first, n):
                    load_slab(parts(s, 0))
            elif turns:
                g0 = g_load[0]
                with repeat(sp.Fori, turns, {x: 2 for x in landed}) as i:
                    for s in range(first, first + 4):
                        load_slab(parts(s, i), i)
                g_load[0] = g0 + 4 * turns

        def split_next(i=None):
            g = g_split[0]
            if g >= total_slabs:
                return
            r = g % RING
            here = (landed[r], 32 * (g // RING + 1), None if i is None else i * 32)
            free = val(consumed, g - RING + 1, i)
            wait(act, here, free)
            hi_done.on(act.activation(hi[r][:, :], raw[r][:, :], ACT.Copy))
            wait(dve, here, free, val(hi_done, g + 1, i))
            lo_done.on(dve.tensor_tensor(lo[r][:, :], raw[r][:, :], hi[r][:, :].bitcast(F32), ALU.subtract))
            g_split[0] += 1

        def slab_ready(i=None):
            g = g_use[0]
            wait(pe, val(hi_done, g + 1, i), val(lo_done, g + 1, i))
            return g % RING

        def slab_used(ins, i=None):
            consumed.on(ins)
            g_use[0] += 1

        def three(dst, xh, xl, wh, wl, start, stop):
            pe.matmul(dst, xh, wh, start=start, stop=False)
            pe.matmul(dst, xh, wl, start=False, stop=False)
            return pe.matmul(dst, xl, wh, start=False, stop=stop)

        def chunk_slab(half, banks, stats, i=None):
            r = slab_ready(i)
            for k in range(4):
                kk = 4 * half + k
                wh, wl = hi[r][:, k * CH:(k + 1) * CH], lo[r][:, k * CH:(k + 1) * CH]
                for b, (xh, xl) in zip(banks, stats):
                    last = three(b[:, :], xh(kk), xl(kk), wh, wl, kk == 0, kk == KD - 1)
            slab_used(last, i)

        def tiles(h, l, k0=0):
            return [((lambda k, t=t: h[:, k0 + k, t * P:(t + 1) * P]),
                     (lambda k, t=t: l[:, k0 + k, t * P:(t + 1) * P])) for t in range(T)]

        def slab_mark(i=None):
            return val(consumed, g_use[0], i)

        def row_tiles(w):
            return w.rearrange("(k p) n -> p k n", p=P)

        def up_parts(wa, ca, wb, cb, width=HALF):
            va, vb = row_tiles(wa), row_tiles(wb)

            def parts(s, i):
                c, half = s // 2, s % 2
                off = c * width if i is None or isinstance(i, int) and i == 0 else i * (2 * width) + c * width

                def into(slot):
                    v = slot[:, :].rearrange("p (k n) -> p k n", k=4)
                    ks = slice(4 * half, 4 * half + 4)
                    return [(v[:, :, 0:HALF], va[:, ks, bass.ds(off + ca, HALF)]),
                            (v[:, :, HALF:CH], vb[:, ks, bass.ds(off + cb, HALF)])]
                return into
            return parts

        def down_parts(w):
            v = row_tiles(w)

            def parts(s, i):
                def into(slot):
                    d = slot[:, :].rearrange("p (k n) -> p k n", k=2)
                    res = []
                    for k in range(2):
                        kk = 2 * s + k if i is None or isinstance(i, int) else i * 8 + (2 * s + k)
                        res.append((d[:, k, :], w[bass.ds(kk * P, P), :]))
                    return res
                return into
            return parts

        def A_(ins):
            return s_act.on(ins)

        def V_(ins):
            return s_dve.on(ins)

        def M_(ins):
            return s_pe.on(ins)

        def G_(ins):
            return s_pool.on(ins)

        acc = [[bank[4 + 2 * t + n] for n in range(2)] for t in range(T)]

        def down(nslab, xh, xl, first_mark, late=None, late_from=0, bias=None):
            wait(pe, *first_mark)
            for s in range(nslab):
                if late is not None and s == nslab - 1:
                    wait(pe, *late_marks[0])
                r = slab_ready()
                for k in range(2):
                    kk = 2 * s + k
                    for t in range(T):
                        sh, sl = xh[:, kk, t * P:(t + 1) * P], xl[:, kk, t * P:(t + 1) * P]
                        w = [(hi[r][:, k * D + n * 512:k * D + n * 512 + 512],
                              lo[r][:, k * D + n * 512:k * D + n * 512 + 512]) for n in range(2)]
                        st, en = kk == 0, kk == 2 * nslab - 1
                        for n in range(2):
                            pe.matmul(acc[t][n][:, :], sh, w[n][0], start=st, stop=False)
                            pe.matmul(acc[t][n][:, :], sh, w[n][1], start=False, stop=False)
                        for n in range(2):
                            last = pe.matmul(acc[t][n][:, :], sl, w[n][0], start=False, stop=en)
                slab_used(last)
                if late is not None and s == late_from:
                    late()
                split_next()

        late_marks = [()]
        x_mark = [None]

        def add_residual(gate=None, half=False, gate_mark=None, bias=None):
            done = slab_mark()
            wait(dve, done, x_mark[0], gate_mark)
            for t in range(T):
                for n in range(2):
                    cols = slice(n * 512, n * 512 + 512)
                    if gate is None:
                        m = V_(dve.scalar_tensor_tensor(out=X[:, t, cols], in0=acc[t][n][:, :],
                                                        scalar=0.5 if half else 1.0, in1=X[:, t, cols],
                                                        op0=ALU.mult, op1=ALU.add))
                    else:
                        src = acc[t][n][:, :]
                        if bias is not None:
                            m = V_(dve.tensor_tensor(XN[:, t, cols], src, bias[:, cols], ALU.add))
                            wait(dve, m)
                            src = XN[:, t, cols]
                        m = V_(dve.tensor_tensor(XN[:, t, cols], src, GATE[:, gate, cols], ALU.mult))
                        wait(dve, m)
                        m = V_(dve.tensor_tensor(X[:, t, cols], X[:, t, cols], XN[:, t, cols], ALU.add))
            x_mark[0] = m
            return m

        def rstd_of(src, t, n, base, mark, junk):
            wait(act, *mark)
            m = A_(act.activation(junk, src, ACT.Square, accum_out=ST[:, base:base + 1]))
            wait(dve, m)
            m = V_(dve.tensor_scalar(ST[:, base:base + 1], ST[:, base:base + 1], 1.0 / n, EPS, ALU.mult, ALU.add))
            wait(act, m)
            m = A_(act.activation(ST[:, base:base + 1], ST[:, base:base + 1], ACT.Sqrt))
            wait(dve, m)
            return V_(dve.reciprocal(ST[:, base:base + 1], ST[:, base:base + 1]))

        def to_columns(rows, rows_mark, gains, shifts, xh, xl, free, kn=KD, k0=0, banks=(4, 5, 6, 7), post=None):
            wait(pe, *rows_mark)
            marks = []
            full_mark = None
            for kp in range(0, kn, 2):
                b = bank[banks[(kp // 2) % len(banks)]]
                if kp // 2 >= len(banks):
                    wait(pe, marks[kp // 2 - len(banks)][0])
                ks = range(kp, min(kp + 2, kn))
                for k in ks:
                    for t in range(T):
                        last = pe.transpose(b[:, (k - kp) * S + t * P:(k - kp) * S + (t + 1) * P],
                                            rows[:, t, k * P:(k + 1) * P], IDENT[:, :])
                turned_m = M_(last)
                wait(dve, turned_m)
                for k in ks:
                    src = b[:, (k - kp) * S:(k - kp + 1) * S]
                    if shifts is not None:
                        m = V_(dve.tensor_scalar(FULL[:, k, :], src, gains[:, k:k + 1], shifts[:, k:k + 1],
                                                 ALU.mult, ALU.add))
                    elif gains is not None:
                        m = V_(dve.tensor_scalar(FULL[:, k, :], src, gains[:, k:k + 1], None, ALU.mult))
                    else:
                        m = V_(dve.tensor_copy(FULL[:, k, :], src))
                full_mark = m
                a, z = kp, kp + len(ks)
                if post is not None:
                    continue
                wait(act, m, *free)
                h = A_(act.activation(xh[:, k0 + a:k0 + z, :], FULL[:, a:z, :], ACT.Copy))
                wait(dve, h, *free)
                l = V_(dve.tensor_tensor(xl[:, k0 + a:k0 + z, :], FULL[:, a:z, :],
                                         xh[:, k0 + a:k0 + z, :].bitcast(F32), ALU.subtract))
                marks.append((full_mark, h, l))
            return [marks[-1][1], marks[-1][2]] if marks else [full_mark]

        def norm_columns(gains, shifts, xh=None, xl=None, src=None, mark=None):
            xh, xl, src = XTh if xh is None else xh, XTl if xl is None else xl, X if src is None else src
            mark = x_mark[0] if mark is None else mark
            rm = []
            for t in range(T):
                m = rstd_of(src[:, t, :], t, D, t, [mark, *pe_idle()], XN[:, t, :])
                wait(dve, m, s_act.now())
                rm.append(V_(dve.tensor_scalar(XN[:, t, :], src[:, t, :], ST[:, t:t + 1], None, ALU.mult)))
            return to_columns(XN, rm, gains, shifts, xh, xl, pe_idle())

        def pe_idle():
            return [slab_mark() if g_use[0] else None, s_pe.now()]

        SGB = [SG, HID]

        def ffn_step(c, pair, i, x_marks, first):
            banks = [bank[2 * pair + t] for t in range(T)]
            if not first or c > 1:
                wait(pe, hid_done.now(2))
            chunk_slab(0, banks, tiles(XTh, XTl), i)
            split_next(i)
            if not (first and c == 0):
                turn_chunk(i, c - 1)
            chunk_slab(1, banks, tiles(XTh, XTl), i)
            done = slab_mark(i)
            wait(act, done)
            for t in range(T):
                silu_done.on(act.activation(SG[:, t, :], banks[t][:, 0:HALF], ACT.Silu))
                wait(dve, silu_done.now())
                hid_done.on(dve.tensor_tensor(HID[:, t, :], SG[:, t, :], banks[t][:, HALF:CH], ALU.mult))
            split_next(i)

        def turn_chunk(i, c, b=None):
            b = bank[4] if b is None else b
            off = 2 * c if i is None else i * 4 + 2 * c
            wait(pe, hid_done.now(), htl_done.now())
            for f in range(2):
                for t in range(T):
                    last = pe.transpose(b[:, f * S + t * P:f * S + (t + 1) * P], HID[:, t, f * P:(f + 1) * P],
                                        IDENT[:, :])
            turned.on(last)
            src = b[:, :].rearrange("p (f s) -> p f s", f=2)
            wait(act, turned.now())
            hth_done.on(act.activation(HTh[:, bass.ds(off, 2), :], src, ACT.Copy))
            wait(dve, hth_done.now())
            htl_done.on(dve.tensor_tensor(HTl[:, bass.ds(off, 2), :], src,
                                          HTh[:, bass.ds(off, 2), :].bitcast(F32), ALU.subtract))

        def ffn_up(x_marks):
            wait(pe, *x_marks)
            ffn_step(0, 0, None, x_marks, True)
            g0 = (g_split[0], g_use[0])
            n = KF // 2
            assert n % 2 == 1
            turns = (n - 1) // 2
            per = {hi_done: 0, silu_done: 4, hid_done: 4, turned: 2, hth_done: 2, htl_done: 2}
            with repeat(nc.Fori, turns, {k: v for k, v in per.items() if v}) as i:
                ffn_step(1, 1, i, x_marks, False)
                ffn_step(2, 0, i, x_marks, False)
            g_split[0], g_use[0] = g0[0] + 4 * turns, g0[1] + 4 * turns
            sync_ring()

        def sync_ring():
            hi_done.n = lo_done.n = g_split[0]
            consumed.n = g_use[0]

        def ffn(gains, shifts, finish):
            xm = norm_columns(gains, shifts)
            ffn_up(xm)

            def late():
                turn_chunk(None, KF // 2 - 1, bank[2])
                late_marks[0] = (hth_done.now(), htl_done.now())
            down(KF // 2, HTh, HTl, [hth_done.now(), htl_done.now(), *acc_free()], late=late)
            finish()

        def acc_free():
            return [s_dve.now(), s_act.now(), htl_done.now(), hth_done.now()]

        def load_const(dst, src):
            s_in.on(act.dma_start(dst, src))
            return s_in.now()

        ROW = at("ROW", [8, 6 * D], ht_at)
        CT = at("CT", [P, KD, P], ht_at + 24576, F32R)
        CS = at("CS", [P, 4, KD], ht_at + 28672)
        UROW = at("UROW", [P, T, 2560], ht_at)
        CTXh = at("CTXh", [P, KD, S], ht_at + 20480, F32R)
        CTXl = at("CTXl", [P, KD, S], ht_at + 28672, F32R)
        CX = at("CX", [P, T, D], ht_at + 36864)
        QT = at("QT", [P, HEADS1, S], ht_at + 20480)
        KT = at("KT", [P, HEADS1, 2 * S], ht_at + 26624)
        OROW = at("OROW", [P, T, DW], ht_at + 38912)
        CROW = at("CROW", [P, T, 2 * DW], tmp_at)
        scr_at = tmp_at - 16384
        VECR = at("VECR", [P, P], tmp_at)
        VECC = at("VECC", [2 * KD, P], tmp_at + 512)
        COMB = at("COMB", [8, 2], ht_at + 29696)
        COMBB = at("COMBB", [8, P], ht_at + 29184)
        ONES = at("ONES", [P, P], cst_at)
        SUBG = place2("SUBG", [P, 8])
        LAM = place2("LAM", [P, 8])
        DFT = at("DFT", [P, T, 2 * S], cst_at)
        CCM = at("CCM", [P, 2, P], cst_at + 4096)

        for _v in ():
            pass
        SCRAP = place("SCRAP", [P, 32])
        scrap = iter(range(32))
        for sig, eng in ((silu_done, pool), (hth_done, pool), (out_act, pool), (out_dve, dve), (hid_done, dve), (htl_done, dve)):
            for _ in range(4):
                n_ = next(scrap)
                sig.on(eng.memset(SCRAP[:, n_:n_ + 1], 0.0))

        vec = {}
        row = 0
        wait_v = G_(pool.memset(VECR[:, :], 0.0))
        wait(act, wait_v)

        def vector_rows(name, src, rows):
            nonlocal row
            load_const(VECR[row:row + rows, :], src)
            vec[name] = row
            row += rows

        load_const(IDENT[:, :], A["ident"])
        for j, n in enumerate(("c", "c_ctx")):
            src = A[n].rearrange("o (k p) -> (o k) p", p=P) if n == "c" else A[n].rearrange("(k p) -> k p", p=P)
            load_const(VECC[j * KD:(j + 1) * KD, :], src)
        for l in range(2):
            vector_rows(f"mix{l}", A["mix_norm_g"][l, :].rearrange("(k p) -> k p", p=P), KD)
            vector_rows(f"ffn{l}", A["ffn_norm_g"][l, :].rearrange("(k p) -> k p", p=P), KD)
            vector_rows(f"ffn1_{l}", A["ffn1_norm_2"][l, :].rearrange("(k p) -> k p", p=P), KD)
            vector_rows(f"mix2_{l}", A["mix_norm_2"][l, :].rearrange("(k p) -> k p", p=P), KD)
            vector_rows(f"ffn2_{l}", A["ffn2_norm_2"][l, :].rearrange("(k p) -> k p", p=P), KD)
            vector_rows(f"lb{l}", A["hgrn_lb_logits_2"][l, :].rearrange("(k p) -> k p", p=P), 2)
            vector_rows(f"conv{l}", A["conv_w_2"][l, :, :].rearrange("t (k p) -> (t k) p", p=P), 6)
        for n in ("od_dw_b", "od_ln_g", "od_ln_b"):
            vector_rows(n, A[n][0, :].rearrange("(k p) -> k p", p=P), KD)
        vector_rows("subln", A["ev_subln_g"], 1)
        for l in range(2):
            for nm, key in (("foxq", "fox_q_gain_2"), ("foxk", "fox_k_gain_2")):
                for hh in range(2):
                    load_const(VECR[row:row + 1, hh * HD:(hh + 1) * HD], A[key][l:l + 1, :])
                vec[f"{nm}{l}"] = row
                row += 1
        load_const(COMB[0:5, :], A["comb"])
        load_const(COMBB[0:5, :], A["combb"])
        load_const(X[:, :, :], A["x"][0, :, :].rearrange("(t p) d -> p t d", p=P))
        load_const(CX[:, :, :], A["ctx"][0, :, :].rearrange("(t p) d -> p t d", p=P))
        load_const(DFT[:, :, :], A["dft"])
        load_const(CCM[:, :, :], A["ccm"])
        bias_row = load_const(ROW[4:5, :], A["ada_b"][0:1, :])

        wait(pe, bias_row)
        wait(dve, bias_row)
        x_mark[0] = bias_row
        m = M_(pe.transpose(bank[7][:, 0:P], VECR[:, :], IDENT[:, :]))
        mc = M_(pe.transpose(bank[6][:, 0:2 * KD], VECC[:, :], IDENT[0:2 * KD, 0:2 * KD]))
        wait(dve, m)
        cols_mark = V_(dve.tensor_copy(COLS[:, :], bank[7][:, 0:P]))
        wait(dve, mc)
        cs_mark = V_(dve.tensor_copy(CS[:, 0:2, :], bank[6][:, 0:2 * KD].rearrange("p (c k) -> p c k", c=2)))

        def col(name, n=KD):
            return COLS[:, vec[name]:vec[name] + n]

        m = V_(dve.memset(CT[:, :, :].bitcast(F32), 0.0))
        wait(act, bias_row, m, cs_mark)
        m = A_(act.activation(CS[:, 2:4, :], CS[:, 0:2, :], ACT.Silu))
        wait(act, m)
        c_src = CS[:, 2:4, :].rearrange("p c k -> p k c")
        m = A_(act.activation(CT[:, :, 0:2], c_src, ACT.Copy))
        wait(dve, m)
        ct_mark = V_(dve.tensor_tensor(CT[:, :, 2:4], c_src, CT[:, :, 0:2].bitcast(F32), ALU.subtract))

        def ada_parts(l):
            w = A["ada_w"][l, :, :]
            return up_parts(w, 0, w, HALF, CH)
        for _ in range(1):
            load_slabs(24, ada_parts(0))
        for _ in range(RING):
            split_next()

        def ada_chunk(c, i):
            b = bank[c % 2]
            wait(pe, out_act.now(1))
            for half in range(2):
                r = slab_ready(i)
                for k in range(4):
                    kk = 4 * half + k
                    st = CT[:, kk, :]
                    pe.matmul(b[:, :], st, hi[r][:, k * CH:(k + 1) * CH], start=(kk == 0), stop=False)
                    last = pe.matmul(b[:, :], st, lo[r][:, k * CH:(k + 1) * CH], start=False, stop=(kk == KD - 1))
                slab_used(last, i)
                if half == 0:
                    split_next(i)
            wait(act, slab_mark(i))
            off = c * CH if i is None else i * (2 * CH) + c * CH
            out_act.on(act.activation(ROW[0:4, bass.ds(off, CH)], b[0:4, :], ACT.Copy))
            split_next(i)

        def ada(l, ready):
            wait(pe, *ready)
            g0 = (g_split[0], g_use[0])
            with repeat(nc.Fori, 6, {out_act: 2}) as i:
                ada_chunk(0, i)
                ada_chunk(1, i)
            g_split[0], g_use[0] = g0[0] + 24, g0[1] + 24
            sync_ring()
            wait(pe, out_act.now())
            for n, mod in enumerate((0, 1, 3, 4)):
                for k in range(KD):
                    o = (n * KD + k) * 2
                    last = pe.matmul(bank[6][:, o:o + 2], ROW[0:5, mod * D + k * P:mod * D + (k + 1) * P],
                                     COMB[0:5, :], start=True, stop=True)
            m = M_(last)
            wait(dve, m)
            v = bank[6][:, 0:8 * KD].rearrange("p (n k c) -> p n k c", n=4, c=2)
            m1 = V_(dve.tensor_copy(MODS[:, l, :, :], v[:, :, :, 0]))
            if l == 0:
                m1 = V_(dve.tensor_copy(MODC[:, :, :], v[:, 0:2, :, 1]))
            wait(dve, m1)
            for n, g in ((1, f"mix{l}"), (3, f"ffn{l}")):
                m1 = V_(dve.scalar_tensor_tensor(out=MODS[:, l, n, :], in0=MODS[:, l, n, :], scalar=1.0,
                                                 in1=col(g), op0=ALU.add, op1=ALU.mult))
            if l == 0:
                m1 = V_(dve.scalar_tensor_tensor(out=MODC[:, 1, :], in0=MODC[:, 1, :], scalar=1.0,
                                                 in1=col("mix0"), op0=ALU.add, op1=ALU.mult))
            for n, mod in enumerate((2, 5)):
                for h in range(2):
                    last = pe.matmul(bank[2 + 2 * n + h][:, :], COMBB[0:5, :],
                                     ROW[0:5, mod * D + h * 512:mod * D + (h + 1) * 512], start=True, stop=True)
            m = M_(last)
            wait(act, m)
            for n in range(2):
                for h in range(2):
                    m2 = A_(act.activation(GATE[:, 2 * l + n, h * 512:(h + 1) * 512], bank[2 + 2 * n + h][:, :],
                                           ACT.Copy))
            return [m1, m2]

        ready = ada(0, [ct_mark, cols_mark])
        load_slabs(24, ada_parts(1))
        wait(act, *ready, s_pe.now())
        m = load_const(ROW[4:5, :], A["ada_b"][1:2, :])
        wait(pe, m)
        mods_ready = ada(1, [])

        w_in = A["ev_w_in"][0, :, :]
        cols5 = [(0, HALF), (512, 2304), (768, 1024), (1280, 1536), (1792, 2048)]
        for c, (a, b2) in enumerate(cols5):
            p_ = up_parts(w_in, a, w_in, b2)
            load_slabs(2, p_)
        w_out1 = A["ev_w_out"][0, :, :]
        load_slabs(4, down_parts(w_out1))

        wait(act, *mods_ready)
        wait(dve, *mods_ready)
        wait(pe, *mods_ready)
        xm = norm_columns(MODS[:, 0, 1, :], MODS[:, 0, 0, :])
        cm = norm_columns(MODC[:, 1, :], MODC[:, 0, :], CTXh, CTXl, CX, bias_row)
        wait(pe, *xm, *cm)
        stats = tiles(XTh, XTl)
        stats_c = tiles(CTXh, CTXl)
        reads = {}
        for c, (a, b2) in enumerate(cols5):
            both = c >= 2
            o = 4 * (c % 2)
            banks = bank[o:o + 4] if both else bank[o:o + 2]
            wait(pe, reads.get(o), reads.get(o + 1))
            if c == 0:
                wait(pe, s_act.now(), s_dve.now())
            chunk_slab(0, banks, stats + (stats_c if both else []))
            split_next()
            chunk_slab(1, banks, stats + (stats_c if both else []))
            done = slab_mark()
            wait(act, done)
            wait(dve, done)
            for j, cc in enumerate((a, b2)):
                src = slice(j * HALF, (j + 1) * HALF)
                m1 = A_(act.activation(UROW[:, 0, cc:cc + HALF], banks[0][:, src], ACT.Copy))
                m2 = V_(dve.tensor_copy(UROW[:, 1, cc:cc + HALF], banks[1][:, src]))
                if both:
                    m1 = A_(act.activation(CROW[:, 0, cc - DW:cc - DW + HALF], banks[2][:, src], ACT.Copy))
                    m2 = V_(dve.tensor_copy(CROW[:, 1, cc - DW:cc - DW + HALF], banks[3][:, src]))
            reads[o], reads[o + 1] = m1, m2
            split_next()
        rows_ready = (m1, m2)

        def scr(name, shape, off, dt=F32):
            return at(name, shape, scr_at + off, dt)
        ROPE = place("ROPE", [P, T, 2, 32])
        assert used_bytes[0] <= nc.sbuf_usable_end, used_bytes[0]
        rope_mark = load_const(ROPE[:, :, :, :], A["rope"])
        free = pe_idle()
        for eng, did, base, off in ((dve, V_, 0, 0), (pool, G_, DW, 6144)):
            tl = [scr(f"rt{off}_{n}", [P, 12, 32], off + n * 1536) for n in range(4)]
            wait(eng, rope_mark, *rows_ready, *free)
            for t in range(T):
                rows = UROW[:, t, base:base + DW].rearrange("p (h x d) -> p h x d", h=12, x=2)
                cos = ROPE[:, t, 0:1, :].broadcast_to([P, 12, 32])
                sin = ROPE[:, t, 1:2, :].broadcast_to([P, 12, 32])
                x1, x2 = rows[:, :, 0, :], rows[:, :, 1, :]
                for dst, u, v in ((tl[0], x1, cos), (tl[1], x2, sin), (tl[2], x1, sin), (tl[3], x2, cos)):
                    m = did(eng.tensor_tensor(dst[:, :, :], u, v, ALU.mult))
                wait(eng, m)
                m = did(eng.tensor_tensor(x1, tl[0][:, :, :], tl[1][:, :, :], ALU.subtract))
                m = did(eng.tensor_tensor(x2, tl[2][:, :, :], tl[3][:, :, :], ALU.add))
                wait(eng, m)
            if eng is dve:
                q_mark = m
            else:
                k_mark = m
        wait(pe, *rows_ready, IDENT and None)
        bank_read = {}
        n = 0
        for src, dst, s0, mk in ((CROW[:, :, 0:DW], KT, 0, None), (UROW[:, :, 0:DW], QT, 0, q_mark),
                                 (UROW[:, :, DW:2 * DW], KT, S, k_mark)):
            wait(pe, mk)
            for hp in range(0, HEADS1, 2):
                b = bank[n % 8]
                wait(pe, bank_read.get(n % 8))
                for h in (hp, hp + 1):
                    for t in range(T):
                        last = pe.transpose(b[:, (h - hp) * S + t * P:(h - hp) * S + (t + 1) * P],
                                            src[:, t, h * P:(h + 1) * P], IDENT[:, :])
                m = M_(last)
                out_ap = dst[:, hp:hp + 2, s0:s0 + S]
                in_ap = b[:, :].rearrange("p (h s) -> p h s", h=2)
                if n % 2:
                    wait(act, m)
                    bank_read[n % 8] = A_(act.activation(out_ap, in_ap, ACT.Copy))
                else:
                    wait(dve, m)
                    bank_read[n % 8] = V_(dve.tensor_copy(out_ap, in_ap))
                n += 1
        heads_ready = [s_act.now(), s_dve.now()]

        LQ = scr("LQ", [P, 4, HD], 12288)
        wait(act, *heads_ready, s_pool.now())
        for n, name in enumerate(("ev_lambda_q1", "ev_lambda_k1", "ev_lambda_q2", "ev_lambda_k2")):
            m = load_const(LQ[:, n, :], A[name][0, :].partition_broadcast(P))
        wait(dve, m)
        for n in range(2):
            m = V_(dve.tensor_tensor(LQ[:, 2 * n, :], LQ[:, 2 * n, :], LQ[:, 2 * n + 1, :], ALU.mult))
        wait(dve, m)
        for n in range(2):
            m = V_(dve.tensor_reduce(LAM[:, n:n + 1], LQ[:, 2 * n, :], AX.X, ALU.add))
        wait(act, m)
        m = A_(act.activation(LAM[:, 2:4], LAM[:, 0:2], ACT.Exp))
        wait(dve, m)
        m = V_(dve.tensor_scalar(LAM[:, 5:6], LAM[:, 3:4], LAMBDA_INIT, None, ALU.subtract))
        wait(dve, m)
        lam_mark = V_(dve.tensor_tensor(LAM[:, 4:5], LAM[:, 2:3], LAM[:, 5:6], ALU.subtract))

        P0 = [scr(f"P0_{j}", [P, 2 * S], 2048 * j) for j in range(2)]
        P1 = [scr(f"P1_{j}", [P, 2 * S], 4096 + 2048 * j) for j in range(2)]
        AT = [scr(f"AT_{j}", [P, 4, P], 8192 + 2048 * j) for j in range(2)]
        units = [(h, t) for h in range(HEADS1) for t in range(T)]
        wait(pe, *heads_ready)
        wait(act, lam_mark, s_pool.now())
        wait(dve, lam_mark, s_pool.now())
        marks = {}

        def diff_scores(u):
            h, t = units[u]
            j = u % 2
            if u >= 2:
                wait(pe, marks["exp", u - 2])
            for c in range(2):
                cs = slice(c * HD, (c + 1) * HD)
                last = pe.matmul(bank[2 * j + c][:, :], QT[cs, h, t * P:(t + 1) * P], KT[cs, h, :],
                                 start=True, stop=True)
            marks["s", u] = M_(last)

        def diff_softmax(u):
            j = u % 2
            st = ST[:, 8 * j:8 * j + 8]
            wait(dve, marks["s", u])
            for c in range(2):
                m = V_(dve.tensor_reduce(st[:, c:c + 1], bank[2 * j + c][:, :], AX.X, ALU.max))
            wait(dve, m)
            m = V_(dve.tensor_scalar(st[:, 2:4], st[:, 0:2], -HD ** -0.5, None, ALU.mult))
            wait(act, m)
            if u >= 2:
                wait(act, marks["at", u - 2], marks["t", u - 2])
            for c, pb in ((0, P0[j]), (1, P1[j])):
                m = A_(act.activation(pb[:, :], bank[2 * j + c][:, :], ACT.Exp, bias=st[:, 2 + c:3 + c],
                                      scale=HD ** -0.5, accum_out=st[:, 4 + c:5 + c]))
            marks["exp", u] = m
            wait(dve, m)
            m = V_(dve.reciprocal(st[:, 6:8], st[:, 4:6]))
            wait(dve, m)
            m = V_(dve.tensor_scalar(st[:, 7:8], st[:, 7:8], LAM[:, 4:5], None, ALU.mult))
            wait(dve, m)
            m = V_(dve.tensor_scalar(P1[j][:, :], P1[j][:, :], st[:, 7:8], None, ALU.mult))
            wait(dve, m)
            marks["a", u] = V_(dve.scalar_tensor_tensor(out=P0[j][:, :], in0=P0[j][:, :], scalar=st[:, 6:7],
                                                        in1=P1[j][:, :], op0=ALU.mult, op1=ALU.subtract))

        def diff_turn(u):
            j = u % 2
            wait(pe, marks["a", u])
            if u >= 2:
                wait(pe, marks["at", u - 2])
            for kt in range(4):
                last = pe.transpose(bank[4 + j][:, kt * P:(kt + 1) * P], P0[j][:, kt * P:(kt + 1) * P], IDENT[:, :])
            marks["t", u] = M_(last)
            wait(act, marks["t", u])
            if u >= 2:
                wait(act, marks["pv", u - 2])
            marks["at", u] = A_(act.activation(AT[j][:, :, :], bank[4 + j][:, :].rearrange("p (k q) -> p k q", k=4),
                                               ACT.Copy))

        def diff_values(u):
            h, t = units[u]
            j = u % 2
            wait(pe, marks["at", u])
            if u >= 2:
                wait(pe, marks["o", u - 2])
            for kt in range(4):
                v = CROW[:, kt, DW + h * P:DW + (h + 1) * P] if kt < 2 else \
                    UROW[:, kt - 2, 2 * DW + h * P:2 * DW + (h + 1) * P]
                last = pe.matmul(bank[6 + j][:, 0:P], AT[j][:, kt, :], v, start=(kt == 0), stop=(kt == 3))
            marks["pv", u] = M_(last)
            wait(dve, marks["pv", u])
            marks["o", u] = V_(dve.tensor_copy(OROW[:, t, h * P:(h + 1) * P], bank[6 + j][:, 0:P]))

        N = len(units)
        diff_scores(0)
        for u in range(N):
            if u + 1 < N:
                diff_scores(u + 1)
            diff_softmax(u)
            if u >= 1:
                diff_values(u - 1)
            diff_turn(u)
        diff_values(N - 1)

        U1 = scr("U1", [P, 2, 2 * S], 0)
        ZT = scr("ZT", [P, 2, S], 4096)
        WB = scr("WB", [P, 2, P], 6144)
        SQ = scr("SQ", [P, T, DW], 8192)
        wait(pool, *pe_idle(), s_act.now(), s_dve.now())
        m = G_(pool.memset(WB[:, :, :], 0.0))
        wait(act, m)
        for g in range(4):
            o = (g % 2) * HD
            wb_mark = load_const(WB[o:o + HD, g // 2, o:o + HD], A["ev_fourier_w"][0, g, :, :])
        wait(pe, s_act.now(), s_dve.now())
        for mt in range(2):
            for t in range(T):
                last = pe.matmul(bank[mt][:, :], UROW[:, t, 2304 + mt * P:2304 + (mt + 1) * P], DFT[:, t, :],
                                 start=(t == 0), stop=(t == T - 1))
        m = M_(last)
        wait(dve, m)
        for mt in range(2):
            m = V_(dve.tensor_copy(U1[:, mt, :], bank[mt][:, :]))
        wait(pe, m)
        for mt in range(2):
            pe.matmul(bank[2][:, mt * S:(mt + 1) * S], CCM[:, 0, :], U1[:, mt, 0:S], start=True, stop=False)
            last = pe.matmul(bank[2][:, mt * S:(mt + 1) * S], CCM[:, 1, :], U1[:, mt, S:2 * S], start=False, stop=True)
        m = M_(last)
        wait(dve, m)
        m = V_(dve.tensor_copy(ZT[:, :, :], bank[2][:, :].rearrange("p (m s) -> p m s", m=2)))
        wait(pe, m, wb_mark)
        for mt in range(2):
            last = pe.matmul(bank[3][:, mt * S:(mt + 1) * S], WB[:, mt, :], ZT[:, mt, :], start=True, stop=True)
        four_mark = M_(last)

        o_ready = [s_dve.now(), s_act.now()]
        for t in range(T):
            wait(dve, *o_ready)
            m = V_(dve.tensor_tensor(SQ[:, t, :], OROW[:, t, :], OROW[:, t, :], ALU.mult))
            wait(dve, m)
            o = 16 + 8 * t
            m = V_(dve.tensor_reduce(ST[:, o:o + 6], SQ[:, t, :].rearrange("p (h d) -> p h d", h=HEADS1), AX.X, ALU.add))
            wait(dve, m)
            m = V_(dve.tensor_scalar(ST[:, o:o + 6], ST[:, o:o + 6], 1.0 / VD, EPS, ALU.mult, ALU.add))
            wait(act, m)
            m = A_(act.activation(ST[:, o:o + 6], ST[:, o:o + 6], ACT.Sqrt))
            wait(dve, m)
            m = V_(dve.reciprocal(ST[:, o:o + 6], ST[:, o:o + 6]))
            wait(dve, m)
            ov = OROW[:, t, :].rearrange("p (h d) -> p h d", h=HEADS1)
            m = V_(dve.tensor_tensor(ov, ov, ST[:, o:o + 6].unsqueeze(2).broadcast_to([P, HEADS1, VD]), ALU.mult))
        o_mark = m
        m = V_(dve.tensor_scalar(SUBG[:, 0:1], COLS[:, vec["subln"]:vec["subln"] + 1], 1.0 - LAMBDA_INIT, None, ALU.mult))
        wait(dve, m)
        m = V_(dve.tensor_copy(SUBG[:, 1:7], SUBG[:, 0:1].broadcast_to([P, 6])))
        wait(dve, m)
        ym = to_columns(OROW, [o_mark], SUBG, None, XTh, XTl, [four_mark, s_dve.now()], kn=6, banks=(4, 5, 6))
        wait(dve, four_mark)
        m = V_(dve.tensor_copy(FULL[:, 6:8, :], bank[3][:, :].rearrange("p (m s) -> p m s", m=2)))
        wait(act, m)
        h = A_(act.activation(XTh[:, 6:8, :], FULL[:, 6:8, :], ACT.Copy))
        wait(dve, h)
        l = V_(dve.tensor_tensor(XTl[:, 6:8, :], FULL[:, 6:8, :], XTh[:, 6:8, :].bitcast(F32), ALU.subtract))
        down(4, XTh, XTl, [*ym, h, l, *acc_free()])
        add_residual(gate=0)

        def ffn1(l, gate):
            load_slabs(2 * (KF // 2), up_parts(A["ffn_w1"][l, :, :], 0, A["ffn_w3"][l, :, :], 0))
            load_slabs(KF // 2, down_parts(A["ffn_w2"][l, :, :]))
            ffn(MODS[:, l, 3, :], MODS[:, l, 2, :], lambda: add_residual(gate=gate))

        ffn1(0, 1)

        load_slabs(8, up_parts(A["od_pw1_w"][0, :, :], 0, A["od_pw1_w"][0, :, :], D))
        load_slabs(4, down_parts(A["od_pw2_w"][0, :, :]))
        PAD = TAPS // 2
        B1 = at("B1", [P, 2 * D], ht_at)
        UR = at("UR", [P, T, D], ht_at + 8192)
        UT = at("UT", [P, KD, 288], ht_at + 16384)
        CV = at("CV", [P, KD, S], ht_at + 25600)
        DWR = at("DWR", [32, D], ht_at + 33792)
        DWW = at("DWW", [P, KD, 32], ht_at + 37888)
        B2 = at("B2", [P, D], ht_at + 38912)
        MEAN = at("MEAN", [P, S], ht_at + 43008)
        RSTD = at("RSTD", [P, S], ht_at + 44032)
        free = [*pe_idle(), s_act.now(), s_dve.now(), htl_done.now(), hth_done.now()]
        wait(act, *free)
        wait(pool, *free)
        for h in range(2):
            load_const(B1[:, h * D:(h + 1) * D], A["od_pw1_b"][0, h * D:(h + 1) * D].partition_broadcast(P))
        load_const(B2[:, :], A["od_pw2_b"][0, :].partition_broadcast(P))
        conv_in = load_const(DWR[0:TAPS, :], A["od_dw_w"][0, :, :])
        pad_mark = G_(pool.memset(UT[:, :, :], 0.0))
        ones_mark = G_(pool.memset(ONES[:, :], 1.0 / D))
        xm = norm_columns(MODS[:, 1, 1, :], MODS[:, 1, 0, :])
        wait(pe, conv_in)
        for k in range(KD):
            last = pe.transpose(bank[3][:, k * 32:k * 32 + TAPS], DWR[0:TAPS, k * P:(k + 1) * P], IDENT[0:TAPS, 0:TAPS])
        m = M_(last)
        wait(dve, m)
        dww_mark = V_(dve.tensor_copy(DWW[:, :, 0:TAPS], bank[3][:, 0:8 * 32].rearrange("p (k j) -> p k j", k=KD)[:, :, 0:TAPS]))
        wait(pe, *xm, dww_mark)
        wait(dve, conv_in)
        read = {}
        for c in range(4):
            banks = [bank[2 * (c % 2) + t] for t in range(T)]
            wait(pe, read.get(c - 2))
            chunk_slab(0, banks, tiles(XTh, XTl))
            split_next()
            chunk_slab(1, banks, tiles(XTh, XTl))
            done = slab_mark()
            wait(dve, done, s_act.now(), s_dve.now())
            cs, gs = slice(c * HALF, (c + 1) * HALF), slice(D + c * HALF, D + (c + 1) * HALF)
            for t in range(T):
                m = V_(dve.tensor_tensor(SG[:, t, :], banks[t][:, HALF:CH], B1[:, gs], ALU.add))
                V_(dve.tensor_tensor(HID[:, t, :], banks[t][:, 0:HALF], B1[:, cs], ALU.add))
                wait(act, m)
                A_(act.activation(SG[:, t, :], SG[:, t, :], ACT.Sigmoid))
            read[c] = s_dve.now()
            wait(dve, s_act.now(), s_dve.now())
            for t in range(T):
                ur_mark = V_(dve.tensor_tensor(UR[:, t, cs], HID[:, t, :], SG[:, t, :], ALU.mult))
            split_next()
        wait(pe, ur_mark)
        wait(act, pad_mark)
        for kp in range(4):
            b = bank[4 + kp]
            for k in (2 * kp, 2 * kp + 1):
                for t in range(T):
                    last = pe.transpose(b[:, (k % 2) * S + t * P:(k % 2) * S + (t + 1) * P],
                                        UR[:, t, k * P:(k + 1) * P], IDENT[:, :])
            wait(act, M_(last))
            ut_mark = A_(act.activation(UT[:, 2 * kp:2 * kp + 2, PAD:PAD + S],
                                        b[:, :].rearrange("p (k s) -> p k s", k=2), ACT.Copy))
        wait(dve, ut_mark, dww_mark)
        for j in range(TAPS):
            mk = []
            for k in range(KD):
                if j >= 1:
                    wait(dve, prev[k])
                if j == 0:
                    m = V_(dve.tensor_scalar(CV[:, k, :], UT[:, k, 0:S], DWW[:, k, 0:1], col("od_dw_b")[:, k:k + 1],
                                             ALU.mult, ALU.add))
                else:
                    m = V_(dve.scalar_tensor_tensor(out=CV[:, k, :], in0=UT[:, k, j:j + S], scalar=DWW[:, k, j:j + 1],
                                                    in1=CV[:, k, :], op0=ALU.mult, op1=ALU.add))
                mk.append(m)
            prev = mk
        wait(pe, *prev, ones_mark)
        for k in range(KD):
            last = pe.matmul(bank[0][:, 0:S], ONES[:, :], CV[:, k, :], start=(k == 0), stop=(k == KD - 1))
        wait(dve, M_(last))
        m = V_(dve.tensor_copy(MEAN[:, :], bank[0][:, 0:S]))
        wait(dve, m)
        m = V_(dve.tensor_tensor(CV[:, :, :], CV[:, :, :], MEAN[:, :].unsqueeze(1).broadcast_to([P, KD, S]), ALU.subtract))
        wait(act, m)
        m = A_(act.activation(UT[:, :, 0:S], CV[:, :, :], ACT.Square))
        wait(pe, m)
        for k in range(KD):
            last = pe.matmul(bank[1][:, 0:S], ONES[:, :], UT[:, k, 0:S], start=(k == 0), stop=(k == KD - 1))
        wait(dve, M_(last))
        m = V_(dve.tensor_scalar(RSTD[:, :], bank[1][:, 0:S], EPS, None, ALU.add))
        wait(act, m)
        m = A_(act.activation(RSTD[:, :], RSTD[:, :], ACT.Sqrt))
        wait(dve, m)
        m = V_(dve.reciprocal(RSTD[:, :], RSTD[:, :]))
        wait(dve, m)
        m = V_(dve.tensor_tensor(CV[:, :, :], CV[:, :, :], RSTD[:, :].unsqueeze(1).broadcast_to([P, KD, S]), ALU.mult))
        wait(act, m)
        for k in range(KD):
            m = A_(act.activation(FULL[:, k, :], CV[:, k, :], ACT.Silu, scale=col("od_ln_g")[:, k:k + 1],
                                  bias=col("od_ln_b")[:, k:k + 1]))
        wait(act, m)
        h = A_(act.activation(XTh[:, :, :], FULL[:, :, :], ACT.Copy))
        wait(dve, h)
        l = V_(dve.tensor_tensor(XTl[:, :, :], FULL[:, :, :], XTh[:, :, :].bitcast(F32), ALU.subtract))
        down(4, XTh, XTl, [h, l, *acc_free()])
        add_residual(gate=2, bias=B2)
        ffn1(1, 3)

        wait(act, x_mark[0])
        m = load_const(GATE[:, 0, :], A["final_g"].partition_broadcast(P))
        wait(dve, m)
        for t in range(T):
            r_ = rstd_of(X[:, t, :], t, D, t, [x_mark[0], *pe_idle()], XN[:, t, :])
            wait(dve, r_)
            m = V_(dve.scalar_tensor_tensor(out=X[:, t, :], in0=X[:, t, :], scalar=ST[:, t:t + 1], in1=GATE[:, 0, :],
                                            op0=ALU.mult, op1=ALU.mult))
        x_mark[0] = m

        UM = at("UM", [P, T, MIX_IN - FOX_H], ht_at)
        o_cx, o_cb, o_cc, o_hq, o_hf, o_hv, o_hg, o_fq, o_fk, o_fv = 0, 256, 512, 768, 1024, 1280, 1536, 1792, 2304, 2816
        NQK = 8
        QKT = at("QKT", [P, NQK, S], ht_at + 26624)
        YR = at("YR", [P, T, DW], ht_at + 34816)
        Q2, ZT2, K2, BC, EX, QKa, QKb, TM = (at(f"hg_{n}", [P, 2, S], scr_at + 2048 * n) for n in range(8))
        HA = at("HA", [P, 2, 4, P], tmp_at)
        HX = at("HX", [P, 4, P], tmp_at + 4096)
        TN = at("TN", [P, 2, S], tmp_at + 6144)
        FS = [at(f"FS{j}", [P, S], tmp_at + 8192 + 1024 * j) for j in range(2)]
        FP = [at(f"FP{j}", [P, S], tmp_at + 10240 + 1024 * j) for j in range(2)]
        FT = [at(f"FT{j}", [P, T, P], tmp_at + 12288 + 1024 * j) for j in range(2)]
        K1 = at("K1", [P, 2, S], gate_at)
        Q1 = at("Q1", [P, 2, S], gate_at + 2048)
        CU = at("CU", [P, T, HALF], gate_at + 4096)
        CUT = at("CUT", [P, 2, S + 4], gate_at + 6144)
        CBT = at("CBT", [P, 2, S], gate_at + 8256)
        FZ = at("FZ", [P, 4, T, FOX_H], gate_at + 10304)
        NCT = at("NCT", [FOX_H, S], gate_at + 10560)
        CC = at("CC", [P, T, FOX_H], gate_at + 11584)
        OG = at("OG", [P, HD], gate_at + 11648)
        FB = at("FB", [P, FOX_H], gate_at + 11904)
        GS = at("GS", [P, T, HALF], gate_at + 11968)
        WF = at("WF", [P, KD, FOX_H], gate_at + 14016)
        FST = at("FST", [P, 2, T, 16], gate_at + 14272)
        LB = at("LB", [P, 8, 2], gate_at + 14528)
        TRI = at("TRI", [P, 2, P], cst_at)
        MASKS = at("MASKS", [P, 8, P], cst_at + 1024, U8)
        MB = at("MB", [P, 2, P], cst_at + 2048)
        RESET = at("RESET", [P, 2, S], cst_at + 3072)

        free = [*pe_idle(), s_act.now(), s_dve.now()]
        wait(act, *free)
        wait(pool, *free)
        wait(dve, *free)
        load_const(TRI[:, :, :], A["tri"])
        MASKF = at("MASKF", [P, 8, P], tmp_at)
        load_const(MASKF[:, :, :], A["masks"])
        mb_mark = load_const(MB[:, :, :], A["causal"])
        wait(dve, mb_mark)
        c2_mark = V_(dve.tensor_copy(MASKS[:, :, :], MASKF[:, :, :]))
        m = G_(pool.memset(RESET[:, :, :], 1.0))
        wait(pool, m)
        reset_mark = G_(pool.memset(RESET[:, :, :].rearrange("p k (c n) -> p k c n", n=64)[:, :, :, 0:1], 0.0))
        l0, l1 = col("lb0", 2), col("lb1", 2)
        m = V_(dve.tensor_tensor(LB[:, 0, :], l0, l1, ALU.max))
        wait(dve, m)
        V_(dve.tensor_tensor(LB[:, 1, :], l0, LB[:, 0, :], ALU.subtract))
        m = V_(dve.tensor_tensor(LB[:, 2, :], l1, LB[:, 0, :], ALU.subtract))
        wait(act, m)
        m = A_(act.activation(LB[:, 3:5, :], LB[:, 1:3, :], ACT.Exp))
        wait(dve, m)
        m = V_(dve.tensor_tensor(LB[:, 5, :], LB[:, 3, :], LB[:, 4, :], ALU.add))
        wait(dve, m)
        m = V_(dve.reciprocal(LB[:, 5, :], LB[:, 5, :]))
        wait(dve, m)
        V_(dve.tensor_tensor(LB[:, 1, :], LB[:, 3, :], LB[:, 5, :], ALU.mult))
        m = V_(dve.tensor_tensor(LB[:, 2, :], LB[:, 4, :], LB[:, 5, :], ALU.mult))
        wait(dve, m)
        m = V_(dve.tensor_tensor(LB[:, 6, :], LB[:, 1, :], LB[:, 2, :], ALU.add))
        wait(dve, m)
        V_(dve.tensor_tensor(LB[:, 0, :], LB[:, 1, :], LB[:, 1, :], ALU.subtract))
        m = V_(dve.tensor_tensor(LB[:, 7, :], LB[:, 6, :], LB[:, 1, :], ALU.subtract))
        wait(dve, m)
        for l, r0 in ((0, 0), (1, 7)):
            m = V_(dve.tensor_scalar(LB[:, 2 * l, :], LB[:, r0, :], 0.0, 1.0, ALU.max, ALU.min))
            wait(dve, m)
            m = V_(dve.tensor_scalar(LB[:, 2 * l + 1, :], LB[:, 2 * l, :], -1.0, 1.0, ALU.mult, ALU.add))
            wait(dve, m)
        lb_mark = m

        def ffn2(w_in_, w_out_, l, gains):
            w = A[w_in_][l, :, :]
            load_slabs(2 * (KF // 2), up_parts(w, 0, w, FF))
            load_slabs(KF // 2, down_parts(A[w_out_][l, :, :]))
            ffn(gains, None, lambda: add_residual(half=True))

        def wide_parts(w, c0):
            v = row_tiles(w)

            def into(slot):
                d = slot[:, :].rearrange("p (k n) -> p k n", k=KD)
                return [(d[:, 4 * h:4 * h + 4, :], v[:, 4 * h:4 * h + 4, c0:c0 + HALF]) for h in range(2)]
            return into

        def mix_in(l):
            w = A["w_mix_in_2"][l, :, :]
            load_slabs(12, up_parts(w, 0, w, HALF, CH))
            load_slab(wide_parts(w, 3072))
            load_slabs(4, down_parts(A["w_mix_out_2"][l, :, :]))
            free = [*pe_idle(), s_act.now(), s_dve.now()]
            wait(act, *free)
            load_const(WF[:, :, :], row_tiles(w)[:, :, MIX_IN - FOX_H:MIX_IN])
            load_const(FB[:, :], A["fox_f_bias_2"][l, :].partition_broadcast(P))
            small = load_const(OG[:, :], A["hgrn_out_gain_2"][l, :].partition_broadcast(P))
            xm = norm_columns(col(f"mix2_{l}"), None)
            wait(pe, *xm, small)
            for t in range(T):
                for k in range(KD):
                    last = pe.matmul(bank[7][:, t * FOX_H:(t + 1) * FOX_H], FULL[:, k, t * P:(t + 1) * P], WF[:, k, :],
                                     start=(k == 0), stop=(k == KD - 1))
            m = M_(last)
            wait(dve, m, small)
            z_mark = V_(dve.tensor_tensor(FZ[:, 0, :, :], bank[7][:, 0:T * FOX_H].rearrange("p (t h) -> p t h", t=T),
                                          FB[:, :].unsqueeze(1).broadcast_to([P, T, FOX_H]), ALU.add))
            wait(act, *xm)
            wait(dve, *xm)

            def chunk(c, i):
                banks = [bank[2 * (c % 2) + t] for t in range(T)]
                wait(pe, out_act.now(1), out_dve.now(1))
                chunk_slab(0, banks, tiles(XTh, XTl), i)
                split_next(i)
                chunk_slab(1, banks, tiles(XTh, XTl), i)
                done = slab_mark(i)
                wait(act, done)
                wait(dve, done)
                off = i * (2 * CH) + c * CH
                out_act.on(act.activation(UM[:, 0, bass.ds(off, CH)], banks[0][:, :], ACT.Copy))
                out_dve.on(dve.tensor_copy(UM[:, 1, bass.ds(off, CH)], banks[1][:, :]))
                split_next(i)

            g0 = (g_split[0], g_use[0])
            with repeat(nc.Fori, 3, {out_act: 2, out_dve: 2}) as i:
                chunk(0, i)
                chunk(1, i)
            g_split[0], g_use[0] = g0[0] + 12, g0[1] + 12
            sync_ring()
            wait(pe, out_act.now(), out_dve.now())
            r = slab_ready()
            for k in range(KD):
                wh, wl = hi[r][:, k * HALF:(k + 1) * HALF], lo[r][:, k * HALF:(k + 1) * HALF]
                for t, (xh, xl) in enumerate(tiles(XTh, XTl)):
                    last = three(bank[t][:, 0:HALF], xh(k), xl(k), wh, wl, k == 0, k == KD - 1)
            slab_used(last)
            wait(act, slab_mark())
            wait(dve, slab_mark())
            A_(act.activation(UM[:, 0, 3072:3328], bank[0][:, 0:HALF], ACT.Copy))
            V_(dve.tensor_copy(UM[:, 1, 3072:3328], bank[1][:, 0:HALF]))
            split_next()
            return [s_act.now(), s_dve.now(), out_act.now(), out_dve.now(), z_mark]

        def conv3(l, rows):
            wait(dve, *rows)
            wait(pe, *rows)
            wait(pool, *rows)
            zero = G_(pool.memset(CUT[:, :, 0:2], 0.0))
            m = V_(dve.tensor_tensor(CU[:, :, :], UM[:, :, o_cx:o_cx + HALF], UM[:, :, o_cc:o_cc + HALF], ALU.mult))
            wait(pe, m)
            for n, src in enumerate((CU[:, :, :], UM[:, :, o_cb:o_cb + HALF])):
                for k in range(2):
                    for t in range(T):
                        last = pe.transpose(bank[2 + n][:, k * S + t * P:k * S + (t + 1) * P], src[:, t, k * P:(k + 1) * P],
                                            IDENT[:, :])
            m = M_(last)
            wait(act, m, zero)
            A_(act.activation(CUT[:, :, 2:2 + S], bank[2][:, :].rearrange("p (k s) -> p k s", k=2), ACT.Copy))
            m = A_(act.activation(CBT[:, :, :], bank[3][:, :].rearrange("p (k s) -> p k s", k=2), ACT.Copy))
            wait(dve, m)
            v0 = vec[f"conv{l}"]
            for k in range(2):
                for j in range(3):
                    w = COLS[:, v0 + 2 * j + k:v0 + 2 * j + k + 1]
                    if j == 0:
                        m = V_(dve.tensor_scalar(CU[:, k, :], CUT[:, k, 0:S], w, None, ALU.mult))
                    else:
                        m = V_(dve.scalar_tensor_tensor(out=CU[:, k, :], in0=CUT[:, k, j:j + S], scalar=w, in1=CU[:, k, :],
                                                        op0=ALU.mult, op1=ALU.add))
                    wait(dve, m)
            m = V_(dve.tensor_tensor(CBT[:, :, :], CBT[:, :, :], CU[:, :, :], ALU.mult))
            wait(act, m)
            h = A_(act.activation(XTh[:, 0:2, :], CBT[:, :, :], ACT.Copy)) if False else None
            return m

        def hgrn(l, rows):
            wait(pe, *rows)
            for n, o in enumerate((o_hq, o_hf)):
                for k in range(2):
                    for t in range(T):
                        last = pe.transpose(bank[n][:, k * S + t * P:k * S + (t + 1) * P],
                                            UM[:, t, o + k * P:o + (k + 1) * P], IDENT[:, :])
            wait(dve, M_(last), *rows)
            for n, dst in enumerate((Q2, ZT2)):
                m = V_(dve.tensor_copy(dst[:, :, :], bank[n][:, :].rearrange("p (k s) -> p k s", k=2)))
            wait(dve, m, lb_mark)
            wait(act, m, lb_mark)
            m = A_(act.activation(K2[:, :, :], ZT2[:, :, :], ACT.Sigmoid, scale=-1.0))
            wait(dve, m)
            for k in range(2):
                V_(dve.tensor_scalar(K2[:, k, :], K2[:, k, :], LB[:, 2 * l + 1, k:k + 1], None, ALU.mult))
            V_(dve.tensor_scalar(EX[:, :, :], ZT2[:, :, :], 0.0, None, ALU.min))
            V_(dve.scalar_tensor_tensor(out=QKa[:, :, :], in0=ZT2[:, :, :], scalar=0.5, in1=ZT2[:, :, :],
                                        op0=ALU.mult, op1=ALU.max))
            m = V_(dve.scalar_tensor_tensor(out=QKb[:, :, :], in0=ZT2[:, :, :], scalar=-1.0, in1=ZT2[:, :, :],
                                            op0=ALU.mult, op1=ALU.max))
            wait(act, m)
            A_(act.activation(TM[:, :, :], EX[:, :, :], ACT.Exp, scale=0.5))
            A_(act.activation(TN[:, :, :], QKa[:, :, :], ACT.Exp, scale=-1.0))
            m = A_(act.activation(ZT2[:, :, :], QKb[:, :, :], ACT.Exp, scale=-1.0))
            wait(dve, m)
            for k in range(2):
                m = V_(dve.scalar_tensor_tensor(out=QKa[:, k, :], in0=TN[:, k, :], scalar=LB[:, 2 * l, k:k + 1],
                                                in1=TM[:, k, :], op0=ALU.mult, op1=ALU.add))
            m = V_(dve.tensor_scalar(QKb[:, :, :], ZT2[:, :, :], 1.0, None, ALU.add))
            wait(act, m)
            A_(act.activation(TN[:, :, :], QKa[:, :, :], ACT.Ln))
            m = A_(act.activation(TM[:, :, :], QKb[:, :, :], ACT.Ln))
            wait(dve, m)
            m = V_(dve.scalar_tensor_tensor(out=TN[:, :, :], in0=EX[:, :, :], scalar=0.5, in1=TN[:, :, :],
                                            op0=ALU.mult, op1=ALU.add))
            wait(dve, m)
            m = V_(dve.tensor_tensor(TM[:, :, :], TN[:, :, :], TM[:, :, :], ALU.subtract))
            wait(dve, m, reset_mark)
            flat = lambda x: x[:, :, :].rearrange("p k s -> p (k s)")
            m = V_(dve.tensor_tensor_scan(flat(BC), flat(RESET), flat(TM), 0.0, ALU.mult, ALU.add))
            wait(dve, m)
            blk = lambda x, n: x[:, :, :].rearrange("p k (c n) -> p (k c) n", n=n)
            mark_free = {0: [s_dve.now()], 1: [s_dve.now()]}
            zero = V_(dve.memset(HA[:, :, :, :], 0.0))

            def products(lhs, rhs, pair, ready, cross=False):
                wait(pe, *ready, *mark_free[pair])
                for h in range(HG_H):
                    for t in range(1 if cross else T):
                        rows_ = slice((h % 2) * HD, (h % 2 + 1) * HD)
                        s_at, t_at = (0, P) if cross else (t * P, t * P)
                        o = (2 * t + h // 2) * P
                        last = pe.matmul(bank[2 * pair + h % 2][:, o:o + P], lhs[rows_, h // 2, s_at:s_at + P],
                                         rhs[rows_, h // 2, t_at:t_at + P], start=True, stop=True)
                return M_(last)

            def select(level, pair, done):
                wait(dve, done, zero, s_dve.now(), c2_mark)
                for t in range(T):
                    mask = MASKS[:, level, :].unsqueeze(1).broadcast_to([P, HG_H, P])
                    m = V_(dve.copy_predicated(HA[:, t, :, :], mask,
                                               bank[2 * pair + t][:, :].rearrange("p (h s) -> p h s", h=HG_H)))
                mark_free[pair] = [m]

            done = products(K2, Q2, 0, [s_dve.now()])
            pending = (7, 0, done)
            pair = 1
            for lv, n in enumerate(LEVELS[1:], 1):
                E2 = (EX, TM)[lv % 2]
                QK = (QKa, QKb)[lv % 2]
                b2, e2, x2 = blk(BC, 2 * n), blk(E2, 2 * n), blk(QK, 2 * n)
                q2, k2 = blk(Q2, 2 * n), blk(K2, 2 * n)
                shape = [P, 2 * S // (2 * n), n]
                anchor = b2[:, :, n - 1:n].broadcast_to(shape)
                wait(dve, s_act.now(), s_dve.now(), s_pe.now(0))
                V_(dve.tensor_tensor(e2[:, :, 0:n], anchor, b2[:, :, 0:n], ALU.subtract))
                m = V_(dve.tensor_tensor(e2[:, :, n:2 * n], b2[:, :, n:2 * n], anchor, ALU.subtract))
                wait(act, m)
                m = A_(act.activation(E2[:, :, :], E2[:, :, :], ACT.Exp))
                select(*pending)
                wait(dve, m)
                V_(dve.tensor_tensor(x2[:, :, 0:n], k2[:, :, 0:n], e2[:, :, 0:n], ALU.mult))
                m = V_(dve.tensor_tensor(x2[:, :, n:2 * n], q2[:, :, n:2 * n], e2[:, :, n:2 * n], ALU.mult))
                pending = (lv, pair, products(QK, QK, pair, [m]))
                pair ^= 1
            bc = blk(BC, 64)
            wait(dve, s_dve.now(), s_pe.now())
            m = V_(dve.tensor_tensor(blk(TN, 64), bc[:, :, 63:64].broadcast_to([P, 8, 64]), bc, ALU.subtract))
            wait(act, m, s_pe.now())
            A_(act.activation(EX[:, :, :], BC[:, :, :], ACT.Exp))
            m = A_(act.activation(TM[:, :, :], TN[:, :, :], ACT.Exp))
            select(*pending)
            wait(dve, m)
            V_(dve.tensor_tensor(K1[:, :, :], K2[:, :, :], TM[:, :, :], ALU.mult))
            m = V_(dve.tensor_tensor(Q1[:, :, :], Q2[:, :, :], EX[:, :, :], ALU.mult))
            done = products(K1, Q1, pair, [m])
            select(0, pair, done)
            pair ^= 1
            wait(dve, done)
            for k in range(2):
                V_(dve.tensor_scalar(K1[:, k, 0:64], K1[:, k, 0:64], EX[:, k, 127:128], None, ALU.mult))
                m = V_(dve.tensor_scalar(Q1[:, k, 192:256], Q1[:, k, 192:256], EX[:, k, 191:192], None, ALU.mult))
            done = products(K1, Q1, pair, [m], cross=True)
            wait(act, done)
            for odd in range(2):
                hx = A_(act.activation(HX[:, 2 * odd:2 * odd + 2, :],
                                       bank[2 * pair + odd][:, 0:S].rearrange("p (h s) -> p h s", h=2), ACT.Copy))
            wait(pe, hx, s_dve.now())
            for t in range(T):
                for h in range(HG_H):
                    d = bank[4 + t][:, h * HD:(h + 1) * HD]
                    v = lambda tt: UM[:, tt, o_hv + h * HD:o_hv + (h + 1) * HD]
                    last = pe.matmul(d, HA[:, h % 2, 2 * t + h // 2, :], v(t), start=True, stop=(t == 0))
                    if t == 1:
                        last = pe.matmul(d, HX[:, 2 * (h % 2) + h // 2, :], v(0), start=False, stop=True)
            m = M_(last)
            wait(act, m)
            gs = A_(act.activation(GS[:, :, :], UM[:, :, o_hg:o_hg + HALF], ACT.Silu))
            wait(dve, m, gs)
            for t in range(T):
                m = V_(dve.tensor_copy(K1[:, t, :], bank[4 + t][:, 0:HALF]))
            wait(dve, m)
            m = V_(dve.tensor_tensor(Q1[:, :, :], K1[:, :, :], K1[:, :, :], ALU.mult))
            wait(dve, m)
            m = V_(dve.tensor_reduce(ST[:, 0:8], Q1[:, :, :].rearrange("p t (h d) -> p (t h) d", h=HG_H), AX.X, ALU.add))
            r = rstd(ST[:, 0:8], HD, m)
            wait(dve, r)
            heads = K1[:, :, :].rearrange("p t (h d) -> p (t h) d", h=HG_H)
            m = V_(dve.tensor_tensor(heads, heads, ST[:, 0:8].unsqueeze(2).broadcast_to([P, 8, HD]), ALU.mult))
            wait(dve, m)
            m = V_(dve.tensor_tensor(heads, heads, OG[:, :].unsqueeze(1).broadcast_to([P, 8, HD]), ALU.mult))
            wait(dve, m)
            return V_(dve.tensor_tensor(YR[:, :, 0:HALF], K1[:, :, :], GS[:, :, :], ALU.mult))

        def rstd(st, n, mark):
            wait(dve, mark)
            m = V_(dve.tensor_scalar(st, st, 1.0 / n, EPS, ALU.mult, ALU.add))
            wait(act, m)
            m = A_(act.activation(st, st, ACT.Sqrt))
            wait(dve, m)
            return V_(dve.reciprocal(st, st))

        def fox(l, rows):
            wait(dve, *rows)
            V_(dve.tensor_scalar(FZ[:, 1, :, :], FZ[:, 0, :, :], 0.0, None, ALU.min))
            m = V_(dve.scalar_tensor_tensor(out=FZ[:, 2, :, :], in0=FZ[:, 0, :, :], scalar=-1.0,
                                            in1=FZ[:, 0, :, :], op0=ALU.mult, op1=ALU.max))
            wait(act, m)
            m = A_(act.activation(FZ[:, 3, :, :], FZ[:, 2, :, :], ACT.Exp, scale=-1.0))
            wait(dve, m)
            m = V_(dve.tensor_scalar(FZ[:, 2, :, :], FZ[:, 3, :, :], 1.0, None, ALU.add))
            wait(act, m)
            m = A_(act.activation(FZ[:, 3, :, :], FZ[:, 2, :, :], ACT.Ln))
            wait(dve, m)
            m = V_(dve.tensor_tensor(FZ[:, 0, :, :], FZ[:, 1, :, :], FZ[:, 3, :, :], ALU.subtract))
            wait(pe, m, c2_mark, s_act.now(), s_dve.now())
            pe.matmul(bank[0][:, 0:FOX_H], TRI[:, 0, :], FZ[:, 0, 0, :], start=True, stop=True)
            pe.matmul(bank[0][:, FOX_H:2 * FOX_H], TRI[:, 1, :], FZ[:, 0, 0, :], start=True, stop=False)
            pe.matmul(bank[0][:, FOX_H:2 * FOX_H], TRI[:, 0, :], FZ[:, 0, 1, :], start=False, stop=True)
            pe.matmul(bank[1][0:FOX_H, 0:P], FZ[:, 0, 0, :], TRI[:, 0, :], start=True, stop=True)
            pe.matmul(bank[1][0:FOX_H, P:S], FZ[:, 0, 0, :], TRI[:, 1, :], start=True, stop=False)
            last = pe.matmul(bank[1][0:FOX_H, P:S], FZ[:, 0, 1, :], TRI[:, 0, :], start=False, stop=True)
            m = M_(last)
            wait(dve, m)
            V_(dve.tensor_copy(CC[:, :, :], bank[0][:, 0:2 * FOX_H].rearrange("p (t h) -> p t h", t=T)))
            V_(dve.tensor_scalar(NCT[:, :], bank[1][0:FOX_H, 0:S], -1.0, None, ALU.mult))
            sq = QKT[:, :, :].rearrange("p a b -> p (a b)").rearrange("p (t n) -> p t n", t=T)
            qk = UM[:, :, o_fq:o_fv]
            m = V_(dve.tensor_tensor(sq, qk, qk, ALU.mult))
            wait(dve, m)
            st = FST[:, 0, :, :]
            m = V_(dve.tensor_reduce(st, sq.rearrange("p t (h d) -> p t h d", d=HD), AX.X, ALU.add))
            r = rstd(st, HD, m)
            wait(dve, r)
            for t in range(T):
                v = qk[:, t, :].rearrange("p (h d) -> p h d", d=HD)
                m = V_(dve.tensor_tensor(v, v, FST[:, 0, t, :].unsqueeze(2).broadcast_to([P, 16, HD]), ALU.mult))
            wait(pe, m)
            for kp in range(0, NQK, 2):
                b = bank[4 + kp // 2]
                for k in (kp, kp + 1):
                    for t in range(T):
                        last = pe.transpose(b[:, (k - kp) * S + t * P:(k - kp) * S + (t + 1) * P],
                                            qk[:, t, k * P:(k + 1) * P], IDENT[:, :])
                m = M_(last)
                wait(dve, m)
                g = COLS[:, vec[f"foxq{l}"]:vec[f"foxq{l}"] + 1] if kp < 4 else COLS[:, vec[f"foxk{l}"]:vec[f"foxk{l}"] + 1]
                V_(dve.tensor_scalar(QKT[:, kp:kp + 2, :], b[:, :].rearrange("p (k s) -> p k s", k=2), g,
                                     HD ** -0.5 if kp < 4 else 1.0, ALU.mult, ALU.mult))
            units = [(h, t) for h in range(FOX_H) for t in range(T)]
            mk = {}
            wait(pe, s_dve.now(), s_act.now())
            wait(dve, s_dve.now())

            def scores(u):
                h, t = units[u]
                j, n = u % 2, (units[u][1] + 1) * P
                if u >= 2:
                    wait(pe, mk["s", u - 2])
                r_ = slice((h % 2) * HD, (h % 2 + 1) * HD)
                b = bank[j]
                pe.matmul(b[:, 0:n], QKT[r_, h // 2, t * P:(t + 1) * P], QKT[r_, 4 + h // 2, 0:n], start=True, stop=False)
                last = pe.matmul(b[:, 0:n], IDENT[0:FOX_H, h:h + 1].broadcast_to([FOX_H, P]), NCT[:, 0:n],
                                 start=False, stop=True)
                mk["q", u] = M_(last)

            def softmax(u):
                h, t = units[u]
                j, n = u % 2, (units[u][1] + 1) * P
                s_ = ST[:, 32 + 8 * j:40 + 8 * j]
                wait(dve, mk["q", u], mk.get(("e", u - 2)))
                mb = MB[:, :, :].rearrange("p a b -> p (a b)")[:, S - n:S]
                mk["s", u] = m = V_(dve.scalar_tensor_tensor(out=FS[j][:, 0:n], in0=bank[j][:, 0:n],
                                                             scalar=CC[:, t, h:h + 1], in1=mb,
                                                             op0=ALU.add, op1=ALU.add))
                wait(dve, m)
                m = V_(dve.tensor_reduce(s_[:, 0:1], FS[j][:, 0:n], AX.X, ALU.max, negate=True))
                wait(act, m, mk.get(("t", u - 2)))
                mk["e", u] = A_(act.activation(FP[j][:, 0:n], FS[j][:, 0:n], ACT.Exp, bias=s_[:, 0:1],
                                               accum_out=s_[:, 1:2]))

            def turn(u):
                h, t = units[u]
                j = u % 2
                wait(pe, mk["e", u], mk.get(("c", u - 2)))
                for kt in range(t + 1):
                    last = pe.transpose(bank[2 + j][:, kt * P:(kt + 1) * P], FP[j][:, kt * P:(kt + 1) * P], IDENT[:, :])
                mk["t", u] = M_(last)
                wait(act, mk["t", u], mk.get(("p", u - 2)))
                mk["c", u] = A_(act.activation(FT[j][:, 0:t + 1, :],
                                               bank[2 + j][:, 0:(t + 1) * P].rearrange("p (k q) -> p k q", q=P), ACT.Copy))

            def values(u):
                h, t = units[u]
                j = u % 2
                s_ = ST[:, 32 + 8 * j:40 + 8 * j]
                wait(pe, mk["c", u], mk.get(("o", u - 2)))
                for kt in range(t + 1):
                    last = pe.matmul(bank[4 + j][:, 0:HD], FT[j][:, kt, :], UM[:, kt, o_fv + h * HD:o_fv + (h + 1) * HD],
                                     start=(kt == 0), stop=(kt == t))
                mk["p", u] = M_(last)
                wait(dve, mk["e", u], mk["p", u])
                m = V_(dve.reciprocal(s_[:, 2:3], s_[:, 1:2]))
                wait(dve, m)
                mk["o", u] = V_(dve.tensor_scalar(YR[:, t, HALF + h * HD:HALF + (h + 1) * HD], bank[4 + j][:, 0:HD],
                                                  s_[:, 2:3], None, ALU.mult))

            scores(0)
            for u in range(len(units)):
                if u + 1 < len(units):
                    scores(u + 1)
                softmax(u)
                if u >= 1:
                    values(u - 1)
                turn(u)
            values(len(units) - 1)
            return s_dve.now()

        for l in range(2):
            ffn2("ffn1_w_in_2", "ffn1_w_out_2", l, col(f"ffn1_{l}"))
            rows_ = mix_in(l)
            cm = conv3(l, rows_)
            hm = hgrn(l, rows_)
            fm = fox(l, rows_)
            ym = to_columns(YR, [hm, fm], None, None, XTh, XTl, [*pe_idle(), s_act.now(), s_dve.now()], kn=6, k0=2)
            wait(act, cm)
            h_ = A_(act.activation(XTh[:, 0:2, :], CBT[:, :, :], ACT.Copy))
            wait(dve, h_)
            l_ = V_(dve.tensor_tensor(XTl[:, 0:2, :], CBT[:, :, :], XTh[:, 0:2, :].bitcast(F32), ALU.subtract))
            down(4, XTh, XTl, [*ym, h_, l_, *acc_free()])
            add_residual()
            ffn2("ffn2_w_in_2", "ffn2_w_out_2", l, col(f"ffn2_{l}"))

        def finish_out():
            wait(sp, x_mark[0])
            s_out = signal("s_out", 16)
            s_out.on(sp.dma_start(out[0, :, :].rearrange("(t p) d -> p t d", p=P), X[:, :, :]))
            wait(sp, s_out.now())
        finish_out()


def constants():
    c = {"ident": np.eye(P, dtype=np.float32)}
    comb = np.zeros((5, 2), np.float32)
    comb[[0, 2, 4], 0] = 1
    comb[[1, 3, 4], 1] = 1
    c["comb"] = comb
    c["combb"] = np.repeat(comb[:, :1], P, axis=1).copy()
    n = np.arange(S)
    ang = 2 * np.pi * (np.outer(n, n) % S) / S
    dft = np.concatenate([np.cos(ang), np.sin(ang)], axis=1).astype(np.float32)
    c["dft"] = dft.reshape(T, P, 2 * S).transpose(1, 0, 2).copy()
    m = np.arange(HD)
    ang = 2 * np.pi * (np.outer(m, m) % HD) / HD
    scale = 1.0 / np.sqrt(S * HD)
    ccm = np.zeros((P, 2, P), np.float32)
    for g in range(2):
        ccm[g * HD:(g + 1) * HD, 0, g * HD:(g + 1) * HD] = np.cos(ang) * scale
        ccm[g * HD:(g + 1) * HD, 1, g * HD:(g + 1) * HD] = -np.sin(ang) * scale
    c["ccm"] = ccm
    s, t = np.arange(P)[:, None], np.arange(P)[None, :]
    c["tri"] = np.stack([(s <= t), np.ones((P, P))], axis=1).astype(np.float32)
    c["causal"] = np.stack([np.zeros((P, P)), np.where(t <= s, 0.0, -1e30)], axis=1).astype(np.float32)
    masks = [(s // n + 1 == t // n) & (s // n % 2 == 0) for n in LEVELS] + [s == t]
    c["masks"] = np.stack(masks, axis=1).astype(np.float32)
    rows = S // GRID_W
    row = np.repeat(np.arange(rows, dtype=np.float32), GRID_W)
    colm = np.tile(np.arange(GRID_W, dtype=np.float32), rows)
    half = HD // 2
    inv = (ROPE_THETA ** (-np.arange(0, half, 2, dtype=np.float32) / half)).astype(np.float32)
    a = np.concatenate([row[:, None] * inv, colm[:, None] * inv], axis=-1)
    r = np.stack([np.cos(a), np.sin(a)], axis=1).astype(np.float32)
    c["rope"] = r.reshape(T, P, 2, half).transpose(1, 0, 2, 3).copy()
    return c


_INS = ['x', 'c', 'ctx', 'c_ctx', 'ada_w', 'ada_b', 'mix_norm_g', 'ffn_norm_g', 'ffn_w1', 'ffn_w3', 'ffn_w2',
        'ev_w_in', 'ev_lambda_q1', 'ev_lambda_k1', 'ev_lambda_q2', 'ev_lambda_k2', 'ev_subln_g', 'ev_fourier_w',
        'ev_w_out', 'od_pw1_w', 'od_pw1_b', 'od_dw_w', 'od_dw_b', 'od_ln_g', 'od_ln_b', 'od_pw2_w', 'od_pw2_b',
        'final_g', 'ffn1_norm_2', 'ffn1_w_in_2', 'ffn1_w_out_2', 'mix_norm_2', 'w_mix_in_2', 'conv_w_2',
        'hgrn_lb_logits_2', 'hgrn_out_gain_2', 'fox_q_gain_2', 'fox_k_gain_2', 'fox_f_bias_2', 'w_mix_out_2',
        'ffn2_norm_2', 'ffn2_w_in_2', 'ffn2_w_out_2']


def kernel(**inputs):
    import concourse.bacc as _bacc
    from concourse.bass_utils import run_bass_kernel_spmd as _run

    nc = _bacc.Bacc("TRN2", target_bir_lowering=False, num_devices=1)
    arrays, aps = {}, {}
    for name in _INS:
        a = np.ascontiguousarray(inputs[name])
        arrays[f"in_{name}"] = a
        aps[name] = nc.dram_tensor(f"in_{name}", a.shape, mybir.dt.from_np(a.dtype), kind="ExternalInput").ap()
    for name, a in constants().items():
        arrays[f"const_{name}"] = a
        aps[name] = nc.dram_tensor(f"const_{name}", a.shape, mybir.dt.from_np(a.dtype), kind="ExternalInput").ap()
    out = nc.dram_tensor("out_0", (1, S, D), F32, kind="ExternalOutput").ap()
    program(nc, aps, out)
    r = _run(nc, [arrays], core_ids=[0])
    return r.results[0]["out_0"]
```

```python
from contextlib import ExitStack, contextmanager

import numpy as np

import concourse.bass as bass
from concourse import mybir

F32 = mybir.dt.float32
F32R = mybir.dt.float32r
U8 = mybir.dt.uint8
ALU = mybir.AluOpType
ACT = mybir.ActivationFunctionType
AX = mybir.AxisListType

P = 128
D = 1024
KD = D // P
T = 2
S = T * P
FF = 2816
KF = FF // P
HALF = 256
CH = 2 * HALF
SLAB = 2048
RING = 4
EPS = 1e-6
GRID_W, ROPE_THETA, HD = 64, 10000.0, 64
DW, FW = 768, 256
VD = 128
HEADS1 = DW // VD
LAMBDA_INIT = 0.8 - 0.6
TAPS = 31
FOX_H, HG_H = 8, 4
MIX_IN = 3336
LEVELS = (64, 32, 16, 8, 4, 2, 1)


class Signal:

    def __init__(self, sem, step=1):
        self.sem, self.step, self.n, self.term, self.per = sem, step, 0, None, 0

    def on(self, ins):
        ins.then_inc(self.sem, self.step)
        self.n += self.step
        return self.now()

    def now(self, back=0):
        return (self, self.n - back * self.step, self.term)


def wait(eng, *marks):
    for m in marks:
        if m is None:
            continue
        sig, n, term = m
        if term is None:
            if n > 0:
                eng.wait_ge(sig.sem, n)
        else:
            eng.wait_ge(sig.sem, term + n)


@contextmanager
def repeat(loop, turns, per):
    with loop(0, turns) as i:
        starts = {}
        for sig, k in per.items():
            starts[sig] = sig.n
            sig.term = i * (k * sig.step)
        yield i
        for sig, k in per.items():
            assert sig.n - starts[sig] == k * sig.step, (sig.sem, sig.n - starts[sig], k)
    for sig, k in per.items():
        sig.n = starts[sig] + k * sig.step * turns
        sig.term = None


def program(nc, A, out, stop=99):
    sem_count = [0]
    ctx = ExitStack()
    with ctx:
        def signal(name, step=1):
            sem_count[0] += 1
            return Signal(ctx.enter_context(nc.semaphore(name)), step)

        used_bytes = [-(-nc.sbuf_base // 32) * 32]

        def at(name, shape, offset, dt=F32):
            return nc.alloc_sbuf_tensor_at(name, list(shape), dt, offset=offset)

        def place(name, shape, dt=F32, bytes_=4):
            size = bytes_ * int(np.prod(shape[1:]))
            o = used_bytes[0]
            used_bytes[0] += -(-size // 32) * 32
            return at(name, shape, o, dt)

        raw = [place(f"raw{r}", [P, SLAB]) for r in range(RING)]
        hi = [place(f"hi{r}", [P, SLAB], F32R) for r in range(RING)]
        lo = [place(f"lo{r}", [P, SLAB], F32R) for r in range(RING)]
        X = place("X", [P, T, D])
        XTh = place("XTh", [P, KD, S], F32R)
        XTl = place("XTl", [P, KD, S], F32R)
        tmp_at = used_bytes[0]
        XN = place("XN", [P, T, D])
        FULL = place("FULL", [P, KD, S])
        ht_at = used_bytes[0]
        HTh = place("HTh", [P, KF, S], F32R)
        HTl = place("HTl", [P, KF, S], F32R)
        ht_end = used_bytes[0]
        gate_at = used_bytes[0]
        GATE = place("GATE", [P, 4, D])
        IDENT = place("IDENT", [P, P])
        n_cols = A["cols"].shape[1]
        COLS = place("COLS", [P, n_cols])
        CT = place("CT", [P, KD, 4], F32R)
        CS = place("CS", [P, 2, KD])
        MODS = place("MODS", [P, 2, 4, KD])
        MODC = place("MODC", [P, 2, KD])
        cst_at = used_bytes[0]
        used_bytes[0] += 5120
        total_slabs = 62 + 33 + 12 + 33 + 2 * (33 + 17 + 33)
        place2 = place
        row_at = used_bytes[0]
        SG = place("SG", [P, T, HALF])
        HID = place("HID", [P, T, HALF])
        ST = place("ST", [P, 64])

        bank = [ctx.enter_context(nc.psum_tensor(f"bank{b}", [P, 512], F32)) for b in range(8)]

        pe, act, dve, pool, sp = nc.tensor, nc.scalar, nc.vector, nc.gpsimd, nc.sync

        landed = [signal(f"landed{r}", 16) for r in range(RING)]
        hi_done = signal("hi_done")
        lo_done = signal("lo_done")
        consumed = signal("consumed")
        s_pe, s_act, s_dve, s_pool = signal("s_pe"), signal("s_act"), signal("s_dve"), signal("s_pool")
        s_in = signal("s_in", 16)
        s_cols, s_bias, s_rope = signal("s_cols", 16), signal("s_bias", 16), signal("s_rope", 16)
        s_x, s_cx = signal("s_x", 16), signal("s_cx", 16)
        s_out = signal("s_out", 16)
        silu_done = signal("silu_done")
        hid_done = signal("hid_done")
        turned = signal("turned")
        hth_done = signal("hth_done")
        htl_done = signal("htl_done")
        out_act = signal("out_act")
        out_dve = signal("out_dve")

        g_load = [0]
        g_split = [0]
        g_use = [0]

        def val(sig, n, i, scale=1):
            return (sig, n, None if i is None else i * (4 * scale))

        def load_slab(parts, i=None):
            g = g_load[0]
            r = g % RING
            if g >= RING:
                wait(sp, val(hi_done, g - RING + 1, i), val(lo_done, g - RING + 1, i))
            for dst, src in parts(raw[r]):
                landed[r].on(sp.dma_start(dst, src))
            g_load[0] += 1

        def load_slabs(n, parts):
            first = n if g_load[0] == 0 or n < 8 else n % 4
            if first < n and g_load[0] < RING:
                first += 4
            for s in range(first):
                load_slab(parts(s, 0))
            turns = (n - first) // 4
            if turns == 1:
                for s in range(first, n):
                    load_slab(parts(s, 0))
            elif turns:
                g0 = g_load[0]
                with repeat(sp.Fori, turns, {x: 2 for x in landed}) as i:
                    for s in range(first, first + 4):
                        load_slab(parts(s, i), i)
                g_load[0] = g0 + 4 * turns

        lo_engine = [dve]

        def split_next(i=None, eng=None):
            eng = dve if eng is None else eng
            g = g_split[0]
            if g >= total_slabs:
                return
            r = g % RING
            here = (landed[r], 32 * (g // RING + 1), None if i is None else i * 32)
            free = val(consumed, g - RING + 1, i)
            wait(act, here, free)
            hi_done.on(act.activation(hi[r][:, :], raw[r][:, :], ACT.Copy))
            wait(eng, here, free, val(hi_done, g + 1, i), val(lo_done, g, i) if eng is not lo_engine[0] else None)
            lo_engine[0] = eng
            lo_done.on(eng.tensor_tensor(lo[r][:, :], raw[r][:, :], hi[r][:, :].bitcast(F32), ALU.subtract))
            g_split[0] += 1

        def slab_ready(i=None):
            g = g_use[0]
            wait(pe, val(hi_done, g + 1, i), val(lo_done, g + 1, i))
            return g % RING

        def ready_ahead(j):
            g = g_use[0] + j
            wait(pe, val(hi_done, g + 1, None), val(lo_done, g + 1, None))
            return g % RING

        def slab_used(ins, i=None):
            consumed.on(ins)
            g_use[0] += 1

        def three(dst, xh, xl, wh, wl, start, stop):
            pe.matmul(dst, xh, wh, start=start, stop=False)
            pe.matmul(dst, xh, wl, start=False, stop=False)
            return pe.matmul(dst, xl, wh, start=False, stop=stop)

        def chunk_slab(half, banks, stats, i=None):
            r = slab_ready(i)
            for k in range(4):
                kk = 4 * half + k
                wh, wl = hi[r][:, k * CH:(k + 1) * CH], lo[r][:, k * CH:(k + 1) * CH]
                for b, (xh, xl) in zip(banks, stats):
                    last = three(b[:, :], xh(kk), xl(kk), wh, wl, kk == 0, kk == KD - 1)
            slab_used(last, i)

        def tiles(h, l, k0=0):
            return [((lambda k, t=t: h[:, k0 + k, t * P:(t + 1) * P]),
                     (lambda k, t=t: l[:, k0 + k, t * P:(t + 1) * P])) for t in range(T)]

        def slab_mark(i=None):
            return val(consumed, g_use[0], i)

        def row_tiles(w):
            return w.rearrange("(k p) n -> p k n", p=P)

        def up_parts(wa, ca, wb, cb, width=HALF):
            va, vb = row_tiles(wa), row_tiles(wb)

            def parts(s, i):
                c, half = s // 2, s % 2
                off = c * width if i is None or isinstance(i, int) and i == 0 else i * (2 * width) + c * width

                def into(slot):
                    v = slot[:, :].rearrange("p (k n) -> p k n", k=4)
                    ks = slice(4 * half, 4 * half + 4)
                    return [(v[:, :, 0:HALF], va[:, ks, bass.ds(off + ca, HALF)]),
                            (v[:, :, HALF:CH], vb[:, ks, bass.ds(off + cb, HALF)])]
                return into
            return parts

        def down_parts(w):
            v = row_tiles(w)

            def parts(s, i):
                def into(slot):
                    d = slot[:, :].rearrange("p (k n) -> p k n", k=2)
                    res = []
                    for k in range(2):
                        kk = 2 * s + k if i is None or isinstance(i, int) else i * 8 + (2 * s + k)
                        res.append((d[:, k, :], w[bass.ds(kk * P, P), :]))
                    return res
                return into
            return parts

        def A_(ins):
            return s_act.on(ins)

        def V_(ins):
            return s_dve.on(ins)

        def M_(ins):
            return s_pe.on(ins)

        def G_(ins):
            return s_pool.on(ins)

        acc = [[bank[4 + 2 * t + n] for n in range(2)] for t in range(T)]

        def down(nslab, xh, xl, first_mark, residual, follow, late=None):
            def products(r, s, t):
                for kk in (2 * s, 2 * s + 1):
                    sh, sl = xh[:, kk, t * P:(t + 1) * P], xl[:, kk, t * P:(t + 1) * P]
                    o = (kk - 2 * s) * D
                    w = [(hi[r][:, o + n * 512:o + n * 512 + 512], lo[r][:, o + n * 512:o + n * 512 + 512])
                         for n in range(2)]
                    for n in range(2):
                        pe.matmul(acc[t][n][:, :], sh, w[n][0], start=kk == 0, stop=False)
                        pe.matmul(acc[t][n][:, :], sh, w[n][1], start=False, stop=False)
                    for n in range(2):
                        last = pe.matmul(acc[t][n][:, :], sl, w[n][0], start=False, stop=kk == 2 * nslab - 1)
                return last

            wait(pe, *first_mark)
            follow.open()
            for s in range(nslab - 3):
                r = slab_ready()
                for t in range(T):
                    last = products(r, s, t)
                slab_used(last)
                if late is not None and s == 0:
                    late_marks = late()
                split_next()
            if late is not None:
                wait(pe, *late_marks)
            tail = [(ready_ahead(j), nslab - 3 + j) for j in range(3)]
            for r, s in tail:
                last = products(r, s, 0)
            follow.rows(0, residual(0, M_(last)))
            slab_used(products(*tail[0], 1))
            follow.turn(0)
            split_next()
            slab_used(products(*tail[1], 1))
            split_next()
            slab_used(products(*tail[2], 1))
            follow.rows(1, residual(1, slab_mark()))

        x_mark = [None, None]

        def add_residual(gate=None, half=False, bias=None):
            def residual(t, done):
                wait(dve, done, x_mark[t])
                for n in range(2):
                    cols = slice(n * 512, n * 512 + 512)
                    src = acc[t][n][:, :]
                    if gate is None:
                        m = V_(dve.scalar_tensor_tensor(out=X[:, t, cols], in0=src, scalar=0.5 if half else 1.0,
                                                        in1=X[:, t, cols], op0=ALU.mult, op1=ALU.add))
                    else:
                        if bias is not None:
                            m = V_(dve.tensor_tensor(XN[:, t, cols], src, bias[:, cols], ALU.add))
                            wait(dve, m)
                            src = XN[:, t, cols]
                        m = V_(dve.tensor_tensor(XN[:, t, cols], src, GATE[:, gate, cols], ALU.mult))
                if gate is not None:
                    wait(dve, m)
                    m = V_(dve.tensor_tensor(X[:, t, :], X[:, t, :], XN[:, t, :], ALU.add))
                x_mark[t] = m
                return m
            return residual

        class Follow:

            def __init__(self, gains, shifts=None, final=None):
                self.gains, self.shifts, self.final = gains, shifts, final
                self.marks = [None, None]

            def open(self):
                self.free = [*pe_idle(), s_act.now(), s_dve.now(), htl_done.now(), hth_done.now()]

            def rows(self, t, mark):
                self.mark = mark
                if self.final is not None:
                    m = rstd_of(X[:, t, :], t, D, 2 + t, [mark, *self.free], XN[:, t, :])
                    wait(dve, m, s_act.now())
                    x_mark[t] = self.mark = V_(dve.scalar_tensor_tensor(
                        out=X[:, t, :], in0=X[:, t, :], scalar=ST[:, 2 + t:3 + t], in1=self.final, op0=ALU.mult,
                        op1=ALU.mult))
                if self.shifts is not None:
                    m = rstd_of(X[:, t, :], t, D, t, [mark, *self.free], XN[:, t, :])
                    wait(dve, m, s_act.now())
                    self.mark = V_(dve.tensor_scalar(XN[:, t, :], X[:, t, :], ST[:, t:t + 1], None, ALU.mult))

            def turn(self, t):
                rows = X if self.shifts is None else XN
                cols = slice(t * P, (t + 1) * P)
                wait(pe, self.mark, *self.free, s_dve.now())
                ms = []
                for h in range(2):
                    b = bank[2 + 2 * t + h]
                    for k in range(4):
                        last = pe.transpose(b[:, k * P:(k + 1) * P], rows[:, t, (4 * h + k) * P:(4 * h + k + 1) * P],
                                            IDENT[:, :])
                    ms.append(M_(last))
                wait(dve, *self.free)
                fs = []
                for h in range(2):
                    b = bank[2 + 2 * t + h]
                    ks = slice(4 * h, 4 * h + 4)
                    wait(dve, ms[h])
                    if self.shifts is None:
                        m = V_(dve.tensor_tensor(FULL[:, ks, cols], b[:, :].rearrange("p (k s) -> p k s", k=4),
                                                 self.gains[:, ks].unsqueeze(2).broadcast_to([P, 4, P]), ALU.mult))
                    else:
                        for k in range(4):
                            kk = 4 * h + k
                            m = V_(dve.tensor_scalar(FULL[:, kk, cols], b[:, k * P:(k + 1) * P],
                                                     self.gains[:, kk:kk + 1], self.shifts[:, kk:kk + 1],
                                                     ALU.mult, ALU.add))
                    fs.append(m)
                wait(act, *self.free, self.mark)
                for h in range(2):
                    ks = slice(4 * h, 4 * h + 4)
                    wait(act, fs[h])
                    m = A_(act.activation(XTh[:, ks, cols], FULL[:, ks, cols], ACT.Copy))
                    wait(dve, m)
                    l = V_(dve.tensor_tensor(XTl[:, ks, cols], FULL[:, ks, cols], XTh[:, ks, cols].bitcast(F32),
                                             ALU.subtract))
                self.marks[t] = [m, l]
                if self.shifts is None:
                    rstd_of(X[:, t, :], t, D, t, [self.mark, *self.free], XN[:, t, :])

        class Last:

            def open(self):
                pass

            def turn(self, t):
                pass

            def rows(self, t, mark):
                wait(sp, mark)
                s_out.on(sp.dma_start(out[0, t * P:(t + 1) * P, :], X[:, t, :]))

        def rstd_of(src, t, n, base, mark, junk):
            wait(act, *mark)
            m = A_(act.activation(junk, src, ACT.Square, accum_out=ST[:, base:base + 1]))
            wait(dve, m)
            m = V_(dve.tensor_scalar(ST[:, base:base + 1], ST[:, base:base + 1], 1.0 / n, EPS, ALU.mult, ALU.add))
            wait(act, m)
            m = A_(act.activation(ST[:, base:base + 1], ST[:, base:base + 1], ACT.Sqrt))
            wait(dve, m)
            return V_(dve.reciprocal(ST[:, base:base + 1], ST[:, base:base + 1]))

        def to_columns(rows, rows_mark, gains, shifts, xh, xl, free, kn=KD, k0=0, banks=(4, 5, 6, 7), post=None):
            wait(pe, *rows_mark)
            marks = []
            full_mark = None
            for kp in range(0, kn, 2):
                b = bank[banks[(kp // 2) % len(banks)]]
                if kp // 2 >= len(banks):
                    wait(pe, marks[kp // 2 - len(banks)][0])
                ks = range(kp, min(kp + 2, kn))
                for k in ks:
                    for t in range(T):
                        last = pe.transpose(b[:, (k - kp) * S + t * P:(k - kp) * S + (t + 1) * P],
                                            rows[:, t, k * P:(k + 1) * P], IDENT[:, :])
                turned_m = M_(last)
                wait(dve, turned_m)
                for k in ks:
                    src = b[:, (k - kp) * S:(k - kp + 1) * S]
                    if shifts is not None:
                        m = V_(dve.tensor_scalar(FULL[:, k, :], src, gains[:, k:k + 1], shifts[:, k:k + 1],
                                                 ALU.mult, ALU.add))
                    elif gains is not None:
                        m = V_(dve.tensor_scalar(FULL[:, k, :], src, gains[:, k:k + 1], None, ALU.mult))
                    else:
                        m = V_(dve.tensor_copy(FULL[:, k, :], src))
                full_mark = m
                a, z = kp, kp + len(ks)
                if post is not None:
                    continue
                wait(act, m, *free)
                h = A_(act.activation(xh[:, k0 + a:k0 + z, :], FULL[:, a:z, :], ACT.Copy))
                wait(dve, h, *free)
                l = V_(dve.tensor_tensor(xl[:, k0 + a:k0 + z, :], FULL[:, a:z, :],
                                         xh[:, k0 + a:k0 + z, :].bitcast(F32), ALU.subtract))
                marks.append((full_mark, h, l))
            return [marks[-1][1], marks[-1][2]] if marks else [full_mark]

        def norm_columns(gains, shifts, xh=None, xl=None, src=None, mark=None):
            xh, xl, src = XTh if xh is None else xh, XTl if xl is None else xl, X if src is None else src
            rm = []
            for t in range(T):
                m = rstd_of(src[:, t, :], t, D, t, [mark, *pe_idle()], XN[:, t, :])
                wait(dve, m, s_act.now())
                rm.append(V_(dve.tensor_scalar(XN[:, t, :], src[:, t, :], ST[:, t:t + 1], None, ALU.mult)))
            return to_columns(XN, rm, gains, shifts, xh, xl, pe_idle())

        def pe_idle():
            return [slab_mark() if g_use[0] else None, s_pe.now()]

        def ffn_step(c, pair, i, follow):
            banks = [bank[2 * pair + t] for t in range(T)]
            first = i is None
            if first:
                first_chunk(banks, follow)
            else:
                wait(pe, hid_done.now(2))
                chunk_slab(0, banks, tiles(XTh, XTl), i)
                split_next(i)
                turn_chunk(i, c - 1)
                chunk_slab(1, banks, tiles(XTh, XTl), i)
            wait(act, slab_mark(i))
            for t in range(T):
                plain = follow.shifts is None
                silu_done.on(act.activation(SG[:, t, :], banks[t][:, 0:HALF], ACT.Silu,
                                            scale=ST[:, t:t + 1] if plain else 1.0))
                wait(dve, silu_done.now())
                if plain:
                    m = dve.scalar_tensor_tensor(out=HID[:, t, :], in0=banks[t][:, HALF:CH], scalar=ST[:, t:t + 1],
                                                 in1=SG[:, t, :], op0=ALU.mult, op1=ALU.mult)
                else:
                    m = dve.tensor_tensor(HID[:, t, :], SG[:, t, :], banks[t][:, HALF:CH], ALU.mult)
                hid_done.on(m)
            split_next(i)

        def first_chunk(banks, follow):
            def products(r, half, t):
                for k in range(4):
                    kk = 4 * half + k
                    xh, xl = XTh[:, kk, t * P:(t + 1) * P], XTl[:, kk, t * P:(t + 1) * P]
                    last = three(banks[t][:, :], xh, xl, hi[r][:, k * CH:(k + 1) * CH], lo[r][:, k * CH:(k + 1) * CH],
                                 kk == 0, kk == KD - 1)
                return last
            rs = [ready_ahead(0), ready_ahead(1)]
            wait(pe, *follow.marks[0])
            products(rs[0], 0, 0)
            follow.turn(1)
            split_next()
            products(rs[1], 1, 0)
            wait(pe, *follow.marks[1])
            slab_used(products(rs[0], 0, 1))
            split_next()
            slab_used(products(rs[1], 1, 1))
            wait(act, s_dve.now())
            wait(dve, s_dve.now())

        def turn_chunk(i, c, b=None):
            b = bank[4] if b is None else b
            off = 2 * c if i is None else i * 4 + 2 * c
            wait(pe, hid_done.now(), htl_done.now())
            for f in range(2):
                for t in range(T):
                    last = pe.transpose(b[:, f * S + t * P:f * S + (t + 1) * P], HID[:, t, f * P:(f + 1) * P],
                                        IDENT[:, :])
            turned.on(last)
            src = b[:, :].rearrange("p (f s) -> p f s", f=2)
            wait(act, turned.now())
            hth_done.on(act.activation(HTh[:, bass.ds(off, 2), :], src, ACT.Copy))
            wait(dve, hth_done.now())
            htl_done.on(dve.tensor_tensor(HTl[:, bass.ds(off, 2), :], src,
                                          HTh[:, bass.ds(off, 2), :].bitcast(F32), ALU.subtract))

        def ffn_up(follow):
            ffn_step(0, 0, None, follow)
            g0 = (g_split[0], g_use[0])
            n = KF // 2
            assert n % 2 == 1
            turns = (n - 1) // 2
            with repeat(nc.Fori, turns, {silu_done: 4, hid_done: 4, turned: 2, hth_done: 2, htl_done: 2}) as i:
                ffn_step(1, 1, i, follow)
                ffn_step(2, 0, i, follow)
            g_split[0], g_use[0] = g0[0] + 4 * turns, g0[1] + 4 * turns
            sync_ring()

        def sync_ring():
            hi_done.n = lo_done.n = g_split[0]
            consumed.n = g_use[0]

        def ffn(follow, residual, then, during=None):
            ffn_up(follow)
            if during is not None:
                during()

            def late():
                turn_chunk(None, KF // 2 - 1, bank[2])
                return hth_done.now(), htl_done.now()
            down(KF // 2, HTh, HTl, [hth_done.now(), htl_done.now(), *acc_free()], residual, then, late)

        def acc_free():
            return [s_dve.now(), s_act.now(), htl_done.now(), hth_done.now()]

        def load_const(dst, src, sig=None):
            sig = s_in if sig is None else sig
            sig.on(act.dma_start(dst, src))
            return sig.now()

        ROW = at("ROW", [8, D], row_at)
        UROW = at("UROW", [P, T, 2560], ht_at)
        CTXh = at("CTXh", [P, KD, S], ht_at + 20480, F32R)
        CTXl = at("CTXl", [P, KD, S], ht_at + 28672, F32R)
        CX = at("CX", [P, T, D], ht_at + 36864)
        QT = at("QT", [P, HEADS1, S], ht_at + 20480)
        KT = at("KT", [P, HEADS1, 2 * S], ht_at + 26624)
        OROW = at("OROW", [P, T, DW], ht_at + 38912)
        CROW = at("CROW", [P, T, 2 * DW], tmp_at)
        scr_at = tmp_at - 16384
        COMBB = place("COMBB", [8, P])
        MSUM = place("MSUM", [P, KD, 5])
        MODC2 = place("MODC2", [P, KD])
        ONES = at("ONES", [P, P], cst_at)
        SUBG = place2("SUBG", [P, 8])
        LAM = place2("LAM", [P, 8])
        DFT = at("DFT", [P, T, 2 * S], cst_at)
        CCM = at("CCM", [P, 2, P], cst_at + 4096)

        SCRAP = place("SCRAP", [P, 32])
        scrap = iter(range(32))
        for sig, eng in ((silu_done, pool), (hth_done, pool), (out_act, pool), (out_dve, dve), (hid_done, dve), (htl_done, dve)):
            for _ in range(4):
                n_ = next(scrap)
                sig.on(eng.memset(SCRAP[:, n_:n_ + 1], 0.0))

        vec = A["vec"]

        def col(name, n=KD):
            return COLS[:, vec[name]:vec[name] + n]

        cols_mark = load_const(COLS[:, :], A["cols"], s_cols)
        load_const(COMBB[0:5, :], A["combb"])
        bias_mark = load_const(ROW[4:5, :], A["ada_b"][0:1, 0:D], s_bias)
        x_in = load_const(X[:, :, :], A["x"][0, :, :].rearrange("(t p) d -> p t d", p=P), s_x)
        x_mark[:] = [x_in] * T
        cx_in = load_const(CX[:, :, :], A["ctx"][0, :, :].rearrange("(t p) d -> p t d", p=P), s_cx)
        ident_mark = load_const(IDENT[:, :], A["ident"])

        wait(act, cols_mark)
        m = A_(act.activation(CS[:, :, :], col("c", 2 * KD).rearrange("p (c k) -> p c k", c=2), ACT.Silu))
        wait(act, m)
        c_src = CS[:, :, :].rearrange("p c k -> p k c")
        m = A_(act.activation(CT[:, :, 0:2], c_src, ACT.Copy))
        wait(dve, m)
        ct_mark = V_(dve.tensor_tensor(CT[:, :, 2:4], c_src, CT[:, :, 0:2].bitcast(F32), ALU.subtract))

        def load_ada(l, mods):
            w = A["ada_w"][l, :, mods[0] * D:(mods[-1] + 1) * D]
            load_slabs(4 * len(mods), up_parts(w, 0, w, HALF, CH))

        lo_turn = [0]

        def split_shared():
            lo_turn[0] += 1
            split_next(eng=pool if lo_turn[0] % 3 == 0 else dve)

        def ada_slabs(l, mod, b, split, bias_mark=None):
            if bias_mark is None:
                wait(act, s_pe.now())
                bias_mark = load_const(ROW[4:5, :], A["ada_b"][l:l + 1, mod * D:(mod + 1) * D], s_bias)
            last_read = [None]
            for ch in range(2):
                wait(pe, last_read[0], *ada_free)
                for half in range(2):
                    r = slab_ready()
                    for k in range(4):
                        st = CT[:, 4 * half + k, :]
                        pe.matmul(b[0:4, :], st, hi[r][:, k * CH:(k + 1) * CH], start=(half + k == 0), stop=False)
                        last = pe.matmul(b[0:4, :], st, lo[r][:, k * CH:(k + 1) * CH], start=False,
                                         stop=(half == 1 and k == 3))
                    slab_used(last)
                    if half == 1:
                        wait(act, slab_mark())
                        last_read[0] = A_(act.activation(ROW[0:4, ch * CH:(ch + 1) * CH], b[0:4, :], ACT.Copy))
                    split()
                    yield
            wait(pe, last_read[0], bias_mark, ident_mark)
            if mod in (2, 5):
                for h in range(2):
                    wait(pe, last_read[0])
                    m = M_(pe.matmul(b[:, :], COMBB[0:5, 0:P], ROW[0:5, h * 512:(h + 1) * 512], start=True, stop=True))
                    wait(act, m, *gate_free)
                    last_read[0] = A_(act.activation(GATE[:, 2 * l + (mod == 5), h * 512:(h + 1) * 512], b[:, :],
                                                     ACT.Copy))
                ada_free[:] = [last_read[0]]
                return
            n = (0, 1, None, 2, 3)[mod]
            for k in range(KD):
                last = pe.transpose(b[:, 8 * k:8 * k + 5], ROW[0:5, k * P:(k + 1) * P], IDENT[0:5, 0:5])
            v = b[:, 0:8 * KD].rearrange("p (k c) -> p k c", c=8)
            wait(dve, M_(last))
            m = V_(dve.tensor_copy(MSUM[:, :, 0:5], v[:, :, 0:5]))
            wait(dve, m)
            ada_free[:] = [m]
            V_(dve.tensor_tensor(MODS[:, l, n, :], MSUM[:, :, 0], MSUM[:, :, 2], ALU.add))
            m = V_(dve.tensor_tensor(MODC2[:, :], MSUM[:, :, 1], MSUM[:, :, 3], ALU.add))
            wait(dve, m)
            m = V_(dve.tensor_tensor(MODS[:, l, n, :], MODS[:, l, n, :], MSUM[:, :, 4], ALU.add))
            if l == 0 and n < 2:
                m = V_(dve.tensor_tensor(MODC[:, n, :], MODC2[:, :], MSUM[:, :, 4], ALU.add))
            wait(dve, m)
            if n % 2:
                g = col(f"mix{l}" if n == 1 else f"ffn{l}")
                wait(dve, m)
                m = V_(dve.scalar_tensor_tensor(out=MODS[:, l, n, :], in0=MODS[:, l, n, :], scalar=1.0,
                                                in1=g, op0=ALU.add, op1=ALU.mult))
                if l == 0 and n == 1:
                    m = V_(dve.scalar_tensor_tensor(out=MODC[:, 1, :], in0=MODC[:, 1, :], scalar=1.0,
                                                    in1=g, op0=ALU.add, op1=ALU.mult))
            mods_mark[0] = m

        ada_free, gate_free, mods_mark = [], [], [None]

        def background(jobs):
            def run():
                for g in jobs:
                    yield from g
            it = run()

            def step(n=1):
                for _ in range(n):
                    next(it, None)
            return step

        load_ada(0, [0, 1])
        w_in = A["ev_w_in"][0, :, :]
        cols5 = [(0, HALF), (512, 2304), (768, 1024), (1280, 1536), (1792, 2048)]
        for a, b2 in cols5:
            load_slabs(2, up_parts(w_in, a, w_in, b2))
        load_ada(0, [2, 3, 4, 5])
        load_ada(1, [0, 1])
        w_out1 = A["ev_w_out"][0, :, :]
        load_slabs(4, down_parts(w_out1))
        for _ in range(RING):
            split_next()
        wait(pe, ct_mark)
        ada_now = background([ada_slabs(0, 0, bank[0], split_next, bias_mark), ada_slabs(0, 1, bank[0], split_next)])
        ada_now(2)
        cn = []
        for src, dst, mark, o in ((X, XN, x_in, 0), (CX, CX, cx_in, 2)):
            for t in range(T):
                m = rstd_of(src[:, t, :], t, D, o + t, [mark, *cn[-1:]], FULL[:, 0:4, :].rearrange("p k s -> p (k s)"))
                wait(dve, m, mark, s_act.now())
                cn.append(V_(dve.tensor_scalar(dst[:, t, :], src[:, t, :], ST[:, o + t:o + t + 1], None, ALU.mult)))
            ada_now(1)
        ada_now(5)

        load_const(DFT[:, :, :], A["dft"], s_rope)
        load_const(CCM[:, :, :], A["ccm"], s_rope)
        ROPE = at("ROPE", [P, T, 2, 32], ht_at + 44032)
        SS = place("SS", [P, T, 8])
        assert used_bytes[0] <= nc.sbuf_usable_end, used_bytes[0]
        wait(pe, ident_mark)
        xm = to_columns(XN, [cn[1], mods_mark[0]], MODS[:, 0, 1, :], MODS[:, 0, 0, :], XTh, XTl, [mods_mark[0]])
        wait(pe, *xm)
        stats = tiles(XTh, XTl)
        stats_c = tiles(CTXh, CTXl)
        reads = {}
        for c, (a, b2) in enumerate(cols5):
            both = c >= 2
            o = 4 * (c % 2)
            banks = bank[o:o + 4] if both else bank[o:o + 2]
            wait(pe, reads.get(o), reads.get(o + 1))
            chunk_slab(0, banks, stats + (stats_c if both else []))
            split_next()
            if c == 0:
                cm = to_columns(CX, [cn[3]], MODC[:, 1, :], MODC[:, 0, :], CTXh, CTXl, [s_act.now(), s_dve.now()],
                                banks=(6, 7, 2, 3))
                wait(act, s_pe.now())
                load_const(ROPE[:, :, :, :], A["rope"], s_rope)
            if c == 1:
                wait(pe, *cm)
            chunk_slab(1, banks, stats + (stats_c if both else []))
            done = slab_mark()
            wait(act, done)
            wait(dve, done)
            for j, cc in enumerate((a, b2)):
                src = slice(j * HALF, (j + 1) * HALF)
                m1 = A_(act.activation(UROW[:, 0, cc:cc + HALF], banks[0][:, src], ACT.Copy))
                m2 = V_(dve.tensor_copy(UROW[:, 1, cc:cc + HALF], banks[1][:, src]))
                if both:
                    m1 = A_(act.activation(CROW[:, 0, cc - DW:cc - DW + HALF], banks[2][:, src], ACT.Copy))
                    m2 = V_(dve.tensor_copy(CROW[:, 1, cc - DW:cc - DW + HALF], banks[3][:, src]))
            reads[o], reads[o + 1] = m1, m2
            split_next()
            wait(dve, m1, m2, s_rope.now())
            for cc in (a, b2):
                if cc >= 2 * DW:
                    continue
                rows = UROW[:, :, cc:cc + HALF].rearrange("p t (h x d) -> p t h x d", h=4, x=2)
                for t in range(T):
                    cos = ROPE[:, t, 0:1, :].broadcast_to([P, 4, 32])
                    sin = ROPE[:, t, 1:2, :].broadcast_to([P, 4, 32])
                    x1, x2 = rows[:, t, :, 0, :], rows[:, t, :, 1, :]
                    tl = [at(f"rt{cc}_{t}_{n}", [P, 4, 32], ht_at + 38912 + 2048 * t + 512 * n) for n in range(4)]
                    for dst, u, v in ((tl[0], x1, cos), (tl[1], x2, sin), (tl[2], x1, sin), (tl[3], x2, cos)):
                        m = V_(dve.tensor_tensor(dst[:, :, :], u, v, ALU.mult))
                    wait(dve, m)
                    V_(dve.tensor_tensor(x1, tl[0][:, :, :], tl[1][:, :, :], ALU.subtract))
                    q_mark = k_mark = V_(dve.tensor_tensor(x2, tl[2][:, :, :], tl[3][:, :, :], ALU.add))
                wait(dve, q_mark)
        rows_ready = (m1, m2)

        def scr(name, shape, off, dt=F32):
            return at(name, shape, scr_at + off, dt)
        ada_jobs = background([ada_slabs(0, mod, bank[7], split_shared) for mod in (2, 3, 4, 5)] +
                              [ada_slabs(1, mod, bank[7], split_shared) for mod in (0, 1)])
        ada_free[:] = [s_act.now(), s_dve.now()]
        wait(pe, *rows_ready, *pe_idle())
        wait(act, *pe_idle())
        wait(dve, *pe_idle())
        bank_read = {}
        n = 0
        for src, dst, s0, mk in ((CROW[:, :, 0:DW], KT, 0, None), (UROW[:, :, 0:DW], QT, 0, q_mark),
                                 (UROW[:, :, DW:2 * DW], KT, S, k_mark)):
            wait(pe, mk)
            for hp in range(0, HEADS1, 2):
                b = bank[n % 7]
                wait(pe, bank_read.get(n % 7))
                for h in (hp, hp + 1):
                    for t in range(T):
                        last = pe.transpose(b[:, (h - hp) * S + t * P:(h - hp) * S + (t + 1) * P],
                                            src[:, t, h * P:(h + 1) * P], IDENT[:, :])
                m = M_(last)
                out_ap = dst[:, hp:hp + 2, s0:s0 + S]
                in_ap = b[:, :].rearrange("p (h s) -> p h s", h=2)
                if n % 2:
                    wait(act, m)
                    bank_read[n % 7] = A_(act.activation(out_ap, in_ap, ACT.Copy))
                else:
                    wait(dve, m)
                    bank_read[n % 7] = V_(dve.tensor_copy(out_ap, in_ap))
                n += 1
            ada_jobs(1)
        heads_ready = [s_act.now(), s_dve.now()]

        LQ = at("LQ", [P, 4, HD], ht_at + 43008)
        wait(act, *heads_ready, s_pool.now())
        for n, name in enumerate(("ev_lambda_q1", "ev_lambda_k1", "ev_lambda_q2", "ev_lambda_k2")):
            m = load_const(LQ[:, n, :], A[name][0, :].partition_broadcast(P))
        wait(dve, m)
        for n in range(2):
            m = V_(dve.tensor_tensor(LQ[:, 2 * n, :], LQ[:, 2 * n, :], LQ[:, 2 * n + 1, :], ALU.mult))
        wait(dve, m)
        for n in range(2):
            m = V_(dve.tensor_reduce(LAM[:, n:n + 1], LQ[:, 2 * n, :], AX.X, ALU.add))
        wait(act, m)
        m = A_(act.activation(LAM[:, 2:4], LAM[:, 0:2], ACT.Exp))
        wait(dve, m)
        m = V_(dve.tensor_scalar(LAM[:, 5:6], LAM[:, 3:4], LAMBDA_INIT, None, ALU.subtract))
        wait(dve, m)
        lam_mark = V_(dve.tensor_tensor(LAM[:, 4:5], LAM[:, 2:3], LAM[:, 5:6], ALU.subtract))

        P0 = [scr(f"P0_{j}", [P, 2 * S], 2048 * j) for j in range(2)]
        P1 = [scr(f"P1_{j}", [P, 2 * S], 4096 + 2048 * j) for j in range(2)]
        AT = [scr(f"AT_{j}", [P, 4, P], 8192 + 2048 * j) for j in range(2)]
        OSQ = scr("OSQ", [P, P], 12288)
        units = [(h, t) for h in range(HEADS1) for t in range(T)]
        wait(pe, *heads_ready)
        wait(act, lam_mark)
        wait(dve, lam_mark)
        marks = {}

        def diff_scores(u):
            h, t = units[u]
            j = u % 2
            if u >= 2:
                wait(pe, marks["exp", u - 2])
            for c in range(2):
                cs = slice(c * HD, (c + 1) * HD)
                last = pe.matmul(bank[2 * j + c][:, :], QT[cs, h, t * P:(t + 1) * P], KT[cs, h, :],
                                 start=True, stop=True)
            marks["s", u] = M_(last)

        def diff_softmax(u):
            j = u % 2
            st = ST[:, 8 * j:8 * j + 8]
            wait(dve, marks["s", u])
            for c in range(2):
                m = V_(dve.tensor_reduce(st[:, c:c + 1], bank[2 * j + c][:, :], AX.X, ALU.max))
            wait(dve, m)
            m = V_(dve.tensor_scalar(st[:, 2:4], st[:, 0:2], -HD ** -0.5, None, ALU.mult))
            wait(act, m)
            if u >= 2:
                wait(act, marks["at", u - 2], marks["t", u - 2])
            for c, pb in ((0, P0[j]), (1, P1[j])):
                m = A_(act.activation(pb[:, :], bank[2 * j + c][:, :], ACT.Exp, bias=st[:, 2 + c:3 + c],
                                      scale=HD ** -0.5, accum_out=st[:, 4 + c:5 + c]))
            marks["exp", u] = m

        def diff_combine(u):
            j = u % 2
            st = ST[:, 8 * j:8 * j + 8]
            wait(dve, marks["exp", u])
            m = V_(dve.reciprocal(st[:, 6:8], st[:, 4:6]))
            wait(dve, m)
            m = V_(dve.tensor_scalar(st[:, 7:8], st[:, 7:8], LAM[:, 4:5], None, ALU.mult))
            wait(dve, m)
            m = V_(dve.tensor_scalar(P1[j][:, :], P1[j][:, :], st[:, 7:8], None, ALU.mult))
            wait(dve, m)
            marks["a", u] = V_(dve.scalar_tensor_tensor(out=P0[j][:, :], in0=P0[j][:, :], scalar=st[:, 6:7],
                                                        in1=P1[j][:, :], op0=ALU.mult, op1=ALU.subtract))

        def diff_turn(u):
            j = u % 2
            wait(pe, marks["a", u])
            if u >= 2:
                wait(pe, marks["at", u - 2])
            for kt in range(4):
                last = pe.transpose(bank[4 + j][:, kt * P:(kt + 1) * P], P0[j][:, kt * P:(kt + 1) * P], IDENT[:, :])
            marks["t", u] = M_(last)
            wait(act, marks["t", u])
            if u >= 2:
                wait(act, marks["pv", u - 2])
            marks["at", u] = A_(act.activation(AT[j][:, :, :], bank[4 + j][:, :].rearrange("p (k q) -> p k q", k=4),
                                               ACT.Copy))

        def diff_values(u):
            h, t = units[u]
            j = u % 2
            wait(pe, marks["at", u])
            if u >= 1:
                wait(pe, marks["o", u - 1])
            for kt in range(4):
                v = CROW[:, kt, DW + h * P:DW + (h + 1) * P] if kt < 2 else \
                    UROW[:, kt - 2, 2 * DW + h * P:2 * DW + (h + 1) * P]
                last = pe.matmul(bank[6][:, 0:P], AT[j][:, kt, :], v, start=(kt == 0), stop=(kt == 3))
            marks["pv", u] = M_(last)
            wait(dve, marks["pv", u])
            m = marks["o", u] = V_(dve.tensor_copy(OROW[:, t, h * P:(h + 1) * P], bank[6][:, 0:P]))
            wait(act, m, marks.get(("sq", u - 1)))
            marks["sq", u] = A_(act.activation(OSQ[:, :], OROW[:, t, h * P:(h + 1) * P], ACT.Square,
                                               accum_out=SS[:, t, h:h + 1]))

        N = len(units)
        diff_scores(0)
        diff_scores(1)
        diff_softmax(0)
        for u in range(N):
            if u + 1 < N:
                diff_softmax(u + 1)
            ada_jobs(1 if u % 2 else 2)
            diff_combine(u)
            if u + 2 < N:
                diff_scores(u + 2)
            if u >= 1:
                diff_values(u - 1)
            diff_turn(u)
        diff_values(N - 1)
        ada_jobs(24)
        o_done = [s_dve.now(), s_act.now()]

        wait(dve, *o_done)
        ss = SS[:, :, 0:HEADS1]
        m = V_(dve.tensor_scalar(ss, ss, 1.0 / VD, EPS, ALU.mult, ALU.add))
        wait(act, m)
        m = A_(act.activation(ss, ss, ACT.Sqrt))
        wait(dve, m)
        m = V_(dve.reciprocal(ss, ss))
        wait(dve, m)
        for t in range(T):
            ov = OROW[:, t, :].rearrange("p (h d) -> p h d", h=HEADS1)
            o_mark = V_(dve.tensor_tensor(ov, ov, SS[:, t, 0:HEADS1].unsqueeze(2).broadcast_to([P, HEADS1, VD]), ALU.mult))

        U1 = scr("U1", [P, 2, 2 * S], 0)
        ZT = scr("ZT", [P, 2, S], 4096)
        WB = scr("WB", [P, 2, P], 12288)
        wait(pool, *o_done, *pe_idle())
        m = G_(pool.memset(WB[:, :, :], 0.0))
        wait(act, m)
        for g in range(4):
            o = (g % 2) * HD
            wb_mark = load_const(WB[o:o + HD, g // 2, o:o + HD], A["ev_fourier_w"][0, g, :, :])
        wait(pe, *o_done, s_rope.now())
        for mt in range(2):
            for t in range(T):
                last = pe.matmul(bank[mt][:, :], UROW[:, t, 2304 + mt * P:2304 + (mt + 1) * P], DFT[:, t, :],
                                 start=(t == 0), stop=(t == T - 1))
        m = M_(last)
        wait(act, m)
        for mt in range(2):
            m = A_(act.activation(U1[:, mt, :], bank[mt][:, :], ACT.Copy))
        wait(pe, m)
        for mt in range(2):
            pe.matmul(bank[2][:, mt * S:(mt + 1) * S], CCM[:, 0, :], U1[:, mt, 0:S], start=True, stop=False)
            last = pe.matmul(bank[2][:, mt * S:(mt + 1) * S], CCM[:, 1, :], U1[:, mt, S:2 * S], start=False, stop=True)
        m = M_(last)
        wait(act, m)
        m = A_(act.activation(ZT[:, :, :], bank[2][:, :].rearrange("p (m s) -> p m s", m=2), ACT.Copy))
        wait(pe, m, wb_mark)
        for mt in range(2):
            last = pe.matmul(bank[3][:, mt * S:(mt + 1) * S], WB[:, mt, :], ZT[:, mt, :], start=True, stop=True)
        four_mark = M_(last)

        m = V_(dve.tensor_scalar(SUBG[:, 0:1], col("subln", 1), 1.0 - LAMBDA_INIT, None, ALU.mult))
        wait(dve, m)
        m = V_(dve.tensor_copy(SUBG[:, 1:7], SUBG[:, 0:1].broadcast_to([P, 6])))
        wait(dve, m)
        ym = to_columns(OROW, [o_mark], SUBG, None, XTh, XTl, [four_mark, s_dve.now()], kn=6, banks=(4, 5, 6))
        wait(dve, four_mark)
        m = V_(dve.tensor_copy(FULL[:, 6:8, :], bank[3][:, :].rearrange("p (m s) -> p m s", m=2)))
        wait(act, m)
        h = A_(act.activation(XTh[:, 6:8, :], FULL[:, 6:8, :], ACT.Copy))
        wait(dve, h)
        l = V_(dve.tensor_tensor(XTl[:, 6:8, :], FULL[:, 6:8, :], XTh[:, 6:8, :].bitcast(F32), ALU.subtract))
        def load_ffn1(l):
            load_slabs(2 * (KF // 2), up_parts(A["ffn_w1"][l, :, :], 0, A["ffn_w3"][l, :, :], 0))
            load_slabs(KF // 2, down_parts(A["ffn_w2"][l, :, :]))

        def modulated(l, n):
            return Follow(MODS[:, l, n + 1, :], MODS[:, l, n, :])

        load_ffn1(0)
        load_slabs(8, up_parts(A["od_pw1_w"][0, :, :], 0, A["od_pw1_w"][0, :, :], D))
        load_ada(1, [2, 3, 4, 5])
        load_slabs(4, down_parts(A["od_pw2_w"][0, :, :]))
        load_ffn1(1)
        up = modulated(0, 2)
        down(4, XTh, XTl, [*ym, h, l, *acc_free()], add_residual(gate=0), up)
        conv = modulated(1, 0)
        ffn(up, add_residual(gate=1), conv)

        PAD = TAPS // 2
        B1 = at("B1", [P, 2 * D], ht_at)
        UR = at("UR", [P, T, D], ht_at + 8192)
        UT = at("UT", [P, KD, 288], ht_at + 16384)
        CV = at("CV", [P, KD, S], ht_at + 25600)
        DWR = at("DWR", [32, D], ht_at + 33792)
        DWW = at("DWW", [P, KD, 32], ht_at + 37888)
        B2 = at("B2", [P, D], ht_at + 38912)
        MEAN = at("MEAN", [P, S], ht_at + 43008)
        RSTD = at("RSTD", [P, S], ht_at + 44032)
        free = [*pe_idle(), s_act.now(), s_dve.now(), htl_done.now(), hth_done.now()]
        wait(act, *free)
        wait(pool, *free)
        for h in range(2):
            load_const(B1[:, h * D:(h + 1) * D], A["od_pw1_b"][0, h * D:(h + 1) * D].partition_broadcast(P))
        load_const(B2[:, :], A["od_pw2_b"][0, :].partition_broadcast(P))
        dww_mark = load_const(DWW[:, :, 0:TAPS], A["taps"])
        conv_in = s_in.now()
        pad_mark = G_(pool.memset(UT[:, :, :], 0.0))
        ones_mark = G_(pool.memset(ONES[:, :], 1.0 / D))
        wait(pe, dww_mark)
        wait(dve, conv_in)
        wait(act, pad_mark)
        PE_TILES = 3
        ut_mark = {}

        def turn_gated(c):
            b = bank[4 + c % 2]
            wait(pe, ur_marks[c], ut_mark.get(c - 2))
            for k in (2 * c, 2 * c + 1):
                for t in range(T):
                    last = pe.transpose(b[:, (k % 2) * S + t * P:(k % 2) * S + (t + 1) * P],
                                        UR[:, t, k * P:(k + 1) * P], IDENT[:, :])
            wait(act, M_(last))
            ut_mark[c] = A_(act.activation(UT[:, 2 * c:2 * c + 2, PAD:PAD + S],
                                           b[:, :].rearrange("p (k s) -> p k s", k=2), ACT.Copy))

        def taps_on_dve():
            for k0 in range(0, KD - PE_TILES, 2):
                ks = [k for k in (k0, k0 + 1) if k < KD - PE_TILES]
                wait(dve, ut_mark[k0 // 2])
                prev = {}
                for j in range(TAPS):
                    for k in ks:
                        wait(dve, prev.get(k))
                        if j == 0:
                            m = V_(dve.tensor_scalar(CV[:, k, :], UT[:, k, 0:S], DWW[:, k, 0:1],
                                                     col("od_dw_b")[:, k:k + 1], ALU.mult, ALU.add))
                        else:
                            m = V_(dve.scalar_tensor_tensor(out=CV[:, k, :], in0=UT[:, k, j:j + S],
                                                            scalar=DWW[:, k, j:j + 1], in1=CV[:, k, :],
                                                            op0=ALU.mult, op1=ALU.add))
                        prev[k] = m
                        yield
        dve_taps = background([taps_on_dve()])
        read, ur_marks = {}, {}
        for c in range(4):
            banks = [bank[2 * (c % 2) + t] for t in range(T)]
            if c == 0:
                first_chunk(banks, conv)
            else:
                wait(pe, read.get(c - 2), s_dve.now() if c == 1 else None)
                chunk_slab(0, banks, tiles(XTh, XTl))
                split_shared()
                turn_gated(c - 1)
                chunk_slab(1, banks, tiles(XTh, XTl))
            done = slab_mark()
            wait(dve, done, s_act.now(), s_dve.now())
            cs, gs = slice(c * HALF, (c + 1) * HALF), slice(D + c * HALF, D + (c + 1) * HALF)
            for t in range(T):
                m = V_(dve.tensor_tensor(SG[:, t, :], banks[t][:, HALF:CH], B1[:, gs], ALU.add))
                V_(dve.tensor_tensor(HID[:, t, :], banks[t][:, 0:HALF], B1[:, cs], ALU.add))
                wait(act, m)
                A_(act.activation(SG[:, t, :], SG[:, t, :], ACT.Sigmoid))
            read[c] = s_dve.now()
            wait(dve, s_act.now(), s_dve.now())
            for t in range(T):
                ur_marks[c] = V_(dve.tensor_tensor(UR[:, t, cs], HID[:, t, :], SG[:, t, :], ALU.mult))
            split_shared()
            if c:
                dve_taps(10)
        turn_gated(3)
        GROUP = 16
        DIAG = [at(f"DIAG{j}", [P, GROUP, P], scr_at + 8192 * j) for j in range(2)]
        taps = [(k, j) for k in range(KD - PE_TILES, KD) for j in range(TAPS)]
        groups = [taps[o:o + GROUP] for o in range(0, len(taps), GROUP)]
        ada_conv = background([ada_slabs(1, mod, bank[7], split_shared) for mod in (2, 3, 4, 5)])
        ada_free[:] = [s_act.now(), s_dve.now()]
        used = {}
        wait(act, slab_mark(), dww_mark)
        cv_marks = []
        for g, group in enumerate(groups):
            wait(act, used.get(g - 2))
            for n, (k, j) in enumerate(group):
                m = A_(act.activation(DIAG[g % 2][:, n, :], IDENT[:, :], ACT.Identity, scale=DWW[:, k, j:j + 1]))
            ada_conv(2)
            wait(pe, m, *ut_mark.values())
            for n, (k, j) in enumerate(group):
                last = pe.matmul(bank[k % 4][:, 0:S], DIAG[g % 2][:, n, :], UT[:, k, j:j + S], start=(j == 0),
                                 stop=(j == TAPS - 1))
                if j == TAPS - 1 or n == len(group) - 1:
                    used[g] = M_(last)
                if j == TAPS - 1:
                    wait(act, used[g])
                    cv_marks.append(A_(act.activation(CV[:, k, :], bank[k % 4][:, 0:S], ACT.Identity,
                                                      bias=col("od_dw_b")[:, k:k + 1])))
            ada_conv(1)
            dve_taps(22)
        dve_taps(KD * TAPS)
        ada_conv(17)
        wait(pe, s_dve.now(), *cv_marks, ones_mark)
        wait(act, s_dve.now())
        lm = {}
        tok = [slice(t * P, (t + 1) * P) for t in range(T)]
        for t in range(T):
            for k in range(KD):
                last = pe.matmul(bank[t][:, 0:P], ONES[:, :], CV[:, k, tok[t]], start=(k == 0), stop=(k == KD - 1))
            lm[t] = M_(last)
        for t in range(T):
            wait(dve, lm[t], *cv_marks)
            m = V_(dve.tensor_copy(MEAN[:, tok[t]], bank[t][:, 0:P]))
            wait(dve, m)
            m = V_(dve.tensor_tensor(CV[:, :, tok[t]], CV[:, :, tok[t]],
                                     MEAN[:, tok[t]].unsqueeze(1).broadcast_to([P, KD, P]), ALU.subtract))
            wait(act, m)
            m = A_(act.activation(UT[:, :, tok[t]], CV[:, :, tok[t]], ACT.Square))
            wait(pe, m)
            for k in range(KD):
                last = pe.matmul(bank[2 + t][:, 0:P], ONES[:, :], UT[:, k, tok[t]], start=(k == 0), stop=(k == KD - 1))
            lm[t] = M_(last)
        for t in range(T):
            wait(dve, lm[t])
            m = V_(dve.tensor_scalar(RSTD[:, tok[t]], bank[2 + t][:, 0:P], EPS, None, ALU.add))
            wait(act, m)
            lm[t] = A_(act.activation(RSTD[:, tok[t]], RSTD[:, tok[t]], ACT.Sqrt))
        for t in range(T):
            wait(dve, lm[t])
            m = V_(dve.reciprocal(RSTD[:, tok[t]], RSTD[:, tok[t]]))
            wait(dve, m)
            m = V_(dve.tensor_tensor(CV[:, :, tok[t]], CV[:, :, tok[t]],
                                     RSTD[:, tok[t]].unsqueeze(1).broadcast_to([P, KD, P]), ALU.mult))
            wait(act, m)
            for k in range(KD):
                m = A_(act.activation(FULL[:, k, tok[t]], CV[:, k, tok[t]], ACT.Silu, scale=col("od_ln_g")[:, k:k + 1],
                                      bias=col("od_ln_b")[:, k:k + 1]))
            wait(act, m)
            h = A_(act.activation(XTh[:, :, tok[t]], FULL[:, :, tok[t]], ACT.Copy))
            wait(dve, h)
            l = V_(dve.tensor_tensor(XTl[:, :, tok[t]], FULL[:, :, tok[t]], XTh[:, :, tok[t]].bitcast(F32),
                                     ALU.subtract))
        up = modulated(1, 2)
        down(4, XTh, XTl, [h, l, *acc_free()], add_residual(gate=2, bias=B2), up)

        def load_final():
            wait(act, s_dve.now())
            wait(dve, load_const(GATE[:, 0, :], A["final_g"].partition_broadcast(P)))
        nxt = Follow(col("ffn1_0"), final=GATE[:, 0, :])
        ffn(up, add_residual(gate=3), nxt, load_final)

        UM = at("UM", [P, T, MIX_IN - FOX_H], ht_at)
        o_cx, o_cb, o_cc, o_hq, o_hf, o_hv, o_hg, o_fq, o_fk, o_fv = 0, 256, 512, 768, 1024, 1280, 1536, 1792, 2304, 2816
        NQK = 8
        QKT = at("QKT", [P, NQK, S], ht_at + 26624)
        YR = at("YR", [P, T, DW], ht_at + 34816)
        Q2, ZT2, K2, BC, EX, QKa, QKb, TM = (at(f"hg_{n}", [P, 2, S], scr_at + 2048 * n) for n in range(8))
        HA = at("HA", [P, 2, 4, P], tmp_at)
        HX = at("HX", [P, 4, P], tmp_at + 4096)
        TN = at("TN", [P, 2, S], tmp_at + 6144)
        FS = [at(f"FS{j}", [P, S], tmp_at + 8192 + 1024 * j) for j in range(2)]
        FP = [at(f"FP{j}", [P, S], tmp_at + 10240 + 1024 * j) for j in range(2)]
        FT = [at(f"FT{j}", [P, T, P], tmp_at + 12288 + 1024 * j) for j in range(2)]
        K1 = at("K1", [P, 2, S], gate_at)
        Q1 = at("Q1", [P, 2, S], gate_at + 2048)
        CU = at("CU", [P, T, HALF], gate_at + 4096)
        CUT = at("CUT", [P, 2, S + 4], gate_at + 6144)
        CBT = at("CBT", [P, 2, S], gate_at + 8256)
        FZ = at("FZ", [P, 4, T, FOX_H], gate_at + 10304)
        NCT = at("NCT", [FOX_H, S], gate_at + 10560)
        CC = at("CC", [P, T, FOX_H], gate_at + 11584)
        OG = at("OG", [P, HD], gate_at + 11648)
        FB = at("FB", [P, FOX_H], gate_at + 11904)
        GS = at("GS", [P, T, HALF], gate_at + 11968)
        WF = at("WF", [P, KD, FOX_H], gate_at + 14016)
        FST = at("FST", [P, 2, T, 16], gate_at + 14272)
        LB = at("LB", [P, 8, 2], gate_at + 14528)
        TRI = at("TRI", [P, 2, P], cst_at)
        MASKS = at("MASKS", [P, 8, P], cst_at + 1024, U8)
        MB = at("MB", [P, 2, P], cst_at + 2048)
        RESET = at("RESET", [P, 2, S], cst_at + 3072)

        set_up = {}

        def block2_constants():
            free = [*pe_idle(), s_act.now(), s_dve.now()]
            wait(act, *free)
            wait(pool, *free)
            wait(dve, *free)
            load_const(TRI[:, :, :], A["tri"])
            MASKF = at("MASKF", [P, 8, P], tmp_at)
            load_const(MASKF[:, :, :], A["masks"])
            mb_mark = load_const(MB[:, :, :], A["causal"])
            wait(dve, mb_mark)
            c2_mark = V_(dve.tensor_copy(MASKS[:, :, :], MASKF[:, :, :]))
            m = G_(pool.memset(RESET[:, :, :], 1.0))
            wait(pool, m)
            reset_mark = G_(pool.memset(RESET[:, :, :].rearrange("p k (c n) -> p k c n", n=64)[:, :, :, 0:1], 0.0))
            l0, l1 = col("lb0", 2), col("lb1", 2)
            m = V_(dve.tensor_tensor(LB[:, 0, :], l0, l1, ALU.max))
            wait(dve, m)
            V_(dve.tensor_tensor(LB[:, 1, :], l0, LB[:, 0, :], ALU.subtract))
            m = V_(dve.tensor_tensor(LB[:, 2, :], l1, LB[:, 0, :], ALU.subtract))
            wait(act, m)
            m = A_(act.activation(LB[:, 3:5, :], LB[:, 1:3, :], ACT.Exp))
            wait(dve, m)
            m = V_(dve.tensor_tensor(LB[:, 5, :], LB[:, 3, :], LB[:, 4, :], ALU.add))
            wait(dve, m)
            m = V_(dve.reciprocal(LB[:, 5, :], LB[:, 5, :]))
            wait(dve, m)
            V_(dve.tensor_tensor(LB[:, 1, :], LB[:, 3, :], LB[:, 5, :], ALU.mult))
            m = V_(dve.tensor_tensor(LB[:, 2, :], LB[:, 4, :], LB[:, 5, :], ALU.mult))
            wait(dve, m)
            m = V_(dve.tensor_tensor(LB[:, 6, :], LB[:, 1, :], LB[:, 2, :], ALU.add))
            wait(dve, m)
            V_(dve.tensor_tensor(LB[:, 0, :], LB[:, 1, :], LB[:, 1, :], ALU.subtract))
            m = V_(dve.tensor_tensor(LB[:, 7, :], LB[:, 6, :], LB[:, 1, :], ALU.subtract))
            wait(dve, m)
            for l, r0 in ((0, 0), (1, 7)):
                m = V_(dve.tensor_scalar(LB[:, 2 * l, :], LB[:, r0, :], 0.0, 1.0, ALU.max, ALU.min))
                wait(dve, m)
                m = V_(dve.tensor_scalar(LB[:, 2 * l + 1, :], LB[:, 2 * l, :], -1.0, 1.0, ALU.mult, ALU.add))
                wait(dve, m)
            lb_mark = m
            set_up.update(c2_mark=c2_mark, reset_mark=reset_mark, lb_mark=lb_mark)

        def ffn2(w_in_, w_out_, l, follow, then, during):
            w = A[w_in_][l, :, :]
            load_slabs(2 * (KF // 2), up_parts(w, 0, w, FF))
            load_slabs(KF // 2, down_parts(A[w_out_][l, :, :]))
            ffn(follow, add_residual(half=True), then, during)

        def wide_parts(w, c0):
            v = row_tiles(w)

            def into(slot):
                d = slot[:, :].rearrange("p (k n) -> p k n", k=KD)
                return [(d[:, 4 * h:4 * h + 4, :], v[:, 4 * h:4 * h + 4, c0:c0 + HALF]) for h in range(2)]
            return into

        def mix_small(l):
            if l == 0:
                block2_constants()
            free = [*pe_idle(), s_act.now(), s_dve.now()]
            wait(act, *free)
            load_const(WF[:, :, :], row_tiles(A["w_mix_in_2"][l, :, :])[:, :, MIX_IN - FOX_H:MIX_IN])
            load_const(FB[:, :], A["fox_f_bias_2"][l, :].partition_broadcast(P))
            return load_const(OG[:, :], A["hgrn_out_gain_2"][l, :].partition_broadcast(P))

        def mix_in(l, follow):
            w = A["w_mix_in_2"][l, :, :]
            load_slabs(12, up_parts(w, 0, w, HALF, CH))
            load_slab(wide_parts(w, 3072))
            load_slabs(4, down_parts(A["w_mix_out_2"][l, :, :]))

            def chunk(c, i, peel=None):
                banks = [bank[2 * (c % 2) + t] for t in range(T)]
                if peel == 0:
                    first_chunk(banks, follow)
                else:
                    wait(pe, out_act.now(1), out_dve.now(1), s_dve.now() if peel else None)
                    chunk_slab(0, banks, tiles(XTh, XTl), i)
                    split_next(i)
                    chunk_slab(1, banks, tiles(XTh, XTl), i)
                done = slab_mark(i)
                wait(act, done)
                wait(dve, done)
                off = c * CH if i is None else i * (2 * CH) + c * CH
                out_act.on(act.activation(UM[:, 0, bass.ds(off, CH)], banks[0][:, :], ACT.Identity,
                                          scale=ST[:, 0:1]))
                out_dve.on(dve.tensor_scalar(UM[:, 1, bass.ds(off, CH)], banks[1][:, :], ST[:, 1:2], None, ALU.mult))
                split_next(i)

            chunk(0, None, 0)
            wait(pe, s_in.now())
            for t in range(T):
                for k in range(KD):
                    last = pe.matmul(bank[7][:, t * FOX_H:(t + 1) * FOX_H], FULL[:, k, t * P:(t + 1) * P], WF[:, k, :],
                                     start=(k == 0), stop=(k == KD - 1))
            m = M_(last)
            wait(dve, m, s_in.now())
            for t in range(T):
                z_mark = V_(dve.scalar_tensor_tensor(out=FZ[:, 0, t, :], in0=bank[7][:, t * FOX_H:(t + 1) * FOX_H],
                                                     scalar=ST[:, t:t + 1], in1=FB[:, :], op0=ALU.mult, op1=ALU.add))
            g0 = (g_split[0], g_use[0])
            with repeat(nc.Fori, 2, {out_act: 2, out_dve: 2}) as i:
                chunk(1, i)
                chunk(2, i)
            g_split[0], g_use[0] = g0[0] + 8, g0[1] + 8
            sync_ring()
            chunk(5, None, 5)
            wait(pe, out_act.now(1), out_dve.now(1))
            r = slab_ready()
            for k in range(KD):
                wh, wl = hi[r][:, k * HALF:(k + 1) * HALF], lo[r][:, k * HALF:(k + 1) * HALF]
                for t, (xh, xl) in enumerate(tiles(XTh, XTl)):
                    last = three(bank[t][:, 0:HALF], xh(k), xl(k), wh, wl, k == 0, k == KD - 1)
            slab_used(last)
            wait(act, slab_mark())
            wait(dve, slab_mark())
            A_(act.activation(UM[:, 0, 3072:3328], bank[0][:, 0:HALF], ACT.Identity, scale=ST[:, 0:1]))
            V_(dve.tensor_scalar(UM[:, 1, 3072:3328], bank[1][:, 0:HALF], ST[:, 1:2], None, ALU.mult))
            split_next()
            return [s_act.now(), s_dve.now(), out_act.now(), out_dve.now(), z_mark]

        def conv3(l, rows):
            wait(dve, *rows)
            wait(pe, *rows)
            wait(pool, *rows)
            zero = G_(pool.memset(CUT[:, :, 0:2], 0.0))
            m = V_(dve.tensor_tensor(CU[:, :, :], UM[:, :, o_cx:o_cx + HALF], UM[:, :, o_cc:o_cc + HALF], ALU.mult))
            wait(pe, m)
            for n, src in enumerate((CU[:, :, :], UM[:, :, o_cb:o_cb + HALF])):
                for k in range(2):
                    for t in range(T):
                        last = pe.transpose(bank[2 + n][:, k * S + t * P:k * S + (t + 1) * P], src[:, t, k * P:(k + 1) * P],
                                            IDENT[:, :])
            m = M_(last)
            wait(act, m, zero)
            A_(act.activation(CUT[:, :, 2:2 + S], bank[2][:, :].rearrange("p (k s) -> p k s", k=2), ACT.Copy))
            m = A_(act.activation(CBT[:, :, :], bank[3][:, :].rearrange("p (k s) -> p k s", k=2), ACT.Copy))
            wait(dve, m)
            v0 = vec[f"conv{l}"]
            for k in range(2):
                for j in range(3):
                    w = COLS[:, v0 + 2 * j + k:v0 + 2 * j + k + 1]
                    if j == 0:
                        m = V_(dve.tensor_scalar(CU[:, k, :], CUT[:, k, 0:S], w, None, ALU.mult))
                    else:
                        m = V_(dve.scalar_tensor_tensor(out=CU[:, k, :], in0=CUT[:, k, j:j + S], scalar=w, in1=CU[:, k, :],
                                                        op0=ALU.mult, op1=ALU.add))
                    wait(dve, m)
            m = V_(dve.tensor_tensor(CBT[:, :, :], CBT[:, :, :], CU[:, :, :], ALU.mult))
            wait(act, m)
            h = A_(act.activation(XTh[:, 0:2, :], CBT[:, :, :], ACT.Copy)) if False else None
            return m

        def hgrn(l, rows):
            wait(pe, *rows)
            for n, o in enumerate((o_hq, o_hf)):
                for k in range(2):
                    for t in range(T):
                        last = pe.transpose(bank[n][:, k * S + t * P:k * S + (t + 1) * P],
                                            UM[:, t, o + k * P:o + (k + 1) * P], IDENT[:, :])
            wait(dve, M_(last), *rows)
            for n, dst in enumerate((Q2, ZT2)):
                m = V_(dve.tensor_copy(dst[:, :, :], bank[n][:, :].rearrange("p (k s) -> p k s", k=2)))
            wait(dve, m, set_up["lb_mark"])
            wait(act, m, set_up["lb_mark"])
            m = A_(act.activation(K2[:, :, :], ZT2[:, :, :], ACT.Sigmoid, scale=-1.0))
            wait(dve, m)
            for k in range(2):
                V_(dve.tensor_scalar(K2[:, k, :], K2[:, k, :], LB[:, 2 * l + 1, k:k + 1], None, ALU.mult))
            V_(dve.tensor_scalar(EX[:, :, :], ZT2[:, :, :], 0.0, None, ALU.min))
            V_(dve.scalar_tensor_tensor(out=QKa[:, :, :], in0=ZT2[:, :, :], scalar=0.5, in1=ZT2[:, :, :],
                                        op0=ALU.mult, op1=ALU.max))
            m = V_(dve.scalar_tensor_tensor(out=QKb[:, :, :], in0=ZT2[:, :, :], scalar=-1.0, in1=ZT2[:, :, :],
                                            op0=ALU.mult, op1=ALU.max))
            wait(act, m)
            A_(act.activation(TM[:, :, :], EX[:, :, :], ACT.Exp, scale=0.5))
            A_(act.activation(TN[:, :, :], QKa[:, :, :], ACT.Exp, scale=-1.0))
            m = A_(act.activation(ZT2[:, :, :], QKb[:, :, :], ACT.Exp, scale=-1.0))
            wait(dve, m)
            for k in range(2):
                m = V_(dve.scalar_tensor_tensor(out=QKa[:, k, :], in0=TN[:, k, :], scalar=LB[:, 2 * l, k:k + 1],
                                                in1=TM[:, k, :], op0=ALU.mult, op1=ALU.add))
            m = V_(dve.tensor_scalar(QKb[:, :, :], ZT2[:, :, :], 1.0, None, ALU.add))
            wait(act, m)
            A_(act.activation(TN[:, :, :], QKa[:, :, :], ACT.Ln))
            m = A_(act.activation(TM[:, :, :], QKb[:, :, :], ACT.Ln))
            wait(dve, m)
            m = V_(dve.scalar_tensor_tensor(out=TN[:, :, :], in0=EX[:, :, :], scalar=0.5, in1=TN[:, :, :],
                                            op0=ALU.mult, op1=ALU.add))
            wait(dve, m)
            m = V_(dve.tensor_tensor(TM[:, :, :], TN[:, :, :], TM[:, :, :], ALU.subtract))
            wait(dve, m, set_up["reset_mark"])
            flat = lambda x: x[:, :, :].rearrange("p k s -> p (k s)")
            m = V_(dve.tensor_tensor_scan(flat(BC), flat(RESET), flat(TM), 0.0, ALU.mult, ALU.add))
            wait(dve, m)
            blk = lambda x, n: x[:, :, :].rearrange("p k (c n) -> p (k c) n", n=n)
            mark_free = {0: [s_dve.now()], 1: [s_dve.now()]}
            zero = V_(dve.memset(HA[:, :, :, :], 0.0))

            def products(lhs, rhs, pair, ready, cross=False):
                wait(pe, *ready, *mark_free[pair])
                for h in range(HG_H):
                    for t in range(1 if cross else T):
                        rows_ = slice((h % 2) * HD, (h % 2 + 1) * HD)
                        s_at, t_at = (0, P) if cross else (t * P, t * P)
                        o = (2 * t + h // 2) * P
                        last = pe.matmul(bank[2 * pair + h % 2][:, o:o + P], lhs[rows_, h // 2, s_at:s_at + P],
                                         rhs[rows_, h // 2, t_at:t_at + P], start=True, stop=True)
                return M_(last)

            def select(level, pair, done):
                wait(dve, done, zero, s_dve.now(), set_up["c2_mark"])
                for t in range(T):
                    mask = MASKS[:, level, :].unsqueeze(1).broadcast_to([P, HG_H, P])
                    m = V_(dve.copy_predicated(HA[:, t, :, :], mask,
                                               bank[2 * pair + t][:, :].rearrange("p (h s) -> p h s", h=HG_H)))
                mark_free[pair] = [m]

            done = products(K2, Q2, 0, [s_dve.now()])
            pending = (7, 0, done)
            pair = 1
            for lv, n in enumerate(LEVELS[1:], 1):
                E2 = (EX, TM)[lv % 2]
                QK = (QKa, QKb)[lv % 2]
                b2, e2, x2 = blk(BC, 2 * n), blk(E2, 2 * n), blk(QK, 2 * n)
                q2, k2 = blk(Q2, 2 * n), blk(K2, 2 * n)
                shape = [P, 2 * S // (2 * n), n]
                anchor = b2[:, :, n - 1:n].broadcast_to(shape)
                wait(dve, s_act.now(), s_dve.now(), s_pe.now(0))
                V_(dve.tensor_tensor(e2[:, :, 0:n], anchor, b2[:, :, 0:n], ALU.subtract))
                m = V_(dve.tensor_tensor(e2[:, :, n:2 * n], b2[:, :, n:2 * n], anchor, ALU.subtract))
                wait(act, m)
                m = A_(act.activation(E2[:, :, :], E2[:, :, :], ACT.Exp))
                select(*pending)
                wait(dve, m)
                V_(dve.tensor_tensor(x2[:, :, 0:n], k2[:, :, 0:n], e2[:, :, 0:n], ALU.mult))
                m = V_(dve.tensor_tensor(x2[:, :, n:2 * n], q2[:, :, n:2 * n], e2[:, :, n:2 * n], ALU.mult))
                pending = (lv, pair, products(QK, QK, pair, [m]))
                pair ^= 1
            bc = blk(BC, 64)
            wait(dve, s_dve.now(), s_pe.now())
            m = V_(dve.tensor_tensor(blk(TN, 64), bc[:, :, 63:64].broadcast_to([P, 8, 64]), bc, ALU.subtract))
            wait(act, m, s_pe.now())
            A_(act.activation(EX[:, :, :], BC[:, :, :], ACT.Exp))
            m = A_(act.activation(TM[:, :, :], TN[:, :, :], ACT.Exp))
            select(*pending)
            wait(dve, m)
            V_(dve.tensor_tensor(K1[:, :, :], K2[:, :, :], TM[:, :, :], ALU.mult))
            m = V_(dve.tensor_tensor(Q1[:, :, :], Q2[:, :, :], EX[:, :, :], ALU.mult))
            done = products(K1, Q1, pair, [m])
            select(0, pair, done)
            pair ^= 1
            wait(dve, done)
            for k in range(2):
                V_(dve.tensor_scalar(K1[:, k, 0:64], K1[:, k, 0:64], EX[:, k, 127:128], None, ALU.mult))
                m = V_(dve.tensor_scalar(Q1[:, k, 192:256], Q1[:, k, 192:256], EX[:, k, 191:192], None, ALU.mult))
            done = products(K1, Q1, pair, [m], cross=True)
            wait(act, done)
            for odd in range(2):
                hx = A_(act.activation(HX[:, 2 * odd:2 * odd + 2, :],
                                       bank[2 * pair + odd][:, 0:S].rearrange("p (h s) -> p h s", h=2), ACT.Copy))
            wait(pe, hx, s_dve.now())
            for t in range(T):
                for h in range(HG_H):
                    d = bank[4 + t][:, h * HD:(h + 1) * HD]
                    v = lambda tt: UM[:, tt, o_hv + h * HD:o_hv + (h + 1) * HD]
                    last = pe.matmul(d, HA[:, h % 2, 2 * t + h // 2, :], v(t), start=True, stop=(t == 0))
                    if t == 1:
                        last = pe.matmul(d, HX[:, 2 * (h % 2) + h // 2, :], v(0), start=False, stop=True)
            m = M_(last)
            wait(act, m)
            gs = A_(act.activation(GS[:, :, :], UM[:, :, o_hg:o_hg + HALF], ACT.Silu))
            wait(dve, m, gs)
            for t in range(T):
                m = V_(dve.tensor_copy(K1[:, t, :], bank[4 + t][:, 0:HALF]))
            wait(dve, m)
            m = V_(dve.tensor_tensor(Q1[:, :, :], K1[:, :, :], K1[:, :, :], ALU.mult))
            wait(dve, m)
            m = V_(dve.tensor_reduce(ST[:, 0:8], Q1[:, :, :].rearrange("p t (h d) -> p (t h) d", h=HG_H), AX.X, ALU.add))
            r = rstd(ST[:, 0:8], HD, m)
            wait(dve, r)
            heads = K1[:, :, :].rearrange("p t (h d) -> p (t h) d", h=HG_H)
            m = V_(dve.tensor_tensor(heads, heads, ST[:, 0:8].unsqueeze(2).broadcast_to([P, 8, HD]), ALU.mult))
            wait(dve, m)
            m = V_(dve.tensor_tensor(heads, heads, OG[:, :].unsqueeze(1).broadcast_to([P, 8, HD]), ALU.mult))
            wait(dve, m)
            return V_(dve.tensor_tensor(YR[:, :, 0:HALF], K1[:, :, :], GS[:, :, :], ALU.mult))

        def rstd(st, n, mark):
            wait(dve, mark)
            m = V_(dve.tensor_scalar(st, st, 1.0 / n, EPS, ALU.mult, ALU.add))
            wait(act, m)
            m = A_(act.activation(st, st, ACT.Sqrt))
            wait(dve, m)
            return V_(dve.reciprocal(st, st))

        def fox(l, rows):
            wait(dve, *rows)
            V_(dve.tensor_scalar(FZ[:, 1, :, :], FZ[:, 0, :, :], 0.0, None, ALU.min))
            m = V_(dve.scalar_tensor_tensor(out=FZ[:, 2, :, :], in0=FZ[:, 0, :, :], scalar=-1.0,
                                            in1=FZ[:, 0, :, :], op0=ALU.mult, op1=ALU.max))
            wait(act, m)
            m = A_(act.activation(FZ[:, 3, :, :], FZ[:, 2, :, :], ACT.Exp, scale=-1.0))
            wait(dve, m)
            m = V_(dve.tensor_scalar(FZ[:, 2, :, :], FZ[:, 3, :, :], 1.0, None, ALU.add))
            wait(act, m)
            m = A_(act.activation(FZ[:, 3, :, :], FZ[:, 2, :, :], ACT.Ln))
            wait(dve, m)
            m = V_(dve.tensor_tensor(FZ[:, 0, :, :], FZ[:, 1, :, :], FZ[:, 3, :, :], ALU.subtract))
            wait(pe, m, set_up["c2_mark"], s_act.now(), s_dve.now())
            pe.matmul(bank[0][:, 0:FOX_H], TRI[:, 0, :], FZ[:, 0, 0, :], start=True, stop=True)
            pe.matmul(bank[0][:, FOX_H:2 * FOX_H], TRI[:, 1, :], FZ[:, 0, 0, :], start=True, stop=False)
            pe.matmul(bank[0][:, FOX_H:2 * FOX_H], TRI[:, 0, :], FZ[:, 0, 1, :], start=False, stop=True)
            pe.matmul(bank[1][0:FOX_H, 0:P], FZ[:, 0, 0, :], TRI[:, 0, :], start=True, stop=True)
            pe.matmul(bank[1][0:FOX_H, P:S], FZ[:, 0, 0, :], TRI[:, 1, :], start=True, stop=False)
            last = pe.matmul(bank[1][0:FOX_H, P:S], FZ[:, 0, 1, :], TRI[:, 0, :], start=False, stop=True)
            m = M_(last)
            wait(dve, m)
            V_(dve.tensor_copy(CC[:, :, :], bank[0][:, 0:2 * FOX_H].rearrange("p (t h) -> p t h", t=T)))
            V_(dve.tensor_scalar(NCT[:, :], bank[1][0:FOX_H, 0:S], -1.0, None, ALU.mult))
            sq = QKT[:, :, :].rearrange("p a b -> p (a b)").rearrange("p (t n) -> p t n", t=T)
            qk = UM[:, :, o_fq:o_fv]
            m = V_(dve.tensor_tensor(sq, qk, qk, ALU.mult))
            wait(dve, m)
            st = FST[:, 0, :, :]
            m = V_(dve.tensor_reduce(st, sq.rearrange("p t (h d) -> p t h d", d=HD), AX.X, ALU.add))
            r = rstd(st, HD, m)
            wait(dve, r)
            for t in range(T):
                v = qk[:, t, :].rearrange("p (h d) -> p h d", d=HD)
                m = V_(dve.tensor_tensor(v, v, FST[:, 0, t, :].unsqueeze(2).broadcast_to([P, 16, HD]), ALU.mult))
            wait(pe, m)
            for kp in range(0, NQK, 2):
                b = bank[4 + kp // 2]
                for k in (kp, kp + 1):
                    for t in range(T):
                        last = pe.transpose(b[:, (k - kp) * S + t * P:(k - kp) * S + (t + 1) * P],
                                            qk[:, t, k * P:(k + 1) * P], IDENT[:, :])
                m = M_(last)
                wait(dve, m)
                g = COLS[:, vec[f"foxq{l}"]:vec[f"foxq{l}"] + 1] if kp < 4 else COLS[:, vec[f"foxk{l}"]:vec[f"foxk{l}"] + 1]
                V_(dve.tensor_scalar(QKT[:, kp:kp + 2, :], b[:, :].rearrange("p (k s) -> p k s", k=2), g,
                                     HD ** -0.5 if kp < 4 else 1.0, ALU.mult, ALU.mult))
            units = [(h, t) for h in range(FOX_H) for t in range(T)]
            mk = {}
            wait(pe, s_dve.now(), s_act.now())
            wait(dve, s_dve.now())

            def scores(u):
                h, t = units[u]
                j, n = u % 2, (units[u][1] + 1) * P
                if u >= 2:
                    wait(pe, mk["s", u - 2])
                r_ = slice((h % 2) * HD, (h % 2 + 1) * HD)
                b = bank[j]
                pe.matmul(b[:, 0:n], QKT[r_, h // 2, t * P:(t + 1) * P], QKT[r_, 4 + h // 2, 0:n], start=True, stop=False)
                last = pe.matmul(b[:, 0:n], IDENT[0:FOX_H, h:h + 1].broadcast_to([FOX_H, P]), NCT[:, 0:n],
                                 start=False, stop=True)
                mk["q", u] = M_(last)

            def softmax(u):
                h, t = units[u]
                j, n = u % 2, (units[u][1] + 1) * P
                s_ = ST[:, 32 + 8 * j:40 + 8 * j]
                wait(dve, mk["q", u], mk.get(("e", u - 2)))
                mb = MB[:, :, :].rearrange("p a b -> p (a b)")[:, S - n:S]
                mk["s", u] = m = V_(dve.scalar_tensor_tensor(out=FS[j][:, 0:n], in0=bank[j][:, 0:n],
                                                             scalar=CC[:, t, h:h + 1], in1=mb,
                                                             op0=ALU.add, op1=ALU.add))
                wait(dve, m)
                m = V_(dve.tensor_reduce(s_[:, 0:1], FS[j][:, 0:n], AX.X, ALU.max, negate=True))
                wait(act, m, mk.get(("t", u - 2)))
                mk["e", u] = A_(act.activation(FP[j][:, 0:n], FS[j][:, 0:n], ACT.Exp, bias=s_[:, 0:1],
                                               accum_out=s_[:, 1:2]))

            def turn(u):
                h, t = units[u]
                j = u % 2
                wait(pe, mk["e", u], mk.get(("c", u - 2)))
                for kt in range(t + 1):
                    last = pe.transpose(bank[2 + j][:, kt * P:(kt + 1) * P], FP[j][:, kt * P:(kt + 1) * P], IDENT[:, :])
                mk["t", u] = M_(last)
                wait(act, mk["t", u], mk.get(("p", u - 2)))
                mk["c", u] = A_(act.activation(FT[j][:, 0:t + 1, :],
                                               bank[2 + j][:, 0:(t + 1) * P].rearrange("p (k q) -> p k q", q=P), ACT.Copy))

            def values(u):
                h, t = units[u]
                j = u % 2
                s_ = ST[:, 32 + 8 * j:40 + 8 * j]
                wait(pe, mk["c", u], mk.get(("o", u - 2)))
                for kt in range(t + 1):
                    last = pe.matmul(bank[4 + j][:, 0:HD], FT[j][:, kt, :], UM[:, kt, o_fv + h * HD:o_fv + (h + 1) * HD],
                                     start=(kt == 0), stop=(kt == t))
                mk["p", u] = M_(last)
                wait(dve, mk["e", u], mk["p", u])
                m = V_(dve.reciprocal(s_[:, 2:3], s_[:, 1:2]))
                wait(dve, m)
                mk["o", u] = V_(dve.tensor_scalar(YR[:, t, HALF + h * HD:HALF + (h + 1) * HD], bank[4 + j][:, 0:HD],
                                                  s_[:, 2:3], None, ALU.mult))

            scores(0)
            for u in range(len(units)):
                if u + 1 < len(units):
                    scores(u + 1)
                softmax(u)
                if u >= 1:
                    values(u - 1)
                turn(u)
            values(len(units) - 1)
            return s_dve.now()

        for l in range(2):
            mixer, second = Follow(col(f"mix2_{l}")), Follow(col(f"ffn2_{l}"))
            ffn2("ffn1_w_in_2", "ffn1_w_out_2", l, nxt, mixer, lambda: mix_small(l))
            rows_ = mix_in(l, mixer)
            cm = conv3(l, rows_)
            hm = hgrn(l, rows_)
            fm = fox(l, rows_)
            ym = to_columns(YR, [hm, fm], None, None, XTh, XTl, [*pe_idle(), s_act.now(), s_dve.now()], kn=6, k0=2)
            wait(act, cm)
            h_ = A_(act.activation(XTh[:, 0:2, :], CBT[:, :, :], ACT.Copy))
            wait(dve, h_)
            l_ = V_(dve.tensor_tensor(XTl[:, 0:2, :], CBT[:, :, :], XTh[:, 0:2, :].bitcast(F32), ALU.subtract))
            down(4, XTh, XTl, [*ym, h_, l_, *acc_free()], add_residual(), second)
            nxt = Follow(col("ffn1_1")) if l == 0 else Last()
            ffn2("ffn2_w_in_2", "ffn2_w_out_2", l, second, nxt, None)
        wait(sp, s_out.now())


def constants():
    c = {"ident": np.eye(P, dtype=np.float32)}
    comb = np.zeros((5, P), np.float32)
    comb[[0, 2, 4]] = 1
    c["combb"] = comb
    n = np.arange(S)
    ang = 2 * np.pi * (np.outer(n, n) % S) / S
    dft = np.concatenate([np.cos(ang), np.sin(ang)], axis=1).astype(np.float32)
    c["dft"] = dft.reshape(T, P, 2 * S).transpose(1, 0, 2).copy()
    m = np.arange(HD)
    ang = 2 * np.pi * (np.outer(m, m) % HD) / HD
    scale = 1.0 / np.sqrt(S * HD)
    ccm = np.zeros((P, 2, P), np.float32)
    for g in range(2):
        ccm[g * HD:(g + 1) * HD, 0, g * HD:(g + 1) * HD] = np.cos(ang) * scale
        ccm[g * HD:(g + 1) * HD, 1, g * HD:(g + 1) * HD] = -np.sin(ang) * scale
    c["ccm"] = ccm
    s, t = np.arange(P)[:, None], np.arange(P)[None, :]
    c["tri"] = np.stack([(s <= t), np.ones((P, P))], axis=1).astype(np.float32)
    c["causal"] = np.stack([np.zeros((P, P)), np.where(t <= s, 0.0, -1e30)], axis=1).astype(np.float32)
    masks = [(s // n + 1 == t // n) & (s // n % 2 == 0) for n in LEVELS] + [s == t]
    c["masks"] = np.stack(masks, axis=1).astype(np.float32)
    rows = S // GRID_W
    row = np.repeat(np.arange(rows, dtype=np.float32), GRID_W)
    colm = np.tile(np.arange(GRID_W, dtype=np.float32), rows)
    half = HD // 2
    inv = (ROPE_THETA ** (-np.arange(0, half, 2, dtype=np.float32) / half)).astype(np.float32)
    a = np.concatenate([row[:, None] * inv, colm[:, None] * inv], axis=-1)
    r = np.stack([np.cos(a), np.sin(a)], axis=1).astype(np.float32)
    c["rope"] = r.reshape(T, P, 2, half).transpose(1, 0, 2, 3).copy()
    return c


_INS = ['x', 'c', 'ctx', 'c_ctx', 'ada_w', 'ada_b', 'mix_norm_g', 'ffn_norm_g', 'ffn_w1', 'ffn_w3', 'ffn_w2',
        'ev_w_in', 'ev_lambda_q1', 'ev_lambda_k1', 'ev_lambda_q2', 'ev_lambda_k2', 'ev_subln_g', 'ev_fourier_w',
        'ev_w_out', 'od_pw1_w', 'od_pw1_b', 'od_dw_w', 'od_dw_b', 'od_ln_g', 'od_ln_b', 'od_pw2_w', 'od_pw2_b',
        'final_g', 'ffn1_norm_2', 'ffn1_w_in_2', 'ffn1_w_out_2', 'mix_norm_2', 'w_mix_in_2', 'conv_w_2',
        'hgrn_lb_logits_2', 'hgrn_out_gain_2', 'fox_q_gain_2', 'fox_k_gain_2', 'fox_f_bias_2', 'w_mix_out_2',
        'ffn2_norm_2', 'ffn2_w_in_2', 'ffn2_w_out_2']


def columns(inputs):
    parts, vec, n = [], {}, 0

    def add(name, a):
        nonlocal n
        a = np.asarray(a).reshape(-1, P)
        parts.append(a)
        vec[name] = n
        n += a.shape[0]

    add("c", inputs["c"])
    add("c_ctx", inputs["c_ctx"])
    for l in range(2):
        for name, key in (("mix", "mix_norm_g"), ("ffn", "ffn_norm_g"), ("ffn1_", "ffn1_norm_2"),
                          ("mix2_", "mix_norm_2"), ("ffn2_", "ffn2_norm_2"), ("lb", "hgrn_lb_logits_2"),
                          ("conv", "conv_w_2")):
            add(f"{name}{l}", inputs[key][l])
        for name, key in (("foxq", "fox_q_gain_2"), ("foxk", "fox_k_gain_2")):
            add(f"{name}{l}", np.concatenate([inputs[key][l], inputs[key][l]]))
    for name in ("od_dw_b", "od_ln_g", "od_ln_b"):
        add(name, inputs[name][0])
    add("subln", inputs["ev_subln_g"])
    taps = np.ascontiguousarray(np.asarray(inputs["od_dw_w"])[0].reshape(TAPS, KD, P).transpose(2, 1, 0))
    return {"cols": np.ascontiguousarray(np.concatenate(parts).T), "taps": taps}, vec


def kernel(**inputs):
    import concourse.bacc as _bacc
    from concourse.bass_utils import run_bass_kernel_spmd as _run

    nc = _bacc.Bacc("TRN2", target_bir_lowering=False, num_devices=1)
    arrays, aps = {}, {}
    for name in _INS:
        a = np.ascontiguousarray(inputs[name])
        arrays[f"in_{name}"] = a
        aps[name] = nc.dram_tensor(f"in_{name}", a.shape, mybir.dt.from_np(a.dtype), kind="ExternalInput").ap()
    small, vec = columns(inputs)
    aps["vec"] = vec
    for name, a in {**constants(), **small}.items():
        arrays[f"const_{name}"] = a
        aps[name] = nc.dram_tensor(f"const_{name}", a.shape, mybir.dt.from_np(a.dtype), kind="ExternalInput").ap()
    out = nc.dram_tensor("out_0", (1, S, D), F32, kind="ExternalOutput").ap()
    program(nc, aps, out)
    r = _run(nc, [arrays], core_ids=[0])
    return r.results[0]["out_0"]
```

```python
from contextlib import ExitStack, contextmanager

import numpy as np

import concourse.bass as bass
from concourse import mybir

F32 = mybir.dt.float32
F32R = mybir.dt.float32r
U8 = mybir.dt.uint8
ALU = mybir.AluOpType
ACT = mybir.ActivationFunctionType
AX = mybir.AxisListType

P = 128
D = 1024
KD = D // P
T = 2
S = T * P
FF = 2816
KF = FF // P
HALF = 256
CH = 2 * HALF
SLAB = 2048
RING = 4
EPS = 1e-6
GRID_W, ROPE_THETA, HD = 64, 10000.0, 64
DW, FW = 768, 256
VD = 128
HEADS1 = DW // VD
LAMBDA_INIT = 0.8 - 0.6
TAPS = 31
FOX_H, HG_H = 8, 4
MIX_IN = 3336
LEVELS = (64, 32, 16, 8, 4, 2, 1)


class Signal:

    def __init__(self, sem, step=1):
        self.sem, self.step, self.n, self.term, self.per = sem, step, 0, None, 0

    def on(self, ins):
        ins.then_inc(self.sem, self.step)
        self.n += self.step
        return self.now()

    def now(self, back=0):
        return (self, self.n - back * self.step, self.term)


def wait(eng, *marks):
    for m in marks:
        if m is None:
            continue
        sig, n, term = m
        if term is None:
            if n > 0:
                eng.wait_ge(sig.sem, n)
        else:
            eng.wait_ge(sig.sem, term + n)


@contextmanager
def repeat(loop, turns, per):
    with loop(0, turns) as i:
        starts = {}
        for sig, k in per.items():
            starts[sig] = sig.n
            sig.term = i * (k * sig.step)
        yield i
        for sig, k in per.items():
            assert sig.n - starts[sig] == k * sig.step, (sig.sem, sig.n - starts[sig], k)
    for sig, k in per.items():
        sig.n = starts[sig] + k * sig.step * turns
        sig.term = None


def program(nc, A, out):
    sem_count = [0]
    ctx = ExitStack()
    with ctx:
        def signal(name, step=1):
            sem_count[0] += 1
            return Signal(ctx.enter_context(nc.semaphore(name)), step)

        used_bytes = [-(-nc.sbuf_base // 32) * 32]

        def at(name, shape, offset, dt=F32):
            return nc.alloc_sbuf_tensor_at(name, list(shape), dt, offset=offset)

        def place(name, shape, dt=F32, bytes_=4):
            size = bytes_ * int(np.prod(shape[1:]))
            o = used_bytes[0]
            used_bytes[0] += -(-size // 32) * 32
            return at(name, shape, o, dt)

        raw = [place(f"raw{r}", [P, SLAB]) for r in range(RING)]
        hi = [place(f"hi{r}", [P, SLAB], F32R) for r in range(RING)]
        lo = [place(f"lo{r}", [P, SLAB], F32R) for r in range(RING)]
        X = place("X", [P, T, D])
        XTh = place("XTh", [P, KD, S], F32R)
        XTl = place("XTl", [P, KD, S], F32R)
        tmp_at = used_bytes[0]
        XN = place("XN", [P, T, D])
        FULL = place("FULL", [P, KD, S])
        ht_at = used_bytes[0]
        HTh = place("HTh", [P, KF, S], F32R)
        HTl = place("HTl", [P, KF, S], F32R)
        gate_at = used_bytes[0]
        GATE = place("GATE", [P, 4, D])
        IDENT = place("IDENT", [P, P])
        n_cols = A["cols"].shape[1]
        COLS = place("COLS", [P, n_cols])
        CS = place("CS", [P, KD, 2])
        MODS = place("MODS", [P, 2, 4, KD])
        MODC = place("MODC", [P, 2, KD])
        cst_at = used_bytes[0]
        used_bytes[0] += 5120
        ffn_slabs = KF + KF // 2
        total_slabs = 2 * 24 + (10 + 4) + (8 + 4) + 2 * ffn_slabs + 2 * (2 * ffn_slabs + 13 + 4)
        row_at = used_bytes[0]
        SG = place("SG", [P, T, HALF])
        HID = place("HID", [P, T, HALF])
        ST = place("ST", [P, 64])

        bank = [ctx.enter_context(nc.psum_tensor(f"bank{b}", [P, 512], F32)) for b in range(8)]

        pe, act, dve, pool, sp = nc.tensor, nc.scalar, nc.vector, nc.gpsimd, nc.sync

        landed = [signal(f"landed{r}", 16) for r in range(RING)]
        hi_done = signal("hi_done")
        lo_done = signal("lo_done")
        consumed = signal("consumed")
        s_pe, s_act, s_dve, s_pool = signal("s_pe"), signal("s_act"), signal("s_dve"), signal("s_pool")
        s_in = signal("s_in", 16)
        s_cols = signal("s_cols", 16)
        s_bias = signal("s_bias", 16)
        s_rope = signal("s_rope", 16)
        s_soft = signal("s_soft", 16)
        s_x, s_cx = signal("s_x", 16), signal("s_cx", 16)
        s_out = signal("s_out", 16)
        silu_done = signal("silu_done")
        hid_done = signal("hid_done")
        turned = signal("turned")
        hth_done = signal("hth_done")
        htl_done = signal("htl_done")

        g_load = [0]
        g_split = [0]
        g_use = [0]

        direct = []

        def splits(g):
            return g - sum(direct[:g])

        def val(sig, n, i):
            return (sig, n, None if i is None else i * 4)

        def load_slab(parts, i=None, raw_use=False):
            g = g_load[0]
            r = g % RING
            if g >= RING and direct[g - RING]:
                wait(sp, val(consumed, g - RING + 1, i))
            elif g >= RING:
                n = splits(g - RING + 1)
                wait(sp, val(hi_done, n, i), val(lo_done, n, i))
            for dst, src in parts(raw[r]):
                landed[r].on(sp.dma_start(dst, src))
            direct.append(raw_use)
            g_load[0] += 1

        def load_slabs(n, parts):
            first = n if n < 8 else n % 4
            if first < n and (g_load[0] < RING or any(direct[-RING:])):
                first += 4
            for s in range(first):
                load_slab(parts(s, 0))
            turns = (n - first) // 4
            if turns == 1:
                for s in range(first, n):
                    load_slab(parts(s, 0))
            elif turns:
                with repeat(sp.Fori, turns, {x: 2 for x in landed}) as i:
                    for s in range(first, first + 4):
                        load_slab(parts(s, i), i)
                direct.extend([False] * 4 * (turns - 1))
                g_load[0] = len(direct)

        def split_next(i=None):
            g = g_split[0]
            g_split[0] += 1
            if g >= total_slabs or any(direct[g:g + 1]):
                return
            r, n = g % RING, splits(g + 1)
            here = (landed[r], 32 * (g // RING + 1), None if i is None else i * 32)
            free = val(consumed, g - RING + 1, i)
            wait(act, here, free)
            hi_done.on(act.activation(hi[r][:, :], raw[r][:, :], ACT.Copy))
            wait(dve, here, free, val(hi_done, n, i))
            lo_done.on(dve.tensor_tensor(lo[r][:, :], raw[r][:, :], hi[r][:, :].bitcast(F32), ALU.subtract))

        def slab_ready(i=None):
            return ready_ahead(0, i)

        def ready_ahead(j, i=None):
            g = g_use[0] + j
            if direct[g]:
                wait(pe, (landed[g % RING], 32 * (g // RING + 1), None))
            else:
                n = splits(g + 1)
                wait(pe, val(hi_done, n, i), val(lo_done, n, i))
            return g % RING

        def slab_used(ins, i=None):
            consumed.on(ins)
            g_use[0] += 1

        def three(dst, xh, xl, wh, wl, start, stop):
            pe.matmul(dst, xh, wh, start=start, stop=False)
            pe.matmul(dst, xh, wl, start=False, stop=False)
            return pe.matmul(dst, xl, wh, start=False, stop=stop)

        def chunk_slab(half, banks, stats, i=None):
            r = slab_ready(i)
            for k in range(4):
                kk = 4 * half + k
                wh, wl = hi[r][:, k * CH:(k + 1) * CH], lo[r][:, k * CH:(k + 1) * CH]
                for b, (xh, xl) in zip(banks, stats):
                    last = three(b[:, :], xh(kk), xl(kk), wh, wl, kk == 0, kk == KD - 1)
            slab_used(last, i)

        def tiles(h, l, k0=0):
            return [((lambda k, t=t: h[:, k0 + k, t * P:(t + 1) * P]),
                     (lambda k, t=t: l[:, k0 + k, t * P:(t + 1) * P])) for t in range(T)]

        def slab_mark(i=None):
            return val(consumed, g_use[0], i)

        def row_tiles(w):
            return w.rearrange("(k p) n -> p k n", p=P)

        def up_parts(wa, ca, wb, cb, width=HALF):
            va, vb = row_tiles(wa), row_tiles(wb)

            def parts(s, i):
                c, half = s // 2, s % 2
                off = c * width if i is None or isinstance(i, int) and i == 0 else i * (2 * width) + c * width

                def into(slot):
                    v = slot[:, :].rearrange("p (k n) -> p k n", k=4)
                    ks = slice(4 * half, 4 * half + 4)
                    return [(v[:, :, 0:HALF], va[:, ks, bass.ds(off + ca, HALF)]),
                            (v[:, :, HALF:CH], vb[:, ks, bass.ds(off + cb, HALF)])]
                return into
            return parts

        def down_parts(w):
            v = row_tiles(w)

            def parts(s, i):
                def into(slot):
                    d = slot[:, :].rearrange("p (k n) -> p k n", k=2)
                    res = []
                    for k in range(2):
                        kk = 2 * s + k if i is None or isinstance(i, int) else i * 8 + (2 * s + k)
                        res.append((d[:, k, :], w[bass.ds(kk * P, P), :]))
                    return res
                return into
            return parts

        def A_(ins):
            return s_act.on(ins)

        def V_(ins):
            return s_dve.on(ins)

        def M_(ins):
            return s_pe.on(ins)

        def G_(ins):
            return s_pool.on(ins)

        acc = [[bank[4 + 2 * t + n] for n in range(2)] for t in range(T)]

        def down(nslab, xh, xl, first_mark, residual, follow, late=None):
            def products(r, s, t):
                for kk in (2 * s, 2 * s + 1):
                    sh, sl = xh[:, kk, t * P:(t + 1) * P], xl[:, kk, t * P:(t + 1) * P]
                    o = (kk - 2 * s) * D
                    w = [(hi[r][:, o + n * 512:o + n * 512 + 512], lo[r][:, o + n * 512:o + n * 512 + 512])
                         for n in range(2)]
                    for n in range(2):
                        pe.matmul(acc[t][n][:, :], sh, w[n][0], start=kk == 0, stop=False)
                        pe.matmul(acc[t][n][:, :], sh, w[n][1], start=False, stop=False)
                    for n in range(2):
                        last = pe.matmul(acc[t][n][:, :], sl, w[n][0], start=False, stop=kk == 2 * nslab - 1)
                return last

            wait(pe, *first_mark)
            follow.open()
            for s in range(nslab - 3):
                r = slab_ready()
                for t in range(T):
                    last = products(r, s, t)
                slab_used(last)
                if late is not None and s == 0:
                    late_marks = late()
                split_next()
            if late is not None:
                wait(pe, *late_marks)
            tail = [(ready_ahead(j), nslab - 3 + j) for j in range(3)]
            for r, s in tail:
                last = products(r, s, 0)
            follow.rows(0, residual(0, M_(last)))
            slab_used(products(*tail[0], 1))
            follow.turn(0)
            split_next()
            slab_used(products(*tail[1], 1))
            split_next()
            slab_used(products(*tail[2], 1))
            follow.rows(1, residual(1, slab_mark()))

        x_mark = [None, None]

        def add_residual(gate=None, half=False, bias=None):
            def residual(t, done):
                wait(dve, done, x_mark[t])
                for n in range(2):
                    cols = slice(n * 512, n * 512 + 512)
                    src = acc[t][n][:, :]
                    if gate is None:
                        m = V_(dve.scalar_tensor_tensor(out=X[:, t, cols], in0=src, scalar=0.5 if half else 1.0,
                                                        in1=X[:, t, cols], op0=ALU.mult, op1=ALU.add))
                    else:
                        if bias is not None:
                            m = V_(dve.tensor_tensor(XN[:, t, cols], src, bias[:, cols], ALU.add))
                            wait(dve, m)
                            src = XN[:, t, cols]
                        m = V_(dve.tensor_tensor(XN[:, t, cols], src, GATE[:, gate, cols], ALU.mult))
                if gate is not None:
                    wait(dve, m)
                    m = V_(dve.tensor_tensor(X[:, t, :], X[:, t, :], XN[:, t, :], ALU.add))
                x_mark[t] = m
                return m
            return residual

        class Follow:

            def __init__(self, gains, shifts=None, final=None):
                self.gains, self.shifts, self.final = gains, shifts, final
                self.marks = [None, None]

            def open(self):
                self.free = [*pe_idle(), s_act.now(), s_dve.now(), htl_done.now(), hth_done.now()]

            def rows(self, t, mark):
                self.mark = mark
                if self.final is not None:
                    m = rstd_of(X[:, t, :], D, 2 + t, [mark, *self.free], XN[:, t, :])
                    wait(dve, m, s_act.now())
                    x_mark[t] = self.mark = V_(dve.scalar_tensor_tensor(
                        out=X[:, t, :], in0=X[:, t, :], scalar=ST[:, 2 + t:3 + t], in1=self.final, op0=ALU.mult,
                        op1=ALU.mult))
                if self.shifts is not None:
                    m = rstd_of(X[:, t, :], D, t, [mark, *self.free], XN[:, t, :])
                    wait(dve, m, s_act.now())
                    self.mark = V_(dve.tensor_scalar(XN[:, t, :], X[:, t, :], ST[:, t:t + 1], None, ALU.mult))

            def turn(self, t):
                rows = X if self.shifts is None else XN
                cols = slice(t * P, (t + 1) * P)
                wait(pe, self.mark, *self.free, s_dve.now())
                ms = []
                for h in range(2):
                    b = bank[2 + 2 * t + h]
                    for k in range(4):
                        last = pe.transpose(b[:, k * P:(k + 1) * P], rows[:, t, (4 * h + k) * P:(4 * h + k + 1) * P],
                                            IDENT[:, :])
                    ms.append(M_(last))
                wait(dve, *self.free)
                fs = []
                for h in range(2):
                    b = bank[2 + 2 * t + h]
                    ks = slice(4 * h, 4 * h + 4)
                    wait(dve, ms[h])
                    if self.shifts is None:
                        m = V_(dve.tensor_tensor(FULL[:, ks, cols], b[:, :].rearrange("p (k s) -> p k s", k=4),
                                                 self.gains[:, ks].unsqueeze(2).broadcast_to([P, 4, P]), ALU.mult))
                    else:
                        for k in range(4):
                            kk = 4 * h + k
                            m = V_(dve.tensor_scalar(FULL[:, kk, cols], b[:, k * P:(k + 1) * P],
                                                     self.gains[:, kk:kk + 1], self.shifts[:, kk:kk + 1],
                                                     ALU.mult, ALU.add))
                    fs.append(m)
                wait(act, *self.free, self.mark)
                for h in range(2):
                    ks = slice(4 * h, 4 * h + 4)
                    wait(act, fs[h])
                    m = A_(act.activation(XTh[:, ks, cols], FULL[:, ks, cols], ACT.Copy))
                    wait(dve, m)
                    l = V_(dve.tensor_tensor(XTl[:, ks, cols], FULL[:, ks, cols], XTh[:, ks, cols].bitcast(F32),
                                             ALU.subtract))
                self.marks[t] = [m, l]

            def factors(self):
                if self.shifts is not None:
                    return
                for t in range(T):
                    wait(act, x_mark[t], *self.free)
                    m = A_(act.activation(XN[:, t, :], X[:, t, :], ACT.Square, accum_out=ST[:, t:t + 1]))
                rstd(ST[:, 0:T], D, m)


        class Last:

            def open(self):
                pass

            def turn(self, t):
                pass

            def rows(self, t, mark):
                wait(sp, mark)
                s_out.on(sp.dma_start(out[0, t * P:(t + 1) * P, :], X[:, t, :]))

        def rstd(st, n, mark):
            wait(dve, mark)
            m = V_(dve.tensor_scalar(st, st, 1.0 / n, EPS, ALU.mult, ALU.add))
            wait(act, m)
            m = A_(act.activation(st, st, ACT.Sqrt))
            wait(dve, m)
            return V_(dve.reciprocal(st, st))

        def rstd_of(src, n, base, mark, junk):
            wait(act, *mark)
            m = A_(act.activation(junk, src, ACT.Square, accum_out=ST[:, base:base + 1]))
            return rstd(ST[:, base:base + 1], n, m)

        def to_columns(rows, rows_mark, gains, shifts, xh, xl, free, kn=KD, k0=0, banks=(4, 5, 6, 7)):
            wait(pe, *rows_mark)
            marks = []
            full_mark = None
            for kp in range(0, kn, 2):
                b = bank[banks[(kp // 2) % len(banks)]]
                if kp // 2 >= len(banks):
                    wait(pe, marks[kp // 2 - len(banks)][0])
                ks = range(kp, min(kp + 2, kn))
                for k in ks:
                    for t in range(T):
                        last = pe.transpose(b[:, (k - kp) * S + t * P:(k - kp) * S + (t + 1) * P],
                                            rows[:, t, k * P:(k + 1) * P], IDENT[:, :])
                turned_m = M_(last)
                wait(dve, turned_m)
                for k in ks:
                    src = b[:, (k - kp) * S:(k - kp + 1) * S]
                    if shifts is not None:
                        m = V_(dve.tensor_scalar(FULL[:, k, :], src, gains[:, k:k + 1], shifts[:, k:k + 1],
                                                 ALU.mult, ALU.add))
                    elif gains is not None:
                        m = V_(dve.tensor_scalar(FULL[:, k, :], src, gains[:, k:k + 1], None, ALU.mult))
                    else:
                        m = V_(dve.tensor_copy(FULL[:, k, :], src))
                full_mark = m
                a, z = kp, kp + len(ks)
                wait(act, m, *free)
                h = A_(act.activation(xh[:, k0 + a:k0 + z, :], FULL[:, a:z, :], ACT.Copy))
                wait(dve, h, *free)
                l = V_(dve.tensor_tensor(xl[:, k0 + a:k0 + z, :], FULL[:, a:z, :],
                                         xh[:, k0 + a:k0 + z, :].bitcast(F32), ALU.subtract))
                marks.append((full_mark, h, l))
            return [marks[-1][1], marks[-1][2]]

        def pe_idle():
            return [slab_mark() if g_use[0] else None, s_pe.now()]

        def ffn_step(c, pair, i, follow):
            banks = [bank[2 * pair + t] for t in range(T)]
            first = i is None
            if first:
                first_chunk(banks, follow)
            else:
                wait(pe, hid_done.now(2))
                chunk_slab(0, banks, tiles(XTh, XTl), i)
                split_next(i)
                turn_chunk(i, c - 1)
                chunk_slab(1, banks, tiles(XTh, XTl), i)
            wait(act, slab_mark(i))
            for t in range(T):
                plain = follow.shifts is None
                silu_done.on(act.activation(SG[:, t, :], banks[t][:, 0:HALF], ACT.Silu,
                                            scale=ST[:, t:t + 1] if plain else 1.0))
                wait(dve, silu_done.now())
                if plain:
                    m = dve.scalar_tensor_tensor(out=HID[:, t, :], in0=banks[t][:, HALF:CH], scalar=ST[:, t:t + 1],
                                                 in1=SG[:, t, :], op0=ALU.mult, op1=ALU.mult)
                else:
                    m = dve.tensor_tensor(HID[:, t, :], SG[:, t, :], banks[t][:, HALF:CH], ALU.mult)
                hid_done.on(m)
            split_next(i)

        def first_chunk(banks, follow):
            def products(r, half, t):
                for k in range(4):
                    kk = 4 * half + k
                    xh, xl = XTh[:, kk, t * P:(t + 1) * P], XTl[:, kk, t * P:(t + 1) * P]
                    last = three(banks[t][:, :], xh, xl, hi[r][:, k * CH:(k + 1) * CH], lo[r][:, k * CH:(k + 1) * CH],
                                 kk == 0, kk == KD - 1)
                return last
            rs = [ready_ahead(0)]
            wait(pe, *follow.marks[0])
            products(rs[0], 0, 0)
            follow.turn(1)
            split_next()
            follow.factors()
            rs.append(ready_ahead(1))
            products(rs[1], 1, 0)
            wait(pe, *follow.marks[1])
            slab_used(products(rs[0], 0, 1))
            split_next()
            slab_used(products(rs[1], 1, 1))
            wait(act, s_dve.now())
            wait(dve, s_dve.now())

        def turn_chunk(i, c, b=None):
            b = bank[4] if b is None else b
            off = 2 * c if i is None else i * 4 + 2 * c
            wait(pe, hid_done.now(), htl_done.now())
            for f in range(2):
                for t in range(T):
                    last = pe.transpose(b[:, f * S + t * P:f * S + (t + 1) * P], HID[:, t, f * P:(f + 1) * P],
                                        IDENT[:, :])
            turned.on(last)
            src = b[:, :].rearrange("p (f s) -> p f s", f=2)
            wait(act, turned.now())
            hth_done.on(act.activation(HTh[:, bass.ds(off, 2), :], src, ACT.Copy))
            wait(dve, hth_done.now())
            htl_done.on(dve.tensor_tensor(HTl[:, bass.ds(off, 2), :], src,
                                          HTh[:, bass.ds(off, 2), :].bitcast(F32), ALU.subtract))

        def ffn_up(follow):
            ffn_step(0, 0, None, follow)
            g0 = (g_split[0], g_use[0])
            n = KF // 2
            assert n % 2 == 1
            turns = (n - 1) // 2
            with repeat(nc.Fori, turns, {silu_done: 4, hid_done: 4, turned: 2, hth_done: 2, htl_done: 2}) as i:
                ffn_step(1, 1, i, follow)
                ffn_step(2, 0, i, follow)
            g_split[0], g_use[0] = g0[0] + 4 * turns, g0[1] + 4 * turns
            sync_ring()

        def sync_ring():
            hi_done.n = lo_done.n = splits(g_split[0])
            consumed.n = g_use[0]

        def ffn(follow, residual, then, during=None):
            ffn_up(follow)
            free = acc_free()
            if during is not None:
                during()

            def late():
                turn_chunk(None, KF // 2 - 1, bank[2])
                return hth_done.now(), htl_done.now()
            down(KF // 2, HTh, HTl, free, residual, then, late)

        def acc_free():
            return [s_dve.now(), s_act.now(), htl_done.now(), hth_done.now()]

        def load_const(dst, src, sig=None, eng=None):
            sig = (s_in if eng is None else s_soft) if sig is None else sig
            sig.on((act if eng is None else eng).dma_start(dst, src))
            return sig.now()

        ROW = at("ROW", [4, D], row_at)
        SUM = place("SUM", [4, P])
        MSUM = place("MSUM", [P, KD, 3])
        UROW = at("UROW", [P, T, 2560], ht_at)
        CTXh = at("CTXh", [P, KD, S], ht_at + 20480, F32R)
        CTXl = at("CTXl", [P, KD, S], ht_at + 28672, F32R)
        CX = at("CX", [P, T, D], ht_at + 36864)
        QT = at("QT", [P, HEADS1, S], ht_at + 20480)
        KT = at("KT", [P, HEADS1, 2 * S], ht_at + 26624)
        OROW = at("OROW", [P, T, DW], ht_at + 38912)
        CROW = at("CROW", [P, T, 2 * DW], tmp_at)
        scr_at = tmp_at - 16384
        ONES = at("ONES", [P, P], cst_at)
        SUBG = place("SUBG", [P, 8])
        LAM = place("LAM", [P, 8])
        DFT = at("DFT", [P, T, 2 * S], cst_at)
        CCM = at("CCM", [P, 2, P], cst_at + 4096)

        SCRAP = place("SCRAP", [P, 16])
        scrap = iter(range(16))
        for sig, eng in ((silu_done, pool), (hth_done, pool), (hid_done, dve), (htl_done, dve)):
            for _ in range(4):
                n_ = next(scrap)
                sig.on(eng.memset(SCRAP[:, n_:n_ + 1], 0.0))

        vec = A["vec"]

        def col(name, n=KD):
            return COLS[:, vec[name]:vec[name] + n]

        cols_mark = load_const(COLS[:, :], A["cols"], s_cols)
        load_const(SUM[0:3, :], A["sum"])
        x_in = load_const(X[:, :, :], A["x"][0, :, :].rearrange("(t p) d -> p t d", p=P), s_x)
        x_mark[:] = [x_in] * T
        cx_in = load_const(CX[:, :, :], A["ctx"][0, :, :].rearrange("(t p) d -> p t d", p=P), s_cx)
        ident_mark = load_const(IDENT[:, :], A["ident"])

        wait(act, cols_mark)
        cs_mark = A_(act.activation(CS[:, :, :], col("c", 2 * KD).rearrange("p (c k) -> p k c", c=2), ACT.Silu))

        def wide_parts(w, c0):
            v = row_tiles(w)

            def into(slot):
                d = slot[:, :].rearrange("p (k n) -> p k n", k=KD)
                return [(d[:, 4 * h:4 * h + 4, :], v[:, 4 * h:4 * h + 4, c0:c0 + HALF]) for h in range(2)]
            return into

        def load_ada(l, mods):
            for mod in mods:
                for s in range(4):
                    load_slab(wide_parts(A["ada_w"][l, :, :], mod * D + s * HALF), raw_use=True)

        def ada_slabs(l, mod, b):
            wait(act, s_pe.now())
            bias_mark = load_const(ROW[2:3, :], A["ada_b"][l:l + 1, mod * D:(mod + 1) * D], s_bias)
            wait(pe, *ada_free)
            for s in range(4):
                r = slab_ready()
                w = raw[r][:, :].rearrange("p (k n) -> p k n", k=KD)
                half = slice((s % 2) * HALF, (s % 2 + 1) * HALF)
                if s == 2:
                    wait(pe, last_read)
                for k in range(KD):
                    last = pe.matmul(b[0:2, half], CS[:, k, :], w[:, k, :], start=(k == 0), stop=(k == KD - 1))
                slab_used(last)
                if s % 2:
                    wait(act, slab_mark())
                    last_read = A_(act.activation(ROW[0:2, (s // 2) * CH:(s // 2 + 1) * CH], b[0:2, :], ACT.Copy))
                split_next()
                yield
            yield
            wait(pe, last_read, bias_mark, ident_mark)
            if mod in (2, 5):
                for h in range(2):
                    if h:
                        yield
                    wait(pe, last_read)
                    m = M_(pe.matmul(b[:, :], SUM[0:3, :], ROW[0:3, h * 512:(h + 1) * 512], start=True, stop=True))
                    wait(act, m)
                    last_read = A_(act.activation(GATE[:, 2 * l + (mod == 5), h * 512:(h + 1) * 512], b[:, :],
                                                  ACT.Copy))
                ada_free[:] = [last_read]
                return
            n = (0, 1, None, 2, 3)[mod]
            for k in range(KD):
                last = pe.transpose(b[:, 4 * k:4 * k + 3], ROW[0:3, k * P:(k + 1) * P], IDENT[0:3, 0:3])
            v = b[:, 0:4 * KD].rearrange("p (k c) -> p k c", c=4)
            wait(dve, M_(last), mods_mark[0])
            m = V_(dve.tensor_copy(MSUM[:, :, :], v[:, :, 0:3]))
            ada_free[:] = [m]
            wait(dve, m)
            m = V_(dve.tensor_tensor(MODS[:, l, n, :], MSUM[:, :, 0], MSUM[:, :, 2], ALU.add))
            if l == 0 and n < 2:
                m = V_(dve.tensor_tensor(MODC[:, n, :], MSUM[:, :, 1], MSUM[:, :, 2], ALU.add))
            if n % 2:
                g = col(f"mix{l}" if n == 1 else f"ffn{l}")
                wait(dve, m)
                m = V_(dve.scalar_tensor_tensor(out=MODS[:, l, n, :], in0=MODS[:, l, n, :], scalar=1.0,
                                                in1=g, op0=ALU.add, op1=ALU.mult))
                if l == 0 and n == 1:
                    m = V_(dve.scalar_tensor_tensor(out=MODC[:, 1, :], in0=MODC[:, 1, :], scalar=1.0,
                                                    in1=g, op0=ALU.add, op1=ALU.mult))
            mods_mark[0] = m

        ada_free, mods_mark = [], [None]

        def background(jobs):
            def run():
                for g in jobs:
                    yield from g
            it = run()

            def step(n=1):
                for _ in range(n):
                    next(it, None)
            return step

        load_ada(0, [0, 1])
        w_in = A["ev_w_in"][0, :, :]
        cols5 = [(0, HALF), (512, 2304), (768, 1024), (1280, 1536), (1792, 2048)]
        for a, b2 in cols5:
            load_slabs(2, up_parts(w_in, a, w_in, b2))
        load_ada(0, [2, 3, 4, 5])
        load_ada(1, [0, 1])
        w_out1 = A["ev_w_out"][0, :, :]
        load_slabs(4, down_parts(w_out1))
        for _ in range(RING):
            split_next()
        wait(pe, cs_mark)
        ada_now = background([ada_slabs(0, 0, bank[0]), ada_slabs(0, 1, bank[0])])
        ada_now(2)
        cn = []
        for src, dst, mark, o in ((X, XN, x_in, 0), (CX, CX, cx_in, 2)):
            for t in range(T):
                m = rstd_of(src[:, t, :], D, o + t, [mark, *cn[-1:]], FULL[:, 0:4, :].rearrange("p k s -> p (k s)"))
                wait(dve, m, mark, s_act.now())
                cn.append(V_(dve.tensor_scalar(dst[:, t, :], src[:, t, :], ST[:, o + t:o + t + 1], None, ALU.mult)))
            ada_now(1)
        ada_now(12)

        load_const(DFT[:, :, :], A["dft"], s_rope)
        load_const(CCM[:, :, :], A["ccm"], s_rope)
        ROPE = at("ROPE", [P, T, 2, 32], ht_at + 44032)
        SS = place("SS", [P, T, 8])
        assert used_bytes[0] <= nc.sbuf_usable_end, used_bytes[0]
        wait(pe, ident_mark)
        xm = to_columns(XN, [cn[1], mods_mark[0]], MODS[:, 0, 1, :], MODS[:, 0, 0, :], XTh, XTl, [mods_mark[0]])
        wait(pe, *xm)
        stats = tiles(XTh, XTl)
        stats_c = tiles(CTXh, CTXl)
        reads = {}
        for c, (a, b2) in enumerate(cols5):
            both = c >= 2
            o = 4 * (c % 2)
            banks = bank[o:o + 4] if both else bank[o:o + 2]
            wait(pe, reads.get(o), reads.get(o + 1))
            chunk_slab(0, banks, stats + (stats_c if both else []))
            split_next()
            if c == 0:
                cm = to_columns(CX, [cn[3]], MODC[:, 1, :], MODC[:, 0, :], CTXh, CTXl, [s_act.now(), s_dve.now()],
                                banks=(6, 7, 2, 3))
                wait(act, s_pe.now())
                load_const(ROPE[:, :, :, :], A["rope"], s_rope)
            if c == 1:
                wait(pe, *cm)
            chunk_slab(1, banks, stats + (stats_c if both else []))
            done = slab_mark()
            wait(act, done)
            wait(dve, done)
            for j, cc in enumerate((a, b2)):
                src = slice(j * HALF, (j + 1) * HALF)
                m1 = A_(act.activation(UROW[:, 0, cc:cc + HALF], banks[0][:, src], ACT.Copy))
                m2 = V_(dve.tensor_copy(UROW[:, 1, cc:cc + HALF], banks[1][:, src]))
                if both:
                    m1 = A_(act.activation(CROW[:, 0, cc - DW:cc - DW + HALF], banks[2][:, src], ACT.Copy))
                    m2 = V_(dve.tensor_copy(CROW[:, 1, cc - DW:cc - DW + HALF], banks[3][:, src]))
            reads[o], reads[o + 1] = m1, m2
            split_next()
            wait(dve, m1, m2, s_rope.now())
            for cc in (a, b2):
                if cc >= 2 * DW:
                    continue
                rows = UROW[:, :, cc:cc + HALF].rearrange("p t (h x d) -> p t h x d", h=4, x=2)
                for t in range(T):
                    cos = ROPE[:, t, 0:1, :].broadcast_to([P, 4, 32])
                    sin = ROPE[:, t, 1:2, :].broadcast_to([P, 4, 32])
                    x1, x2 = rows[:, t, :, 0, :], rows[:, t, :, 1, :]
                    tl = [at(f"rt{cc}_{t}_{n}", [P, 4, 32], ht_at + 38912 + 2048 * t + 512 * n) for n in range(4)]
                    for dst, u, v in ((tl[0], x1, cos), (tl[1], x2, sin), (tl[2], x1, sin), (tl[3], x2, cos)):
                        m = V_(dve.tensor_tensor(dst[:, :, :], u, v, ALU.mult))
                    wait(dve, m)
                    V_(dve.tensor_tensor(x1, tl[0][:, :, :], tl[1][:, :, :], ALU.subtract))
                    q_mark = k_mark = V_(dve.tensor_tensor(x2, tl[2][:, :, :], tl[3][:, :, :], ALU.add))
                wait(dve, q_mark)
        rows_ready = (m1, m2)

        def scr(name, shape, off, dt=F32):
            return at(name, shape, scr_at + off, dt)
        ada_jobs = background([ada_slabs(0, mod, bank[7]) for mod in (2, 3, 4, 5)] +
                              [ada_slabs(1, mod, bank[7]) for mod in (0, 1)])
        ada_free[:] = [s_act.now(), s_dve.now()]
        wait(pe, *rows_ready, *pe_idle())
        wait(act, *pe_idle())
        wait(dve, *pe_idle())
        bank_read = {}
        n = 0
        for src, dst, s0, mk in ((CROW[:, :, 0:DW], KT, 0, None), (UROW[:, :, 0:DW], QT, 0, q_mark),
                                 (UROW[:, :, DW:2 * DW], KT, S, k_mark)):
            wait(pe, mk)
            for hp in range(0, HEADS1, 2):
                b = bank[n % 7]
                wait(pe, bank_read.get(n % 7))
                for h in (hp, hp + 1):
                    for t in range(T):
                        last = pe.transpose(b[:, (h - hp) * S + t * P:(h - hp) * S + (t + 1) * P],
                                            src[:, t, h * P:(h + 1) * P], IDENT[:, :])
                m = M_(last)
                out_ap = dst[:, hp:hp + 2, s0:s0 + S]
                in_ap = b[:, :].rearrange("p (h s) -> p h s", h=2)
                if n % 2:
                    wait(act, m)
                    bank_read[n % 7] = A_(act.activation(out_ap, in_ap, ACT.Copy))
                else:
                    wait(dve, m)
                    bank_read[n % 7] = V_(dve.tensor_copy(out_ap, in_ap))
                n += 1
            ada_jobs(1)
        heads_ready = [s_act.now(), s_dve.now()]

        LQ = at("LQ", [P, 4, HD], ht_at + 43008)
        wait(act, *heads_ready, s_pool.now())
        for n, name in enumerate(("ev_lambda_q1", "ev_lambda_k1", "ev_lambda_q2", "ev_lambda_k2")):
            m = load_const(LQ[:, n, :], A[name][0, :].partition_broadcast(P))
        wait(dve, m)
        for n in range(2):
            m = V_(dve.tensor_tensor(LQ[:, 2 * n, :], LQ[:, 2 * n, :], LQ[:, 2 * n + 1, :], ALU.mult))
        wait(dve, m)
        for n in range(2):
            m = V_(dve.tensor_reduce(LAM[:, n:n + 1], LQ[:, 2 * n, :], AX.X, ALU.add))
        wait(act, m)
        m = A_(act.activation(LAM[:, 2:4], LAM[:, 0:2], ACT.Exp))
        wait(dve, m)
        m = V_(dve.tensor_scalar(LAM[:, 5:6], LAM[:, 3:4], LAMBDA_INIT, None, ALU.subtract))
        wait(dve, m)
        lam_mark = V_(dve.tensor_tensor(LAM[:, 4:5], LAM[:, 2:3], LAM[:, 5:6], ALU.subtract))

        P0 = [scr(f"P0_{j}", [P, 2 * S], 2048 * j) for j in range(2)]
        P1 = [scr(f"P1_{j}", [P, 2 * S], 4096 + 2048 * j) for j in range(2)]
        AT = [scr(f"AT_{j}", [P, 4, P], 8192 + 2048 * j) for j in range(2)]
        OSQ = scr("OSQ", [P, P], 12288)
        units = [(h, t) for h in range(HEADS1) for t in range(T)]
        wait(pe, *heads_ready)
        wait(act, lam_mark)
        wait(dve, lam_mark)
        marks = {}

        def diff_scores(u):
            h, t = units[u]
            j = u % 2
            if u >= 2:
                wait(pe, marks["exp", u - 2])
            for c in range(2):
                cs = slice(c * HD, (c + 1) * HD)
                last = pe.matmul(bank[2 * j + c][:, :], QT[cs, h, t * P:(t + 1) * P], KT[cs, h, :],
                                 start=True, stop=True)
            marks["s", u] = M_(last)

        def diff_softmax(u):
            j = u % 2
            st = ST[:, 8 * j:8 * j + 8]
            wait(dve, marks["s", u])
            for c in range(2):
                m = V_(dve.tensor_reduce(st[:, c:c + 1], bank[2 * j + c][:, :], AX.X, ALU.max))
            wait(dve, m)
            m = V_(dve.tensor_scalar(st[:, 2:4], st[:, 0:2], -HD ** -0.5, None, ALU.mult))
            wait(act, m)
            if u >= 2:
                wait(act, marks["at", u - 2], marks["t", u - 2])
            for c, pb in ((0, P0[j]), (1, P1[j])):
                m = A_(act.activation(pb[:, :], bank[2 * j + c][:, :], ACT.Exp, bias=st[:, 2 + c:3 + c],
                                      scale=HD ** -0.5, accum_out=st[:, 4 + c:5 + c]))
            marks["exp", u] = m

        def diff_combine(u):
            j = u % 2
            st = ST[:, 8 * j:8 * j + 8]
            wait(dve, marks["exp", u])
            m = V_(dve.reciprocal(st[:, 6:8], st[:, 4:6]))
            wait(dve, m)
            m = V_(dve.tensor_scalar(st[:, 7:8], st[:, 7:8], LAM[:, 4:5], None, ALU.mult))
            wait(dve, m)
            m = V_(dve.tensor_scalar(P1[j][:, :], P1[j][:, :], st[:, 7:8], None, ALU.mult))
            wait(dve, m)
            marks["a", u] = V_(dve.scalar_tensor_tensor(out=P0[j][:, :], in0=P0[j][:, :], scalar=st[:, 6:7],
                                                        in1=P1[j][:, :], op0=ALU.mult, op1=ALU.subtract))

        def diff_turn(u):
            j = u % 2
            wait(pe, marks["a", u])
            if u >= 2:
                wait(pe, marks["at", u - 2])
            for kt in range(4):
                last = pe.transpose(bank[4 + j][:, kt * P:(kt + 1) * P], P0[j][:, kt * P:(kt + 1) * P], IDENT[:, :])
            marks["t", u] = M_(last)
            wait(act, marks["t", u])
            if u >= 2:
                wait(act, marks["pv", u - 2])
            marks["at", u] = A_(act.activation(AT[j][:, :, :], bank[4 + j][:, :].rearrange("p (k q) -> p k q", k=4),
                                               ACT.Copy))

        def diff_values(u):
            h, t = units[u]
            j = u % 2
            wait(pe, marks["at", u])
            if u >= 1:
                wait(pe, marks["o", u - 1])
            for kt in range(4):
                v = CROW[:, kt, DW + h * P:DW + (h + 1) * P] if kt < 2 else \
                    UROW[:, kt - 2, 2 * DW + h * P:2 * DW + (h + 1) * P]
                last = pe.matmul(bank[6][:, 0:P], AT[j][:, kt, :], v, start=(kt == 0), stop=(kt == 3))
            marks["pv", u] = M_(last)
            wait(dve, marks["pv", u])
            m = marks["o", u] = V_(dve.tensor_copy(OROW[:, t, h * P:(h + 1) * P], bank[6][:, 0:P]))
            wait(act, m, marks.get(("sq", u - 1)))
            marks["sq", u] = A_(act.activation(OSQ[:, :], OROW[:, t, h * P:(h + 1) * P], ACT.Square,
                                               accum_out=SS[:, t, h:h + 1]))

        N = len(units)
        diff_scores(0)
        diff_scores(1)
        diff_softmax(0)
        for u in range(N):
            if u + 1 < N:
                diff_softmax(u + 1)
            ada_jobs()
            diff_combine(u)
            if u + 2 < N:
                diff_scores(u + 2)
            if u >= 1:
                diff_values(u - 1)
            ada_jobs()
            diff_turn(u)
            ada_jobs()
        diff_values(N - 1)
        ada_jobs(40)
        o_done = [s_dve.now(), s_act.now()]

        wait(dve, *o_done)
        ss = SS[:, :, 0:HEADS1]
        m = V_(dve.tensor_scalar(ss, ss, 1.0 / VD, EPS, ALU.mult, ALU.add))
        wait(act, m)
        m = A_(act.activation(ss, ss, ACT.Sqrt))
        wait(dve, m)
        m = V_(dve.reciprocal(ss, ss))
        wait(dve, m)
        for t in range(T):
            ov = OROW[:, t, :].rearrange("p (h d) -> p h d", h=HEADS1)
            o_mark = V_(dve.tensor_tensor(ov, ov, SS[:, t, 0:HEADS1].unsqueeze(2).broadcast_to([P, HEADS1, VD]), ALU.mult))

        U1 = scr("U1", [P, 2, 2 * S], 0)
        ZT = scr("ZT", [P, 2, S], 4096)
        WB = scr("WB", [P, 2, P], 12288)
        wait(pool, *o_done, *pe_idle())
        m = G_(pool.memset(WB[:, :, :], 0.0))
        wait(act, m)
        for g in range(4):
            o = (g % 2) * HD
            wb_mark = load_const(WB[o:o + HD, g // 2, o:o + HD], A["ev_fourier_w"][0, g, :, :])
        wait(pe, *o_done, s_rope.now())
        for mt in range(2):
            for t in range(T):
                last = pe.matmul(bank[mt][:, :], UROW[:, t, 2304 + mt * P:2304 + (mt + 1) * P], DFT[:, t, :],
                                 start=(t == 0), stop=(t == T - 1))
        m = M_(last)
        wait(act, m)
        for mt in range(2):
            m = A_(act.activation(U1[:, mt, :], bank[mt][:, :], ACT.Copy))
        wait(pe, m)
        for mt in range(2):
            pe.matmul(bank[2][:, mt * S:(mt + 1) * S], CCM[:, 0, :], U1[:, mt, 0:S], start=True, stop=False)
            last = pe.matmul(bank[2][:, mt * S:(mt + 1) * S], CCM[:, 1, :], U1[:, mt, S:2 * S], start=False, stop=True)
        m = M_(last)
        wait(act, m)
        m = A_(act.activation(ZT[:, :, :], bank[2][:, :].rearrange("p (m s) -> p m s", m=2), ACT.Copy))
        wait(pe, m, wb_mark)
        for mt in range(2):
            last = pe.matmul(bank[3][:, mt * S:(mt + 1) * S], WB[:, mt, :], ZT[:, mt, :], start=True, stop=True)
        four_mark = M_(last)

        m = V_(dve.tensor_scalar(SUBG[:, 0:1], col("subln", 1), 1.0 - LAMBDA_INIT, None, ALU.mult))
        wait(dve, m)
        m = V_(dve.tensor_copy(SUBG[:, 1:7], SUBG[:, 0:1].broadcast_to([P, 6])))
        wait(dve, m)
        ym = to_columns(OROW, [o_mark], SUBG, None, XTh, XTl, [four_mark, s_dve.now()], kn=6, banks=(4, 5, 6))
        wait(dve, four_mark)
        m = V_(dve.tensor_copy(FULL[:, 6:8, :], bank[3][:, :].rearrange("p (m s) -> p m s", m=2)))
        wait(act, m)
        h = A_(act.activation(XTh[:, 6:8, :], FULL[:, 6:8, :], ACT.Copy))
        wait(dve, h)
        l = V_(dve.tensor_tensor(XTl[:, 6:8, :], FULL[:, 6:8, :], XTh[:, 6:8, :].bitcast(F32), ALU.subtract))
        def load_ffn1(l):
            load_slabs(2 * (KF // 2), up_parts(A["ffn_w1"][l, :, :], 0, A["ffn_w3"][l, :, :], 0))
            load_slabs(KF // 2, down_parts(A["ffn_w2"][l, :, :]))

        def modulated(l, n):
            return Follow(MODS[:, l, n + 1, :], MODS[:, l, n, :])

        load_ffn1(0)
        load_slabs(8, up_parts(A["od_pw1_w"][0, :, :], 0, A["od_pw1_w"][0, :, :], D))
        load_ada(1, [2, 3, 4, 5])
        load_slabs(4, down_parts(A["od_pw2_w"][0, :, :]))
        load_ffn1(1)
        up = modulated(0, 2)
        down(4, XTh, XTl, [*ym, h, l, *acc_free()], add_residual(gate=0), up)
        conv = modulated(1, 0)
        ffn(up, add_residual(gate=1), conv)

        PAD = TAPS // 2
        B1 = at("B1", [P, 2 * D], ht_at)
        UR = at("UR", [P, T, D], ht_at + 8192)
        UT = at("UT", [P, KD, 288], ht_at + 16384)
        CV = at("CV", [P, KD, S], ht_at + 25600)
        DWW = at("DWW", [P, KD, 32], ht_at + 37888)
        B2 = at("B2", [P, D], ht_at + 38912)
        MEAN = at("MEAN", [P, S], ht_at + 43008)
        RSTD = at("RSTD", [P, S], ht_at + 44032)
        free = [*pe_idle(), s_act.now(), s_dve.now(), htl_done.now(), hth_done.now()]
        wait(pool, *free)
        for h in range(2):
            load_const(B1[:, h * D:(h + 1) * D], A["od_pw1_b"][0, h * D:(h + 1) * D].partition_broadcast(P), eng=pool)
        load_const(B2[:, :], A["od_pw2_b"][0, :].partition_broadcast(P), eng=pool)
        dww_mark = load_const(DWW[:, :, 0:TAPS], A["taps"], eng=pool)
        conv_in = s_soft.now()
        pad_mark = G_(pool.memset(UT[:, :, :], 0.0))
        ones_mark = G_(pool.memset(ONES[:, :], 1.0 / D))
        PE_TILES = 2
        ut_mark = {}

        def turn_gated(c):
            b = bank[4 + c % 2]
            wait(pe, ur_marks[c], ut_mark.get(c - 2))
            for k in (2 * c, 2 * c + 1):
                for t in range(T):
                    last = pe.transpose(b[:, (k % 2) * S + t * P:(k % 2) * S + (t + 1) * P],
                                        UR[:, t, k * P:(k + 1) * P], IDENT[:, :])
            wait(act, M_(last), pad_mark)
            ut_mark[c] = A_(act.activation(UT[:, 2 * c:2 * c + 2, PAD:PAD + S],
                                           b[:, :].rearrange("p (k s) -> p k s", k=2), ACT.Copy))

        def taps_on_dve():
            for k0 in range(0, KD - PE_TILES, 2):
                ks = [k for k in (k0, k0 + 1) if k < KD - PE_TILES]
                wait(dve, ut_mark[k0 // 2])
                prev = {}
                for j in range(TAPS):
                    for k in ks:
                        wait(dve, prev.get(k))
                        if j == 0:
                            m = V_(dve.tensor_scalar(CV[:, k, :], UT[:, k, 0:S], DWW[:, k, 0:1],
                                                     col("od_dw_b")[:, k:k + 1], ALU.mult, ALU.add))
                        else:
                            m = V_(dve.scalar_tensor_tensor(out=CV[:, k, :], in0=UT[:, k, j:j + S],
                                                            scalar=DWW[:, k, j:j + 1], in1=CV[:, k, :],
                                                            op0=ALU.mult, op1=ALU.add))
                        prev[k] = m
                        yield
        dve_taps = background([taps_on_dve()])
        read, ur_marks = {}, {}
        for c in range(4):
            banks = [bank[2 * (c % 2) + t] for t in range(T)]
            if c == 0:
                first_chunk(banks, conv)
            else:
                wait(pe, read.get(c - 2), s_dve.now() if c == 1 else None)
                chunk_slab(0, banks, tiles(XTh, XTl))
                split_next()
                turn_gated(c - 1)
                chunk_slab(1, banks, tiles(XTh, XTl))
            done = slab_mark()
            wait(dve, done, s_act.now(), s_dve.now(), conv_in)
            cs, gs = slice(c * HALF, (c + 1) * HALF), slice(D + c * HALF, D + (c + 1) * HALF)
            for t in range(T):
                m = V_(dve.tensor_tensor(SG[:, t, :], banks[t][:, HALF:CH], B1[:, gs], ALU.add))
                V_(dve.tensor_tensor(HID[:, t, :], banks[t][:, 0:HALF], B1[:, cs], ALU.add))
                wait(act, m)
                A_(act.activation(SG[:, t, :], SG[:, t, :], ACT.Sigmoid))
            read[c] = s_dve.now()
            wait(dve, s_act.now(), s_dve.now())
            for t in range(T):
                ur_marks[c] = V_(dve.tensor_tensor(UR[:, t, cs], HID[:, t, :], SG[:, t, :], ALU.mult))
            split_next()
            if c:
                dve_taps(16)
        turn_gated(3)
        GROUP, SLOTS = 8, 4
        DIAG = [at(f"DIAG{j}", [P, GROUP, P], scr_at + 4096 * j) for j in range(SLOTS)]
        taps = [(k, j) for k in range(KD - PE_TILES, KD) for j in range(TAPS)]
        groups = [taps[o:o + GROUP] for o in range(0, len(taps), GROUP)]
        ada_conv = background([ada_slabs(1, mod, bank[7]) for mod in (2, 3, 4, 5)])
        ada_free[:] = [s_act.now(), s_dve.now()]
        used, built = {}, {}
        wait(act, slab_mark(), dww_mark)
        cv_marks = []

        def build(g):
            if g < len(groups):
                wait(act, used.get(g - SLOTS))
                for n, (k, j) in enumerate(groups[g]):
                    built[g] = A_(act.activation(DIAG[g % SLOTS][:, n, :], IDENT[:, :], ACT.Identity,
                                                 scale=DWW[:, k, j:j + 1]))

        def taps_on_pe(g):
            wait(pe, built[g], *ut_mark.values())
            for n, (k, j) in enumerate(groups[g]):
                last = pe.matmul(bank[k % 4][:, 0:S], DIAG[g % SLOTS][:, n, :], UT[:, k, j:j + S], start=(j == 0),
                                 stop=(j == TAPS - 1))
                if j == TAPS - 1 or n == len(groups[g]) - 1:
                    used[g] = M_(last)
                if j == TAPS - 1:
                    wait(act, used[g])
                    cv_marks.append(A_(act.activation(CV[:, k, :], bank[k % 4][:, 0:S], ACT.Identity,
                                                      bias=col("od_dw_b")[:, k:k + 1])))
        build(0)
        build(1)
        for g in range(len(groups)):
            ada_conv(2)
            taps_on_pe(g)
            dve_taps(9)
            ada_conv(2)
            build(g + 2)
            dve_taps(9)
        dve_taps(KD * TAPS)
        ada_conv(40)
        wait(pe, s_dve.now(), *cv_marks, ones_mark)
        wait(act, s_dve.now())
        lm = {}
        tok = [slice(t * P, (t + 1) * P) for t in range(T)]
        for t in range(T):
            for k in range(KD):
                last = pe.matmul(bank[t][:, 0:P], ONES[:, :], CV[:, k, tok[t]], start=(k == 0), stop=(k == KD - 1))
            lm[t] = M_(last)
        for t in range(T):
            wait(dve, lm[t], *cv_marks)
            m = V_(dve.tensor_copy(MEAN[:, tok[t]], bank[t][:, 0:P]))
            wait(dve, m)
            m = V_(dve.tensor_tensor(CV[:, :, tok[t]], CV[:, :, tok[t]],
                                     MEAN[:, tok[t]].unsqueeze(1).broadcast_to([P, KD, P]), ALU.subtract))
            wait(act, m)
            m = A_(act.activation(UT[:, :, tok[t]], CV[:, :, tok[t]], ACT.Square))
            wait(pe, m)
            for k in range(KD):
                last = pe.matmul(bank[2 + t][:, 0:P], ONES[:, :], UT[:, k, tok[t]], start=(k == 0), stop=(k == KD - 1))
            lm[t] = M_(last)
        for t in range(T):
            wait(dve, lm[t])
            m = V_(dve.tensor_scalar(RSTD[:, tok[t]], bank[2 + t][:, 0:P], EPS, None, ALU.add))
            wait(act, m)
            lm[t] = A_(act.activation(RSTD[:, tok[t]], RSTD[:, tok[t]], ACT.Sqrt))
        for t in range(T):
            wait(dve, lm[t])
            m = V_(dve.reciprocal(RSTD[:, tok[t]], RSTD[:, tok[t]]))
            wait(dve, m)
            m = V_(dve.tensor_tensor(CV[:, :, tok[t]], CV[:, :, tok[t]],
                                     RSTD[:, tok[t]].unsqueeze(1).broadcast_to([P, KD, P]), ALU.mult))
            wait(act, m)
            for k in range(KD):
                m = A_(act.activation(FULL[:, k, tok[t]], CV[:, k, tok[t]], ACT.Silu, scale=col("od_ln_g")[:, k:k + 1],
                                      bias=col("od_ln_b")[:, k:k + 1]))
            wait(act, m)
            h = A_(act.activation(XTh[:, :, tok[t]], FULL[:, :, tok[t]], ACT.Copy))
            wait(dve, h)
            l = V_(dve.tensor_tensor(XTl[:, :, tok[t]], FULL[:, :, tok[t]], XTh[:, :, tok[t]].bitcast(F32),
                                     ALU.subtract))
        up = modulated(1, 2)
        down(4, XTh, XTl, [h, l, *acc_free()], add_residual(gate=2, bias=B2), up)

        def load_final():
            wait(act, s_dve.now())
            wait(dve, load_const(GATE[:, 0, :], A["final_g"].partition_broadcast(P)))
        nxt = Follow(col("ffn1_0"), final=GATE[:, 0, :])
        ffn(up, add_residual(gate=3), nxt, load_final)

        UM = at("UM", [P, T, MIX_IN - FOX_H], ht_at)
        o_cx, o_cb, o_cc, o_hq, o_hf, o_hv, o_hg, o_fq, o_fk, o_fv = 0, 256, 512, 768, 1024, 1280, 1536, 1792, 2304, 2816
        NQK = 8
        QKT = at("QKT", [P, NQK, S], ht_at + 26624)
        YR = at("YR", [P, T, DW], ht_at + 34816)
        Q2, K2 = at("hg_Q2", [P, 2, S], ht_at + 40960), at("hg_K2", [P, 2, S], ht_at + 43008)
        BC = at("hg_BC", [P, 2, S], tmp_at + 14336)
        PZ, PX, PA, PB, PM, PN = (at(f"hg_p{n}", [P, 2, S], ht_at + 26624 + 2048 * n) for n in range(6))
        EX, TM, QKa, QKb, EXP, TMP = (at(f"hg_{n}", [P, 2, S], scr_at + 2048 * n) for n in range(6))
        HA = at("HA", [P, 2, 4, P], tmp_at)
        HX = at("HX", [P, 4, P], tmp_at + 4096)
        TN = at("TN", [P, 2, S], tmp_at + 6144)
        FS = [at(f"FS{j}", [P, S], tmp_at + 8192 + 1024 * j) for j in range(2)]
        FP = [at(f"FP{j}", [P, S], tmp_at + 10240 + 1024 * j) for j in range(2)]
        FT = [at(f"FT{j}", [P, T, P], tmp_at + 12288 + 1024 * j) for j in range(2)]
        K1 = at("K1", [P, 2, S], gate_at)
        Q1 = at("Q1", [P, 2, S], gate_at + 2048)
        CU = at("CU", [P, T, HALF], gate_at + 4096)
        CUT = at("CUT", [P, 2, S + 4], gate_at + 6144)
        CBT = at("CBT", [P, 2, S], gate_at + 8256)
        FZ = at("FZ", [P, 4, T, FOX_H], gate_at + 10304)
        NCT = at("NCT", [FOX_H, S], gate_at + 10560)
        CC = at("CC", [P, T, FOX_H], gate_at + 11584)
        OG = at("OG", [P, HD], gate_at + 11648)
        FB = at("FB", [P, FOX_H], gate_at + 11904)
        GS = at("GS", [P, T, HALF], gate_at + 11968)
        WF = at("WF", [P, KD, FOX_H], gate_at + 14016)
        FST = at("FST", [P, 2, T, 16], gate_at + 14272)
        LB = at("LB", [P, 8, 2], gate_at + 14528)
        TRI = at("TRI", [P, 2, P], cst_at)
        MASKS = at("MASKS", [P, 8, P], cst_at + 1024, U8)
        MB = at("MB", [P, 2, P], cst_at + 2048)
        RESET = at("RESET", [P, 2, S], cst_at + 3072)

        set_up = {}

        def block2_constants():
            free = [*pe_idle(), s_act.now(), s_dve.now()]
            wait(pool, *free)
            wait(dve, *free)
            load_const(TRI[:, :, :], A["tri"], eng=pool)
            MASKF = at("MASKF", [P, 8, P], tmp_at)
            load_const(MASKF[:, :, :], A["masks"], eng=pool)
            mb_mark = load_const(MB[:, :, :], A["causal"], eng=pool)
            wait(dve, mb_mark)
            c2_mark = V_(dve.tensor_copy(MASKS[:, :, :], MASKF[:, :, :]))
            zero_mark = G_(pool.memset(CUT[:, :, 0:2], 0.0))
            m = G_(pool.memset(RESET[:, :, :], 1.0))
            wait(pool, m)
            reset_mark = G_(pool.memset(RESET[:, :, :].rearrange("p k (c n) -> p k c n", n=64)[:, :, :, 0:1], 0.0))
            l0, l1 = col("lb0", 2), col("lb1", 2)
            m = V_(dve.tensor_tensor(LB[:, 0, :], l0, l1, ALU.max))
            wait(dve, m)
            V_(dve.tensor_tensor(LB[:, 1, :], l0, LB[:, 0, :], ALU.subtract))
            m = V_(dve.tensor_tensor(LB[:, 2, :], l1, LB[:, 0, :], ALU.subtract))
            wait(act, m)
            m = A_(act.activation(LB[:, 3:5, :], LB[:, 1:3, :], ACT.Exp))
            wait(dve, m)
            m = V_(dve.tensor_tensor(LB[:, 5, :], LB[:, 3, :], LB[:, 4, :], ALU.add))
            wait(dve, m)
            m = V_(dve.reciprocal(LB[:, 5, :], LB[:, 5, :]))
            wait(dve, m)
            V_(dve.tensor_tensor(LB[:, 1, :], LB[:, 3, :], LB[:, 5, :], ALU.mult))
            m = V_(dve.tensor_tensor(LB[:, 2, :], LB[:, 4, :], LB[:, 5, :], ALU.mult))
            wait(dve, m)
            m = V_(dve.tensor_tensor(LB[:, 6, :], LB[:, 1, :], LB[:, 2, :], ALU.add))
            wait(dve, m)
            V_(dve.tensor_tensor(LB[:, 0, :], LB[:, 1, :], LB[:, 1, :], ALU.subtract))
            m = V_(dve.tensor_tensor(LB[:, 7, :], LB[:, 6, :], LB[:, 1, :], ALU.subtract))
            wait(dve, m)
            for l, r0 in ((0, 0), (1, 7)):
                m = V_(dve.tensor_scalar(LB[:, 2 * l, :], LB[:, r0, :], 0.0, 1.0, ALU.max, ALU.min))
                wait(dve, m)
                m = V_(dve.tensor_scalar(LB[:, 2 * l + 1, :], LB[:, 2 * l, :], -1.0, 1.0, ALU.mult, ALU.add))
                wait(dve, m)
            lb_mark = m
            set_up.update(c2_mark=c2_mark, zero_mark=zero_mark, reset_mark=reset_mark, lb_mark=lb_mark)

        def ffn2(w_in_, w_out_, l, follow, then, during):
            w = A[w_in_][l, :, :]
            load_slabs(2 * (KF // 2), up_parts(w, 0, w, FF))
            load_slabs(KF // 2, down_parts(A[w_out_][l, :, :]))
            ffn(follow, add_residual(half=True), then, during)

        def mix_small(l):
            if l == 0:
                block2_constants()
            free = [*pe_idle(), s_act.now(), s_dve.now()]
            wait(pool, *free)
            load_const(WF[:, :, :], row_tiles(A["w_mix_in_2"][l, :, :])[:, :, MIX_IN - FOX_H:MIX_IN], eng=pool)
            load_const(FB[:, :], A["fox_f_bias_2"][l, :].partition_broadcast(P), eng=pool)
            return load_const(OG[:, :], A["hgrn_out_gain_2"][l, :].partition_broadcast(P), eng=pool)

        def mix_in(l, follow):
            w = A["w_mix_in_2"][l, :, :]
            load_slabs(12, up_parts(w, 0, w, HALF, CH))
            load_slab(wide_parts(w, 3072))
            load_slabs(4, down_parts(A["w_mix_out_2"][l, :, :]))
            marks = {}
            jobs = background([fox_decay(marks), hgrn_decay(l, marks)])
            for c in range(6):
                banks = [bank[2 * (c % 2) + t] for t in range(T)]
                if c == 0:
                    first_chunk(banks, follow)
                else:
                    wait(pe, marks.get(("out", c - 2)), marks.get(("out2", c - 2)), s_dve.now() if c == 1 else None)
                    chunk_slab(0, banks, tiles(XTh, XTl))
                    split_next()
                    jobs(1)
                    chunk_slab(1, banks, tiles(XTh, XTl))
                wait(act, slab_mark())
                wait(dve, slab_mark())
                cols = slice(c * CH, (c + 1) * CH)
                marks["out", c] = A_(act.activation(UM[:, 0, cols], banks[0][:, :], ACT.Identity, scale=ST[:, 0:1]))
                marks["out2", c] = V_(dve.tensor_scalar(UM[:, 1, cols], banks[1][:, :], ST[:, 1:2], None, ALU.mult))
                marks["rows"] = [marks["out", c], marks["out2", c]]
                split_next()
                if c == 0:
                    wait(pe, s_soft.now())
                    for t in range(T):
                        for k in range(KD):
                            last = pe.matmul(bank[7][:, t * FOX_H:(t + 1) * FOX_H], FULL[:, k, t * P:(t + 1) * P],
                                             WF[:, k, :], start=(k == 0), stop=(k == KD - 1))
                    m = M_(last)
                    wait(dve, m, s_soft.now())
                    for t in range(T):
                        marks["z"] = V_(dve.scalar_tensor_tensor(
                            out=FZ[:, 0, t, :], in0=bank[7][:, t * FOX_H:(t + 1) * FOX_H], scalar=ST[:, t:t + 1],
                            in1=FB[:, :], op0=ALU.mult, op1=ALU.add))
                jobs(1)
            wait(pe, marks["out", 4], marks["out2", 4])
            r = slab_ready()
            for k in range(KD):
                wh, wl = hi[r][:, k * HALF:(k + 1) * HALF], lo[r][:, k * HALF:(k + 1) * HALF]
                for t, (xh, xl) in enumerate(tiles(XTh, XTl)):
                    last = three(bank[t][:, 0:HALF], xh(k), xl(k), wh, wl, k == 0, k == KD - 1)
            slab_used(last)
            jobs(20)
            marks["fox_job"] = fox(l, marks)
            next(marks["fox_job"])
            next(marks["fox_job"])
            wait(act, slab_mark())
            wait(dve, slab_mark())
            a = A_(act.activation(UM[:, 0, 3072:3328], bank[0][:, 0:HALF], ACT.Identity, scale=ST[:, 0:1]))
            v = V_(dve.tensor_scalar(UM[:, 1, 3072:3328], bank[1][:, 0:HALF], ST[:, 1:2], None, ALU.mult))
            marks["rows"] = [a, v]
            split_next()
            return marks

        def conv3(l, marks):
            zero = set_up["zero_mark"]
            wait(dve, *marks["rows"])
            m = V_(dve.tensor_tensor(CU[:, :, :], UM[:, :, o_cx:o_cx + HALF], UM[:, :, o_cc:o_cc + HALF], ALU.mult))
            yield
            read = marks["fox_banks"]
            for n, src in enumerate((CU[:, :, :], UM[:, :, o_cb:o_cb + HALF])):
                wait(pe, m, *read)
                for k in range(2):
                    for t in range(T):
                        last = pe.transpose(bank[4][:, k * S + t * P:k * S + (t + 1) * P], src[:, t, k * P:(k + 1) * P],
                                            IDENT[:, :])
                wait(act, M_(last), zero)
                dst = (CUT[:, :, 2:2 + S], CBT[:, :, :])[n]
                done = A_(act.activation(dst, bank[4][:, :].rearrange("p (k s) -> p k s", k=2), ACT.Copy))
                read = [done]
            marks["conv_bank"] = done
            yield
            wait(dve, done)
            v0 = vec[f"conv{l}"]
            prev = {}
            for j in range(3):
                for k in range(2):
                    w = COLS[:, v0 + 2 * j + k:v0 + 2 * j + k + 1]
                    wait(dve, prev.get(k))
                    if j == 0:
                        prev[k] = V_(dve.tensor_scalar(CU[:, k, :], CUT[:, k, 0:S], w, None, ALU.mult))
                    else:
                        prev[k] = V_(dve.scalar_tensor_tensor(out=CU[:, k, :], in0=CUT[:, k, j:j + S], scalar=w,
                                                              in1=CU[:, k, :], op0=ALU.mult, op1=ALU.add))
            wait(dve, *prev.values())
            marks["conv"] = V_(dve.tensor_tensor(CBT[:, :, :], CBT[:, :, :], CU[:, :, :], ALU.mult))
            yield

        def hgrn_decay(l, marks):
            wait(pe, *marks["rows"])
            for n, o in enumerate((o_hq, o_hf)):
                for k in range(2):
                    for t in range(T):
                        last = pe.transpose(bank[4 + n][:, k * S + t * P:k * S + (t + 1) * P],
                                            UM[:, t, o + k * P:o + (k + 1) * P], IDENT[:, :])
            m = M_(last)
            wait(dve, m, set_up["lb_mark"])
            wait(act, m, set_up["lb_mark"])
            q = V_(dve.tensor_copy(Q2[:, :, :], bank[4][:, :].rearrange("p (k s) -> p k s", k=2)))
            z = A_(act.activation(PZ[:, :, :], bank[5][:, :].rearrange("p (k s) -> p k s", k=2), ACT.Copy))
            yield
            wait(act, z)
            sg = A_(act.activation(K2[:, :, :], PZ[:, :, :], ACT.Sigmoid, scale=-1.0))
            wait(dve, z)
            V_(dve.tensor_scalar(PX[:, :, :], PZ[:, :, :], 0.0, None, ALU.min))
            V_(dve.scalar_tensor_tensor(out=PA[:, :, :], in0=PZ[:, :, :], scalar=0.5, in1=PZ[:, :, :],
                                        op0=ALU.mult, op1=ALU.max))
            m = V_(dve.scalar_tensor_tensor(out=PB[:, :, :], in0=PZ[:, :, :], scalar=-1.0, in1=PZ[:, :, :],
                                            op0=ALU.mult, op1=ALU.max))
            wait(dve, sg)
            for k in range(2):
                kk = V_(dve.tensor_scalar(K2[:, k, :], K2[:, k, :], LB[:, 2 * l + 1, k:k + 1], None, ALU.mult))
            yield
            wait(act, m, sg)
            A_(act.activation(PM[:, :, :], PX[:, :, :], ACT.Exp, scale=0.5))
            A_(act.activation(PN[:, :, :], PA[:, :, :], ACT.Exp, scale=-1.0))
            m = A_(act.activation(PZ[:, :, :], PB[:, :, :], ACT.Exp, scale=-1.0))
            yield
            wait(dve, m)
            for k in range(2):
                m = V_(dve.scalar_tensor_tensor(out=PA[:, k, :], in0=PN[:, k, :], scalar=LB[:, 2 * l, k:k + 1],
                                                in1=PM[:, k, :], op0=ALU.mult, op1=ALU.add))
            m = V_(dve.tensor_scalar(PB[:, :, :], PZ[:, :, :], 1.0, None, ALU.add))
            yield
            wait(act, m)
            A_(act.activation(PN[:, :, :], PA[:, :, :], ACT.Ln))
            m = A_(act.activation(PM[:, :, :], PB[:, :, :], ACT.Ln))
            yield
            wait(dve, m)
            m = V_(dve.scalar_tensor_tensor(out=PN[:, :, :], in0=PX[:, :, :], scalar=0.5, in1=PN[:, :, :],
                                            op0=ALU.mult, op1=ALU.add))
            wait(dve, m)
            m = V_(dve.tensor_tensor(PM[:, :, :], PN[:, :, :], PM[:, :, :], ALU.subtract))
            wait(dve, m, set_up["reset_mark"])
            marks["b"] = V_(dve.tensor_tensor_scan(flat(BC), flat(RESET), flat(PM), 0.0, ALU.mult, ALU.add))
            marks["qk2"] = [q, kk]
            yield

        def flat(x):
            return x[:, :, :].rearrange("p k s -> p (k s)")

        def hgrn(l, marks):
            def blk(x, n):
                return x[:, :, :].rearrange("p k (c n) -> p (k c) n", n=n)

            start = [*pe_idle(), *marks["qk2"], marks["b"]]
            wait(dve, *start)
            selected = V_(dve.memset(HA[:, :, :, :], 0.0))
            bank_free = {0: marks["rows"], 1: []}

            def products(lhs, rhs, pair, ready, cross=False):
                wait(pe, *ready, *bank_free[pair])
                for h in range(HG_H):
                    for t in range(1 if cross else T):
                        rows_ = slice((h % 2) * HD, (h % 2 + 1) * HD)
                        s_at, t_at = (0, P) if cross else (t * P, t * P)
                        o = (2 * t + h // 2) * P
                        last = pe.matmul(bank[2 * pair + h % 2][:, o:o + P], lhs[rows_, h // 2, s_at:s_at + P],
                                         rhs[rows_, h // 2, t_at:t_at + P], start=True, stop=True)
                return M_(last)

            def select(level, pair, done):
                nonlocal selected
                wait(dve, done, selected, set_up["c2_mark"])
                for t in range(T):
                    mask = MASKS[:, level, :].unsqueeze(1).broadcast_to([P, HG_H, P])
                    selected = V_(dve.copy_predicated(HA[:, t, :, :], mask,
                                                      bank[2 * pair + t][:, :].rearrange("p (h s) -> p h s", h=HG_H)))
                bank_free[pair] = [selected]

            used, decayed, exped = {}, {}, {}

            def decay(lv):
                n = LEVELS[lv]
                E2 = (EX, TM)[lv % 2]
                b2, e2 = blk(BC, 2 * n), blk(E2, 2 * n)
                anchor = b2[:, :, n - 1:n].broadcast_to([P, 2 * S // (2 * n), n])
                wait(dve, decayed.get(lv - 2))
                V_(dve.tensor_tensor(e2[:, :, 0:n], anchor, b2[:, :, 0:n], ALU.subtract))
                m = V_(dve.tensor_tensor(e2[:, :, n:2 * n], b2[:, :, n:2 * n], anchor, ALU.subtract))
                wait(act, m)
                exped[lv] = A_(act.activation(E2[:, :, :], E2[:, :, :], ACT.Exp))

            pending = (7, 0, products(K2, Q2, 0, start))
            decay(1)
            bc = blk(BC, 64)
            m = V_(dve.tensor_tensor(blk(TN, 64), bc[:, :, 63:64].broadcast_to([P, 8, 64]), bc, ALU.subtract))
            wait(act, m, marks["b"])
            A_(act.activation(EXP[:, :, :], BC[:, :, :], ACT.Exp))
            pair_exp = A_(act.activation(TMP[:, :, :], TN[:, :, :], ACT.Exp))
            yield
            pair = 1
            for lv in range(1, len(LEVELS)):
                n = LEVELS[lv]
                E2, QK = (EX, TM)[lv % 2], (QKa, QKb)[lv % 2]
                if lv + 1 < len(LEVELS):
                    decay(lv + 1)
                e2, x2, q2, k2 = (blk(x, 2 * n) for x in (E2, QK, Q2, K2))
                wait(dve, exped[lv], used.get(lv - 2))
                V_(dve.tensor_tensor(x2[:, :, 0:n], k2[:, :, 0:n], e2[:, :, 0:n], ALU.mult))
                decayed[lv] = V_(dve.tensor_tensor(x2[:, :, n:2 * n], q2[:, :, n:2 * n], e2[:, :, n:2 * n], ALU.mult))
                used[lv] = products(QK, QK, pair, [decayed[lv]])
                select(*pending)
                pending = (lv, pair, used[lv])
                pair ^= 1
                yield
            wait(dve, pair_exp)
            V_(dve.tensor_tensor(K1[:, :, :], K2[:, :, :], TMP[:, :, :], ALU.mult))
            m = V_(dve.tensor_tensor(Q1[:, :, :], Q2[:, :, :], EXP[:, :, :], ALU.mult))
            done = products(K1, Q1, pair, [m])
            select(*pending)
            yield
            select(0, pair, done)
            pair ^= 1
            for k in range(2):
                V_(dve.tensor_scalar(K1[:, k, 0:64], K1[:, k, 0:64], EXP[:, k, 127:128], None, ALU.mult))
                m = V_(dve.tensor_scalar(Q1[:, k, 192:256], Q1[:, k, 192:256], EXP[:, k, 191:192], None, ALU.mult))
            done = products(K1, Q1, pair, [m], cross=True)
            wait(act, done)
            for odd in range(2):
                hx = A_(act.activation(HX[:, 2 * odd:2 * odd + 2, :],
                                       bank[2 * pair + odd][:, 0:S].rearrange("p (h s) -> p h s", h=2), ACT.Copy))
            gs = A_(act.activation(GS[:, :, :], UM[:, :, o_hg:o_hg + HALF], ACT.Silu))
            yield
            o = [bank[2 * (pair ^ 1) + t] for t in range(T)]
            wait(pe, hx, selected)
            for t in range(T):
                for h in range(HG_H):
                    d = o[t][:, h * HD:(h + 1) * HD]
                    v = lambda tt: UM[:, tt, o_hv + h * HD:o_hv + (h + 1) * HD]
                    last = pe.matmul(d, HA[:, h % 2, 2 * t + h // 2, :], v(t), start=True, stop=(t == 0))
                    if t == 1:
                        last = pe.matmul(d, HX[:, 2 * (h % 2) + h // 2, :], v(0), start=False, stop=True)
            m = M_(last)
            wait(act, m)
            for t in range(T):
                m = A_(act.activation(K1[:, t, :], o[t][:, 0:HALF], ACT.Copy))
            wait(act, m)
            m = A_(act.activation(Q1[:, :, :], K1[:, :, :], ACT.Square))
            yield
            wait(dve, m)
            m = V_(dve.tensor_reduce(ST[:, 8:16], Q1[:, :, :].rearrange("p t (h d) -> p (t h) d", h=HG_H), AX.X, ALU.add))
            r = rstd(ST[:, 8:16], HD, m)
            heads = K1[:, :, :].rearrange("p t (h d) -> p (t h) d", h=HG_H)
            wait(dve, gs, s_soft.now())
            gsh = GS[:, :, :].rearrange("p t (h d) -> p (t h) d", h=HG_H)
            g = V_(dve.tensor_tensor(gsh, gsh, OG[:, :].unsqueeze(1).broadcast_to([P, 8, HD]), ALU.mult))
            yield
            wait(dve, r, g)
            m = V_(dve.tensor_tensor(heads, heads, ST[:, 8:16].unsqueeze(2).broadcast_to([P, 8, HD]), ALU.mult))
            wait(dve, m)
            marks["hgrn"] = V_(dve.tensor_tensor(YR[:, :, 0:HALF], K1[:, :, :], GS[:, :, :], ALU.mult))
            yield

        def fox_decay(marks):
            wait(dve, marks["z"])
            V_(dve.tensor_scalar(FZ[:, 1, :, :], FZ[:, 0, :, :], 0.0, None, ALU.min))
            m = V_(dve.scalar_tensor_tensor(out=FZ[:, 2, :, :], in0=FZ[:, 0, :, :], scalar=-1.0,
                                            in1=FZ[:, 0, :, :], op0=ALU.mult, op1=ALU.max))
            wait(act, m)
            m = A_(act.activation(FZ[:, 3, :, :], FZ[:, 2, :, :], ACT.Exp, scale=-1.0))
            yield
            wait(dve, m)
            m = V_(dve.tensor_scalar(FZ[:, 2, :, :], FZ[:, 3, :, :], 1.0, None, ALU.add))
            wait(act, m)
            m = A_(act.activation(FZ[:, 3, :, :], FZ[:, 2, :, :], ACT.Ln))
            yield
            wait(dve, m)
            m = V_(dve.tensor_tensor(FZ[:, 0, :, :], FZ[:, 1, :, :], FZ[:, 3, :, :], ALU.subtract))
            yield
            wait(pe, m, set_up["c2_mark"])
            pe.matmul(bank[6][:, 0:FOX_H], TRI[:, 0, :], FZ[:, 0, 0, :], start=True, stop=True)
            pe.matmul(bank[6][:, FOX_H:2 * FOX_H], TRI[:, 1, :], FZ[:, 0, 0, :], start=True, stop=False)
            pe.matmul(bank[6][:, FOX_H:2 * FOX_H], TRI[:, 0, :], FZ[:, 0, 1, :], start=False, stop=True)
            pe.matmul(bank[7][0:FOX_H, 0:P], FZ[:, 0, 0, :], TRI[:, 0, :], start=True, stop=True)
            pe.matmul(bank[7][0:FOX_H, P:S], FZ[:, 0, 0, :], TRI[:, 1, :], start=True, stop=False)
            last = pe.matmul(bank[7][0:FOX_H, P:S], FZ[:, 0, 1, :], TRI[:, 0, :], start=False, stop=True)
            m = M_(last)
            wait(dve, m)
            V_(dve.tensor_copy(CC[:, :, :], bank[6][:, 0:2 * FOX_H].rearrange("p (t h) -> p t h", t=T)))
            marks["c"] = V_(dve.tensor_scalar(NCT[:, :], bank[7][0:FOX_H, 0:S], -1.0, None, ALU.mult))
            yield

        def fox(l, marks):
            sq = QKT[:, :, :].rearrange("p a b -> p (a b)").rearrange("p (t n) -> p t n", t=T)
            qk = UM[:, :, o_fq:o_fv]
            wait(act, *marks["rows"], marks["b"])
            m = A_(act.activation(sq, qk, ACT.Square))
            wait(dve, m, *marks["rows"])
            st = FST[:, 0, :, :]
            m = V_(dve.tensor_reduce(st, sq.rearrange("p t (h d) -> p t h d", d=HD), AX.X, ALU.add))
            r = rstd(st, HD, m)
            yield
            wait(dve, r)
            for t in range(T):
                v = qk[:, t, :].rearrange("p (h d) -> p h d", d=HD)
                m = V_(dve.tensor_tensor(v, v, FST[:, 0, t, :].unsqueeze(2).broadcast_to([P, 16, HD]), ALU.mult))
            yield
            qkt_mark = []
            wait(pe, m, marks["c"], *marks["qk2"])
            for kp in range(0, NQK, 2):
                b = bank[4 + kp // 2]
                for k in (kp, kp + 1):
                    for t in range(T):
                        last = pe.transpose(b[:, (k - kp) * S + t * P:(k - kp) * S + (t + 1) * P],
                                            qk[:, t, k * P:(k + 1) * P], IDENT[:, :])
                m = M_(last)
                src = b[:, :].rearrange("p (k s) -> p k s", k=2)
                if kp < 4:
                    wait(dve, m)
                    qkt_mark.append(V_(dve.tensor_scalar(QKT[:, kp:kp + 2, :], src, col(f"foxq{l}", 1), HD ** -0.5,
                                                         ALU.mult, ALU.mult)))
                else:
                    wait(act, m)
                    qkt_mark.append(A_(act.activation(QKT[:, kp:kp + 2, :], src, ACT.Identity,
                                                      scale=col(f"foxk{l}", 1))))
            marks["fox_banks"] = qkt_mark
            yield
            units = [(h, t) for h in range(FOX_H) for t in range(T)]
            N = len(units)
            mk = {}
            wait(pe, *qkt_mark)

            def scores(u):
                h, t = units[u]
                j, n = u % 2, (units[u][1] + 1) * P
                wait(pe, mk.get(("s", u - 2)))
                r_ = slice((h % 2) * HD, (h % 2 + 1) * HD)
                b = bank[6 + j]
                pe.matmul(b[:, 0:n], QKT[r_, h // 2, t * P:(t + 1) * P], QKT[r_, 4 + h // 2, 0:n], start=True, stop=False)
                last = pe.matmul(b[:, 0:n], IDENT[0:FOX_H, h:h + 1].broadcast_to([FOX_H, P]), NCT[:, 0:n],
                                 start=False, stop=True)
                mk["q", u] = M_(last)

            def softmax(u):
                h, t = units[u]
                j, n = u % 2, (units[u][1] + 1) * P
                s_ = ST[:, 32 + 8 * (u % 4):40 + 8 * (u % 4)]
                wait(dve, mk["q", u], mk.get(("e", u - 2)), mk.get(("o", u - 4)), marks["c"])
                mb = MB[:, :, :].rearrange("p a b -> p (a b)")[:, S - n:S]
                mk["s", u] = m = V_(dve.scalar_tensor_tensor(out=FS[j][:, 0:n], in0=bank[6 + j][:, 0:n],
                                                             scalar=CC[:, t, h:h + 1], in1=mb,
                                                             op0=ALU.add, op1=ALU.add))
                wait(dve, m)
                m = V_(dve.tensor_reduce(s_[:, 0:1], FS[j][:, 0:n], AX.X, ALU.max, negate=True))
                wait(act, m, mk.get(("t", u - 2)))
                mk["e", u] = A_(act.activation(FP[j][:, 0:n], FS[j][:, 0:n], ACT.Exp, bias=s_[:, 0:1],
                                               accum_out=s_[:, 1:2]))

            def turn(u):
                h, t = units[u]
                j = u % 2
                wait(pe, mk["e", u], mk.get(("c", u - 1)))
                for kt in range(t + 1):
                    last = pe.transpose(bank[5][:, kt * P:(kt + 1) * P], FP[j][:, kt * P:(kt + 1) * P], IDENT[:, :])
                mk["t", u] = M_(last)
                wait(act, mk["t", u], mk.get(("p", u - 2)))
                mk["c", u] = A_(act.activation(FT[j][:, 0:t + 1, :],
                                               bank[5][:, 0:(t + 1) * P].rearrange("p (k q) -> p k q", q=P), ACT.Copy))

            def values(u):
                h, t = units[u]
                j = u % 2
                s_ = ST[:, 32 + 8 * (u % 4):40 + 8 * (u % 4)]
                wait(pe, mk["c", u], mk.get(("o", u - 1)), marks.get("conv_bank"), *marks["rows"])
                for kt in range(t + 1):
                    last = pe.matmul(bank[4][:, 0:HD], FT[j][:, kt, :], UM[:, kt, o_fv + h * HD:o_fv + (h + 1) * HD],
                                     start=(kt == 0), stop=(kt == t))
                mk["p", u] = M_(last)
                wait(dve, mk["e", u])
                m = V_(dve.reciprocal(s_[:, 2:3], s_[:, 1:2]))
                wait(dve, m, mk["p", u], marks["b"])
                mk["o", u] = V_(dve.tensor_scalar(YR[:, t, HALF + h * HD:HALF + (h + 1) * HD], bank[4][:, 0:HD],
                                                  s_[:, 2:3], None, ALU.mult))

            scores(0)
            scores(1)
            softmax(0)
            yield
            for u in range(N):
                if u + 1 < N:
                    softmax(u + 1)
                if u + 2 < N:
                    scores(u + 2)
                if u >= 1:
                    values(u - 1)
                turn(u)
                yield
            values(N - 1)
            marks["fox"] = mk["o", N - 1]
            yield

        def mixers(l, marks):
            h, f, c = hgrn(l, marks), marks["fox_job"], conv3(l, marks)
            order = [h, f, h, c, f, h, c, f, h, c] + [h, f] * 16 + [f] * 20
            for g in order:
                next(g, None)
            for g in (h, f, c):
                assert next(g, None) is None

        for l in range(2):
            mixer, second = Follow(col(f"mix2_{l}")), Follow(col(f"ffn2_{l}"))
            ffn2("ffn1_w_in_2", "ffn1_w_out_2", l, nxt, mixer, lambda: mix_small(l))
            marks = mix_in(l, mixer)
            mixers(l, marks)
            ym = to_columns(YR, [marks["hgrn"], marks["fox"]], None, None, XTh, XTl,
                            [*pe_idle(), s_act.now(), s_dve.now()], kn=6, k0=2)
            wait(act, marks["conv"])
            h_ = A_(act.activation(XTh[:, 0:2, :], CBT[:, :, :], ACT.Copy))
            wait(dve, h_)
            l_ = V_(dve.tensor_tensor(XTl[:, 0:2, :], CBT[:, :, :], XTh[:, 0:2, :].bitcast(F32), ALU.subtract))
            down(4, XTh, XTl, [*ym, h_, l_, *acc_free()], add_residual(), second)
            nxt = Follow(col("ffn1_1")) if l == 0 else Last()
            ffn2("ffn2_w_in_2", "ffn2_w_out_2", l, second, nxt, None)
        wait(sp, s_out.now())


def constants():
    c = {"ident": np.eye(P, dtype=np.float32)}
    c["sum"] = np.repeat(np.array([[1], [0], [1]], np.float32), P, axis=1)
    n = np.arange(S)
    ang = 2 * np.pi * (np.outer(n, n) % S) / S
    dft = np.concatenate([np.cos(ang), np.sin(ang)], axis=1).astype(np.float32)
    c["dft"] = dft.reshape(T, P, 2 * S).transpose(1, 0, 2).copy()
    m = np.arange(HD)
    ang = 2 * np.pi * (np.outer(m, m) % HD) / HD
    scale = 1.0 / np.sqrt(S * HD)
    ccm = np.zeros((P, 2, P), np.float32)
    for g in range(2):
        ccm[g * HD:(g + 1) * HD, 0, g * HD:(g + 1) * HD] = np.cos(ang) * scale
        ccm[g * HD:(g + 1) * HD, 1, g * HD:(g + 1) * HD] = -np.sin(ang) * scale
    c["ccm"] = ccm
    s, t = np.arange(P)[:, None], np.arange(P)[None, :]
    c["tri"] = np.stack([(s <= t), np.ones((P, P))], axis=1).astype(np.float32)
    c["causal"] = np.stack([np.zeros((P, P)), np.where(t <= s, 0.0, -1e30)], axis=1).astype(np.float32)
    masks = [(s // n + 1 == t // n) & (s // n % 2 == 0) for n in LEVELS] + [s == t]
    c["masks"] = np.stack(masks, axis=1).astype(np.float32)
    rows = S // GRID_W
    row = np.repeat(np.arange(rows, dtype=np.float32), GRID_W)
    colm = np.tile(np.arange(GRID_W, dtype=np.float32), rows)
    half = HD // 2
    inv = (ROPE_THETA ** (-np.arange(0, half, 2, dtype=np.float32) / half)).astype(np.float32)
    a = np.concatenate([row[:, None] * inv, colm[:, None] * inv], axis=-1)
    r = np.stack([np.cos(a), np.sin(a)], axis=1).astype(np.float32)
    c["rope"] = r.reshape(T, P, 2, half).transpose(1, 0, 2, 3).copy()
    return c


_INS = ['x', 'c', 'ctx', 'c_ctx', 'ada_w', 'ada_b', 'mix_norm_g', 'ffn_norm_g', 'ffn_w1', 'ffn_w3', 'ffn_w2',
        'ev_w_in', 'ev_lambda_q1', 'ev_lambda_k1', 'ev_lambda_q2', 'ev_lambda_k2', 'ev_subln_g', 'ev_fourier_w',
        'ev_w_out', 'od_pw1_w', 'od_pw1_b', 'od_dw_w', 'od_dw_b', 'od_ln_g', 'od_ln_b', 'od_pw2_w', 'od_pw2_b',
        'final_g', 'ffn1_norm_2', 'ffn1_w_in_2', 'ffn1_w_out_2', 'mix_norm_2', 'w_mix_in_2', 'conv_w_2',
        'hgrn_lb_logits_2', 'hgrn_out_gain_2', 'fox_q_gain_2', 'fox_k_gain_2', 'fox_f_bias_2', 'w_mix_out_2',
        'ffn2_norm_2', 'ffn2_w_in_2', 'ffn2_w_out_2']


def columns(inputs):
    parts, vec, n = [], {}, 0

    def add(name, a):
        nonlocal n
        a = np.asarray(a).reshape(-1, P)
        parts.append(a)
        vec[name] = n
        n += a.shape[0]

    add("c", inputs["c"])
    add("c_ctx", inputs["c_ctx"])
    for l in range(2):
        for name, key in (("mix", "mix_norm_g"), ("ffn", "ffn_norm_g"), ("ffn1_", "ffn1_norm_2"),
                          ("mix2_", "mix_norm_2"), ("ffn2_", "ffn2_norm_2"), ("lb", "hgrn_lb_logits_2"),
                          ("conv", "conv_w_2")):
            add(f"{name}{l}", inputs[key][l])
        for name, key in (("foxq", "fox_q_gain_2"), ("foxk", "fox_k_gain_2")):
            add(f"{name}{l}", np.concatenate([inputs[key][l], inputs[key][l]]))
    for name in ("od_dw_b", "od_ln_g", "od_ln_b"):
        add(name, inputs[name][0])
    add("subln", inputs["ev_subln_g"])
    taps = np.ascontiguousarray(np.asarray(inputs["od_dw_w"])[0].reshape(TAPS, KD, P).transpose(2, 1, 0))
    return {"cols": np.ascontiguousarray(np.concatenate(parts).T), "taps": taps}, vec


def kernel(**inputs):
    import concourse.bacc as _bacc
    from concourse.bass_utils import run_bass_kernel_spmd as _run

    nc = _bacc.Bacc("TRN2", target_bir_lowering=False, num_devices=1)
    arrays, aps = {}, {}
    for name in _INS:
        a = np.ascontiguousarray(inputs[name])
        arrays[f"in_{name}"] = a
        aps[name] = nc.dram_tensor(f"in_{name}", a.shape, mybir.dt.from_np(a.dtype), kind="ExternalInput").ap()
    small, vec = columns(inputs)
    aps["vec"] = vec
    for name, a in {**constants(), **small}.items():
        arrays[f"const_{name}"] = a
        aps[name] = nc.dram_tensor(f"const_{name}", a.shape, mybir.dt.from_np(a.dtype), kind="ExternalInput").ap()
    out = nc.dram_tensor("out_0", (1, S, D), F32, kind="ExternalOutput").ap()
    program(nc, aps, out)
    r = _run(nc, [arrays], core_ids=[0])
    return r.results[0]["out_0"]
```
